# Optimizing a Trainium2 kernel written in Bass

```python
import math
import jax, jax.numpy as jnp
from jax import lax
import numpy as np

D_MODEL = 2048
BATCH = 1
SEQ = 256
DEPTH = 1

HEAD_DIM = 128
N_HEADS_TOTAL = D_MODEL // HEAD_DIM
N_HEADS_A = N_HEADS_TOTAL // 2
N_HEADS_B = N_HEADS_TOTAL - N_HEADS_A
DIFF_QK_DIM = HEAD_DIM // 2
WIDTH_A = N_HEADS_A * HEAD_DIM
WIDTH_B = N_HEADS_B * HEAD_DIM
MIX_WIDTH = WIDTH_A + WIDTH_B
IN_PROJ_WIDTH = 3 * WIDTH_A + 3 * WIDTH_B
DILATED_PATTERNS = ((128, 1), (512, 4), (2048, 16))
D_FF = -(-8 * D_MODEL // (3 * 256)) * 256
ROPE_THETA = 10000.0
RMS_EPS = 1e-6
Q_BLOCK = 128


def rmsnorm(x, g):
    xf = x.astype(jnp.float32)
    y = xf * lax.rsqrt(jnp.mean(xf * xf, axis=-1, keepdims=True) + RMS_EPS)
    return (y * g.astype(jnp.float32)).astype(x.dtype)

def rope(x, positions):
    e = x.shape[-1]
    half = e // 2
    inv = ROPE_THETA ** (-jnp.arange(half, dtype=jnp.float32) / half)
    ang = positions.astype(jnp.float32)[..., None] * inv
    ang = ang.reshape(ang.shape[:2] + (1,) * (x.ndim - 3) + (half,))
    cos, sin = jnp.cos(ang), jnp.sin(ang)
    xf = x.astype(jnp.float32)
    x1, x2 = xf[..., :half], xf[..., half:]
    return jnp.concatenate([x1 * cos - x2 * sin, x2 * cos + x1 * sin], axis=-1).astype(x.dtype)

def dilated_window_attention(q, k, v, window, dilation):
    B, S, H, E = q.shape
    n = window // dilation
    L = S // dilation
    nblk = -(-L // n)
    Lp = nblk * n

    def to_blocks(a):
        a = a.reshape(B, L, dilation, H, E)
        a = jnp.pad(a, ((0, 0), (0, Lp - L), (0, 0), (0, 0), (0, 0)))
        return a.reshape(B, nblk, n, dilation, H, E)

    def with_prev(a):
        prev = jnp.pad(a, ((0, 0), (1, 0), (0, 0), (0, 0), (0, 0), (0, 0)))[:, :-1]
        return jnp.concatenate([prev, a], axis=2)

    qb = to_blocks(q)
    kc = with_prev(to_blocks(k))
    vc = with_prev(to_blocks(v))

    s = jnp.einsum('bnqrhe,bnkrhe->bnrhqk', qb, kc).astype(jnp.float32)
    qi = jnp.arange(n)[:, None]
    kj = jnp.arange(2 * n)[None, :]
    dist = qi + n - kj
    band = (dist >= 0) & (dist <= n)
    blk = jnp.arange(nblk)[:, None, None]
    mask = band[None] & ((blk > 0) | (kj[None] >= n))
    s = jnp.where(mask[None, :, None, None], s, -jnp.inf)
    m = jnp.max(s, axis=-1, keepdims=True)
    p = jnp.exp(s - m)
    den = jnp.sum(p, axis=-1)
    o = jnp.einsum('bnrhqk,bnkrhe->bnqrhe', p, vc.astype(jnp.float32))
    o = o / den.transpose(0, 1, 4, 2, 3)[..., None]
    lse = (m[..., 0] + jnp.log(den)).transpose(0, 1, 4, 2, 3)
    o = o.reshape(B, Lp, dilation, H, E)[:, :L].reshape(B, S, H, E)
    lse = lse.reshape(B, Lp, dilation, H)[:, :L].reshape(B, S, H)
    return o, lse

def dilated_mixture_attention(q, k, v):
    outs, lses = [], []
    for window, dilation in DILATED_PATTERNS:
        o, lse = dilated_window_attention(q, k, v, window, dilation)
        outs.append(o)
        lses.append(lse)
    w = jax.nn.softmax(jnp.stack(lses, axis=0), axis=0)
    return jnp.sum(w[..., None] * jnp.stack(outs, axis=0), axis=0)

def differential_attention(q, k, v, lam):
    B, S, _, H, e = q.shape
    n_q = S // Q_BLOCK
    q_blocks = q.reshape(B, n_q, Q_BLOCK, 2, H, e).transpose(1, 0, 2, 3, 4, 5)
    kpos = jnp.arange(S)
    vf = v.astype(jnp.float32)

    def one_block(args):
        bi, qblk = args
        s = jnp.einsum('bqmhe,bkmhe->bmhqk', qblk, k).astype(jnp.float32)
        qpos = bi * Q_BLOCK + jnp.arange(Q_BLOCK)
        causal = kpos[None, :] <= qpos[:, None]
        s = jnp.where(causal, s, -jnp.inf)
        a = jax.nn.softmax(s, axis=-1)
        attn = a[:, 0] - lam * a[:, 1]
        return jnp.einsum('bhqk,bkhe->bqhe', attn, vf)

    out = lax.map(one_block, (jnp.arange(n_q), q_blocks))
    return out.transpose(1, 0, 2, 3, 4).reshape(B, S, H, v.shape[-1])

def first_inputs(seed: int = 0) -> dict:
    key = jax.random.key(seed)
    ks = jax.random.split(key, 20)
    f32 = jnp.float32

    def nrm(k, shape, scale):
        return jax.random.normal(k, shape, f32) * scale

    def gain(k):
        return 1.0 + nrm(k, (DEPTH, D_MODEL), 0.05)

    x = jax.random.normal(ks[0], (BATCH, SEQ, D_MODEL), f32)
    c = jax.random.normal(ks[1], (BATCH, D_MODEL), f32)
    offset = jax.random.randint(ks[2], (BATCH, 1), 0, 4096, dtype=jnp.int32)
    positions = offset + jnp.arange(SEQ, dtype=jnp.int32)[None, :]
    return {
        "x": x,
        "c": c,
        "positions": positions,
        "w_ada": nrm(ks[3], (DEPTH, D_MODEL, 6 * D_MODEL), 0.5 * D_MODEL ** -0.5),
        "b_ada": nrm(ks[4], (DEPTH, 6 * D_MODEL), 0.02),
        "g_pre_attn": gain(ks[5]),
        "w_in": nrm(ks[6], (DEPTH, D_MODEL, IN_PROJ_WIDTH), D_MODEL ** -0.5),
        "g_out_a": 1.0 + nrm(ks[7], (DEPTH, HEAD_DIM), 0.05),
        "lambda_q1": nrm(ks[8], (DEPTH, DIFF_QK_DIM), 0.1),
        "lambda_k1": nrm(ks[9], (DEPTH, DIFF_QK_DIM), 0.1),
        "lambda_q2": nrm(ks[10], (DEPTH, DIFF_QK_DIM), 0.1),
        "lambda_k2": nrm(ks[11], (DEPTH, DIFF_QK_DIM), 0.1),
        "g_subln_b": 1.0 + nrm(ks[12], (DEPTH, HEAD_DIM), 0.05),
        "w_out": nrm(ks[13], (DEPTH, MIX_WIDTH, D_MODEL), MIX_WIDTH ** -0.5),
        "g_post_attn": gain(ks[14]),
        "g_pre_ffn": gain(ks[15]),
        "w_gate": nrm(ks[16], (DEPTH, D_MODEL, D_FF), D_MODEL ** -0.5),
        "w_up": nrm(ks[17], (DEPTH, D_MODEL, D_FF), D_MODEL ** -0.5),
        "w_down": nrm(ks[18], (DEPTH, D_FF, D_MODEL), D_FF ** -0.5),
        "g_post_ffn": gain(ks[19]),
    }

def first_block(x, c, positions, w_ada, b_ada, g_pre_attn, w_in, g_out_a,
              lambda_q1, lambda_k1, lambda_q2, lambda_k2, g_subln_b, w_out,
              g_post_attn, g_pre_ffn, w_gate, w_up, w_down, g_post_ffn):
    B, S, _ = x.shape
    scale_a = HEAD_DIM ** -0.5
    scale_b = DIFF_QK_DIM ** -0.5
    for l in range(DEPTH):
        lambda_init = 0.8 - 0.6 * math.exp(-0.3 * l)
        mod = jax.nn.silu(c) @ w_ada[l] + b_ada[l]
        sh_a, sc_a, gt_a, sh_f, sc_f, gt_f = [m[:, None, :] for m in jnp.split(mod, 6, axis=-1)]

        h = rmsnorm(x, g_pre_attn[l]) * (1.0 + sc_a) + sh_a
        proj = h @ w_in[l]
        qa, ka, va, qb, kb, vb = jnp.split(proj, 6, axis=-1)

        qa = rope(qa.reshape(B, S, N_HEADS_A, HEAD_DIM), positions) * scale_a
        ka = rope(ka.reshape(B, S, N_HEADS_A, HEAD_DIM), positions)
        va = va.reshape(B, S, N_HEADS_A, HEAD_DIM)
        oa = dilated_mixture_attention(qa, ka, va).astype(x.dtype)
        oa = rmsnorm(oa, g_out_a[l])

        qb = rope(qb.reshape(B, S, 2, N_HEADS_B, DIFF_QK_DIM), positions) * scale_b
        kb = rope(kb.reshape(B, S, 2, N_HEADS_B, DIFF_QK_DIM), positions)
        vb = vb.reshape(B, S, N_HEADS_B, HEAD_DIM)
        lam = (jnp.exp(jnp.sum(lambda_q1[l].astype(jnp.float32) * lambda_k1[l].astype(jnp.float32)))
               - jnp.exp(jnp.sum(lambda_q2[l].astype(jnp.float32) * lambda_k2[l].astype(jnp.float32)))
               + lambda_init)
        ob = differential_attention(qb, kb, vb, lam).astype(x.dtype)
        ob = rmsnorm(ob, g_subln_b[l]) * (1.0 - lambda_init)

        mix = jnp.concatenate([oa.reshape(B, S, WIDTH_A), ob.reshape(B, S, WIDTH_B)], axis=-1)
        x = x + gt_a * rmsnorm(mix @ w_out[l], g_post_attn[l])

        h = rmsnorm(x, g_pre_ffn[l]) * (1.0 + sc_f) + sh_f
        f = (jax.nn.silu(h @ w_gate[l]) * (h @ w_up[l])) @ w_down[l]
        x = x + gt_f * rmsnorm(f, g_post_ffn[l])
    return x


CHUNK = 64
ROPE_THETA_2 = 500000.0
N_MEM = 256
EPS = 1e-6

MLA_HEADS = 8
MLA_NOPE = 128
MLA_ROPE = 64
MLA_V = 128
MLA_Q_LORA = 512
MLA_KV_LORA = 256
DSA_HEADS = 8
DSA_HEAD_DIM = 128
DSA_ROT = DSA_HEAD_DIM // 4
IDX_HEADS = 16
IDX_DIM = 64
IDX_ROT = IDX_DIM // 4
TOPK_MAX = 256
X_HEADS = 4
X_HEAD_DIM = 128
D_FF_2 = 4 * D_MODEL

MIX_WIDTH_2 = MLA_HEADS * MLA_V + DSA_HEADS * DSA_HEAD_DIM
IN_SPLITS = (
    MLA_Q_LORA,
    MLA_KV_LORA,
    MLA_ROPE,
    DSA_HEADS * DSA_HEAD_DIM,
    DSA_HEADS * DSA_HEAD_DIM,
    DSA_HEADS * DSA_HEAD_DIM,
    IDX_HEADS * IDX_DIM,
    IDX_DIM,
    IDX_HEADS,
)
D_IN = int(sum(IN_SPLITS))


def rmsnorm_2(x, g):
    xf = x.astype(jnp.float32)
    y = xf * lax.rsqrt(jnp.mean(xf * xf, axis=-1, keepdims=True) + EPS)
    return (y * g.astype(jnp.float32)).astype(x.dtype)

def rope_2(x, pos, rot_dim):
    half = rot_dim // 2
    inv_freq = ROPE_THETA_2 ** (-jnp.arange(half, dtype=jnp.float32) / half)
    ang = pos.astype(jnp.float32)[..., None] * inv_freq
    ang = ang.reshape(ang.shape[:2] + (1,) * (x.ndim - 3) + (half,))
    cos, sin = jnp.cos(ang), jnp.sin(ang)
    xf = x.astype(jnp.float32)
    x1, x2, rest = xf[..., :half], xf[..., half:rot_dim], xf[..., rot_dim:]
    out = jnp.concatenate([x1 * cos - x2 * sin, x2 * cos + x1 * sin, rest], axis=-1)
    return out.astype(x.dtype)

def to_blocks(a):
    b, s = a.shape[:2]
    a = a.reshape((b, s // Q_BLOCK, Q_BLOCK) + a.shape[2:])
    return jnp.moveaxis(a, 1, 0)

def from_blocks(a):
    a = jnp.moveaxis(a, 0, 1)
    return a.reshape((a.shape[0], a.shape[1] * a.shape[2]) + a.shape[3:])

def query_chunks(i):
    return (i * Q_BLOCK + jnp.arange(Q_BLOCK)) // CHUNK

def mla_mixer(c_q, c_kv, k_rope, pos, g_cq, g_ckv, w_qb, w_kvb):
    b, s, _ = c_q.shape
    q = (rmsnorm_2(c_q, g_cq) @ w_qb).reshape(b, s, MLA_HEADS, MLA_NOPE + MLA_ROPE)
    q_nope = q[..., :MLA_NOPE]
    q_rope = rope_2(q[..., MLA_NOPE:], pos, MLA_ROPE)
    kv = (rmsnorm_2(c_kv, g_ckv) @ w_kvb).reshape(b, s, MLA_HEADS, MLA_NOPE + MLA_V)
    k_nope, v = kv[..., :MLA_NOPE], kv[..., MLA_NOPE:]
    k_rope = rope_2(k_rope, pos, MLA_ROPE)
    scale = (MLA_NOPE + MLA_ROPE) ** -0.5
    key_chunk = jnp.arange(s) // CHUNK

    def block(args):
        i, qn, qr = args
        sc = (jnp.einsum('bqhd,bkhd->bhqk', qn, k_nope)
              + jnp.einsum('bqhr,bkr->bhqk', qr, k_rope)).astype(jnp.float32) * scale
        allowed = key_chunk[None, :] <= query_chunks(i)[:, None]
        sc = jnp.where(allowed[None, None], sc, -jnp.inf)
        p = jax.nn.softmax(sc, axis=-1).astype(v.dtype)
        return jnp.einsum('bhqk,bkhd->bqhd', p, v)

    o = lax.map(block, (jnp.arange(s // Q_BLOCK), to_blocks(q_nope), to_blocks(q_rope)))
    return from_blocks(o).reshape(b, s, MLA_HEADS * MLA_V)

def dsa_mixer(q, k, v, q_idx, k_idx, w_idx, pos):
    b, s, _ = q.shape
    q = rope_2(q.reshape(b, s, DSA_HEADS, DSA_HEAD_DIM), pos, DSA_ROT)
    k = rope_2(k.reshape(b, s, DSA_HEADS, DSA_HEAD_DIM), pos, DSA_ROT)
    v = v.reshape(b, s, DSA_HEADS, DSA_HEAD_DIM)
    q_idx = rope_2(q_idx.reshape(b, s, IDX_HEADS, IDX_DIM), pos, IDX_ROT)
    k_idx = rope_2(k_idx, pos, IDX_ROT)
    w_idx = w_idx * (IDX_HEADS ** -0.5)
    n_sel = min(TOPK_MAX, s // 4)
    key_chunk = jnp.arange(s) // CHUNK
    gather = jax.vmap(lambda arr, idx: arr[idx])

    def block(args):
        i, qb, qib, wb = args
        qc = query_chunks(i)
        logits = jax.nn.relu(jnp.einsum('bqhd,bkd->bqhk', qib, k_idx).astype(jnp.float32) * (IDX_DIM ** -0.5))
        score = jnp.einsum('bqhk,bqh->bqk', logits, wb.astype(jnp.float32))
        allowed = key_chunk[None, :] <= qc[:, None]
        score = jnp.where(allowed[None], score, -jnp.inf)
        _, sel = lax.top_k(score, n_sel)
        sel_ok = (sel // CHUNK) <= qc[None, :, None]
        k_sel = gather(k, sel)
        v_sel = gather(v, sel)
        sc = jnp.einsum('bqhd,bqnhd->bhqn', qb, k_sel).astype(jnp.float32) * (DSA_HEAD_DIM ** -0.5)
        sc = jnp.where(sel_ok[:, None], sc, -jnp.inf)
        p = jax.nn.softmax(sc, axis=-1).astype(v.dtype)
        return jnp.einsum('bhqn,bqnhd->bqhd', p, v_sel)

    o = lax.map(block, (jnp.arange(s // Q_BLOCK), to_blocks(q), to_blocks(q_idx), to_blocks(w_idx)))
    return from_blocks(o).reshape(b, s, DSA_HEADS * DSA_HEAD_DIM)

def memory_cross_attention(h, mem_n, wq, wk, wv, wo):
    b, s, _ = h.shape
    m = mem_n.shape[1]
    q = (h @ wq).reshape(b, s, X_HEADS, X_HEAD_DIM)
    k = (mem_n @ wk).reshape(b, m, X_HEADS, X_HEAD_DIM)
    v = (mem_n @ wv).reshape(b, m, X_HEADS, X_HEAD_DIM)
    sc = jnp.einsum('bshd,bmhd->bhsm', q, k).astype(jnp.float32) * (X_HEAD_DIM ** -0.5)
    p = jax.nn.softmax(sc, axis=-1).astype(v.dtype)
    o = jnp.einsum('bhsm,bmhd->bshd', p, v).reshape(b, s, X_HEADS * X_HEAD_DIM)
    return o @ wo

def second_inputs(seed: int = 0) -> dict:
    key = jax.random.key(seed)
    ks = jax.random.split(key, 24)
    f32 = jnp.float32

    def w(k, shape, fan_in):
        return jax.random.normal(k, (DEPTH,) + shape, f32) * (fan_in ** -0.5)

    def gain(k, n):
        return 1.0 + 0.02 * jax.random.normal(k, (DEPTH, n), f32)

    x = jax.random.normal(ks[0], (BATCH, SEQ, D_MODEL), f32)
    mem = jax.random.normal(ks[1], (BATCH, N_MEM, D_MODEL), f32)
    offset = jax.random.randint(ks[2], (BATCH, 1), 0, 16, dtype=jnp.int32) * CHUNK
    positions = (offset + jnp.arange(SEQ, dtype=jnp.int32)[None, :]).astype(jnp.int32)
    return {
        "x": x,
        "mem": mem,
        "positions": positions,
        "g_mix": gain(ks[3], D_MODEL),
        "w_in": w(ks[4], (D_MODEL, D_IN), D_MODEL),
        "g_cq": gain(ks[5], MLA_Q_LORA),
        "g_ckv": gain(ks[6], MLA_KV_LORA),
        "w_qb": w(ks[7], (MLA_Q_LORA, MLA_HEADS * (MLA_NOPE + MLA_ROPE)), MLA_Q_LORA),
        "w_kvb": w(ks[8], (MLA_KV_LORA, MLA_HEADS * (MLA_NOPE + MLA_V)), MLA_KV_LORA),
        "w_out": w(ks[9], (MIX_WIDTH_2, D_MODEL), MIX_WIDTH_2),
        "g_cross": gain(ks[10], D_MODEL),
        "g_mem": gain(ks[11], D_MODEL),
        "w_q_cross": w(ks[12], (D_MODEL, X_HEADS * X_HEAD_DIM), D_MODEL),
        "w_k_cross": w(ks[13], (D_MODEL, X_HEADS * X_HEAD_DIM), D_MODEL),
        "w_v_cross": w(ks[14], (D_MODEL, X_HEADS * X_HEAD_DIM), D_MODEL),
        "w_o_cross": w(ks[15], (X_HEADS * X_HEAD_DIM, D_MODEL), X_HEADS * X_HEAD_DIM),
        "g_mlp": gain(ks[16], D_MODEL),
        "w_up": w(ks[17], (D_MODEL, D_FF_2), D_MODEL),
        "w_down": w(ks[18], (D_FF_2, D_MODEL), D_FF_2),
        "g_final": 1.0 + 0.02 * jax.random.normal(ks[19], (D_MODEL,), f32),
    }

def second_block(x, mem, positions, g_mix, w_in, g_cq, g_ckv, w_qb, w_kvb, w_out,
              g_cross, g_mem, w_q_cross, w_k_cross, w_v_cross, w_o_cross,
              g_mlp, w_up, w_down, g_final):
    offsets = np.cumsum(np.array(IN_SPLITS))[:-1].tolist()
    for l in range(DEPTH):
        h = rmsnorm_2(x, g_mix[l])
        c_q, c_kv, k_rope, q_d, k_d, v_d, q_idx, k_idx, w_idx = jnp.split(h @ w_in[l], offsets, axis=-1)
        a = mla_mixer(c_q, c_kv, k_rope, positions, g_cq[l], g_ckv[l], w_qb[l], w_kvb[l])
        bb = dsa_mixer(q_d, k_d, v_d, q_idx, k_idx, w_idx, positions)
        x = x + jnp.concatenate([a, bb], axis=-1) @ w_out[l]
        hc = rmsnorm_2(x, g_cross[l])
        mem_n = rmsnorm_2(mem, g_mem[l])
        x = x + memory_cross_attention(hc, mem_n, w_q_cross[l], w_k_cross[l], w_v_cross[l], w_o_cross[l])
        hm = rmsnorm_2(x, g_mlp[l])
        x = x + jnp.square(jax.nn.relu(hm @ w_up[l])) @ w_down[l]
    return rmsnorm_2(x, g_final)


def setup_inputs(seed=0):
    out = dict(first_inputs(seed))
    for name, value in second_inputs(seed + 1).items():
        if name != "x":
            out[name + "_2"] = value
    return out


def reference(
    x, c, positions, w_ada, b_ada, g_pre_attn, w_in, g_out_a, lambda_q1, lambda_k1, lambda_q2,
    lambda_k2, g_subln_b, w_out, g_post_attn, g_pre_ffn, w_gate, w_up, w_down, g_post_ffn,
    mem_2, positions_2, g_mix_2, w_in_2, g_cq_2, g_ckv_2, w_qb_2, w_kvb_2, w_out_2, g_cross_2,
    g_mem_2, w_q_cross_2, w_k_cross_2, w_v_cross_2, w_o_cross_2, g_mlp_2, w_up_2, w_down_2,
    g_final_2,
):
    x = first_block(
        x, c, positions, w_ada, b_ada, g_pre_attn, w_in, g_out_a, lambda_q1, lambda_k1,
        lambda_q2, lambda_k2, g_subln_b, w_out, g_post_attn, g_pre_ffn, w_gate, w_up, w_down,
        g_post_ffn,
    )
    return second_block(
        x, mem_2, positions_2, g_mix_2, w_in_2, g_cq_2, g_ckv_2, w_qb_2, w_kvb_2, w_out_2,
        g_cross_2, g_mem_2, w_q_cross_2, w_k_cross_2, w_v_cross_2, w_o_cross_2, g_mlp_2, w_up_2,
        w_down_2, g_final_2,
    )


_drawn_inputs = setup_inputs


def setup_inputs(seed=0):
    import zlib

    import numpy as np

    out = dict(_drawn_inputs(seed))
    spreads = {}
    factors = {'g_out_a': 2.715,
     'lambda_q1': 2.81,
     'lambda_k1': 8.0,
     'lambda_q2': 8.0,
     'g_subln_b': 3.432,
     'g_mix_2': 2.994,
     'g_cq_2': 8.0,
     'g_ckv_2': 8.0,
     'g_cross_2': 8.0,
     'g_mem_2': 8.0,
     'g_mlp_2': 9.739,
     'g_final_2': 7.868}
    for name, (base, spread) in spreads.items():
        noise = np.random.default_rng([zlib.crc32(name.encode()), seed]).standard_normal(out[name].shape)
        drawn = base * np.exp(spread * noise) if base else spread * noise
        out[name] = __import__('jax').numpy.asarray(drawn.astype(out[name].dtype))
    for name, factor in factors.items():
        out[name] = (out[name] * factor).astype(out[name].dtype)
    return out
```

```python
import numpy as np
import concourse.bass as bass
from concourse import mybir

F32 = mybir.dt.float32
F32R = mybir.dt.float32r
I32 = mybir.dt.int32
ALU = mybir.AluOpType
ACT = mybir.ActivationFunctionType
AX = mybir.AxisListType.X

P = 128
S = 256
MT = S // P
D = 2048
KD = D // P
DFF1, DFF2 = 5632, 8192
IN1, IN2 = 6144, 5008
BANK = 512
RAW, SPLIT = 8, 4
TILE = 1024
EPS = 1e-6
NEG = -1e30
DROPPED = -3.0e38
TAKEN = -3.3e38
MAGIC = 12582912.0
TOPK = 64
KB = 1024

C_C, C_BADA, C_GPOSTA = 0, 16, 112
C_GPRE, C_GFFN, C_GMIX, C_GCROSS, C_GMEM, C_GMLP, C_GCQ, C_GCKV, C_GPOSTF = (
    128, 144, 160, 176, 192, 208, 224, 228, 230)
NCOL = 246

R_A, R_B, R_MLA, R_DSA, R_IDX = (0, 64), (64, 32), (96, 32), (128, 16), (144, 8)
NROT, NROT1 = 152, 96
PI2 = 2 * np.pi
PI_A = 6.28125
PI_B = float(np.float32(PI2 - PI_A))
PI_C = float(np.float32(PI2 - PI_A - PI_B))


def shape_constants():
    t = np.arange(P)[:, None] + P
    k = np.arange(S)[None, :]
    d = t - k
    count = ((d >= 0) & (d <= 128)).astype(np.float32)
    count += (d >= 0) & (d % 4 == 0)
    count += (d >= 0) & (d % 16 == 0)
    dilated = np.where(count > 0, 0, NEG).astype(np.float32)
    causal = np.where(d >= 0, 0, NEG).astype(np.float32)
    chunk = np.where(k // 64 <= t // 64, 0, NEG).astype(np.float32)
    f = lambda theta, half: (np.float32(theta) ** (-np.arange(half, dtype=np.float32) / np.float32(half))).astype(np.float32)
    inv = np.concatenate([f(10000.0, 64), f(10000.0, 32), f(500000.0, 32), f(500000.0, 16), f(500000.0, 8)])
    return {
        "k_ident": np.eye(P, dtype=np.float32), "k_count": count, "k_dilated": dilated,
        "k_causal": causal, "k_chunk": chunk, "k_inv": inv[None, :].astype(np.float32),
    }


class Tok:

    def __init__(self, track, v, loop, epoch):
        self.track, self.v, self.loop, self.epoch = track, v, loop, epoch


class Loop:

    def __init__(self, reg, start, n, per):
        self.reg, self.start, self.n, self.per, self.live = reg, start, n, per, True


class Clock:

    def __init__(self):
        self.loop, self.epoch, self.tracks = None, 0, []


class Track:

    def __init__(self, nc, clock, name, step=1):
        self.sem, self.clock, self.step, self.n, self.name = nc.alloc_semaphore(name), clock, step, 0, name
        clock.tracks.append(self)

    def done(self, ins):
        ins.then_inc(self.sem, self.step)
        self.n += self.step
        return Tok(self, self.n, self.clock.loop, self.clock.epoch)

    def last(self):
        return Tok(self, self.n, self.clock.loop, self.clock.epoch)


def build(nc, a, out):
    clock = Clock()
    PE, DVE, SCA, POOL, SP = nc.tensor, nc.vector, nc.scalar, nc.gpsimd, nc.sync
    tp, tv, ta, tg = (Track(nc, clock, n) for n in ("s_tensor", "s_vector", "s_scalar", "s_pool"))
    track_of = {id(PE): tp, id(DVE): tv, id(SCA): ta, id(POOL): tg}
    t_raw = [Track(nc, clock, f"s_raw{r}", 16) for r in range(RAW)]
    t_par = Track(nc, clock, "s_parameters", 16)
    t_x = Track(nc, clock, "s_x", 16)
    t_mem = Track(nc, clock, "s_mem", 16)
    t_late = Track(nc, clock, "s_late", 16)
    t_out = Track(nc, clock, "s_out", 16)
    st = {}
    waited = {}

    def need(eng, *toks):
        best = {}
        for tok in toks:
            if tok is None:
                continue
            if isinstance(tok, (list, tuple)):
                for x in tok:
                    if x is not None:
                        best.setdefault(id(x.track), []).append(x)
                continue
            best.setdefault(id(tok.track), []).append(tok)
        for group in best.values():
            fixed = [t for t in group if t.loop is None or not t.loop.live]
            moving = [t for t in group if t.loop is not None and t.loop.live]
            if moving:
                v = max(t.v for t in moving)
                lp, tr = moving[0].loop, moving[0].track
                DVE_ = lp.reg * lp.per[tr] + (v - lp.start * lp.per[tr])
                eng.wait_ge(tr.sem, DVE_)
            if fixed:
                tr = fixed[0].track
                v = max(t.v + ((t.loop.n - 1 - t.loop.start) * t.loop.per[tr] if t.loop else 0) for t in fixed)
                if waited.get((id(eng), id(tr)), 0) >= v:
                    continue
                if clock.loop is None:
                    waited[(id(eng), id(tr))] = v
                eng.wait_ge(tr.sem, v)

    def done(eng, ins):
        return track_of[id(eng)].done(ins)

    def repeat(n, body, peel=1, tail=0):
        peel, ends = min(peel, n), n
        n = max(peel, n - tail)
        for i in range(peel):
            clock.epoch += 1
            before = {t: t.n for t in clock.tracks}
            body(i)
        if n == peel:
            for i in range(n, ends):
                body(i)
            return
        per = {t: t.n - before[t] for t in clock.tracks}
        mine, epoch = clock.epoch, clock.epoch
        clock.epoch += 1
        base = {t: t.n for t in clock.tracks}
        with nc.Fori(peel, n) as reg:
            lp = Loop(reg, peel, n, per)
            clock.loop = lp
            old = dict(st)
            for k, tok in old.items():
                st[k] = [Tok(x.track, x.v, lp, -1) if x.epoch == mine else x for x in tok]
            body(reg)
            for t in clock.tracks:
                assert t.n - base[t] == per[t], (t.name, t.n - base[t], per[t])
            for k, tok in old.items():
                for x, y in zip(tok, st[k]):
                    if x.epoch == mine:
                        assert y.epoch == clock.epoch and y.v == x.v + per[x.track], (k, x.v, y.v, per[x.track])
            lp.live = False
            clock.loop = None
        for t in clock.tracks:
            t.n = base[t] + per[t] * (n - peel)
        clock.epoch += 1
        waited.clear()
        for i in range(n, ends):
            body(i)

    base0 = -(-nc.sbuf_base // 128) * 128
    plan = {}
    at_ = base0
    for name, size in (("raw", 32 * KB), ("whi", 16 * KB), ("wlo", 16 * KB), ("x", 16 * KB), ("h", 32 * KB),
                       ("big", 64 * KB), ("acc", 16 * KB), ("mem", 8 * KB), ("small", 7 * KB + 256)):
        plan[name] = (at_, size)
        at_ += size

    def sb(name, region, off, shape, dt=F32):
        start, size = plan[region]
        n = 4 * int(np.prod(shape))
        assert off + n <= size, (name, off, n, size)
        return nc.alloc_sbuf_tensor_at(name, [P] + list(shape), dt, offset=start + off)

    raw = [sb(f"raw{r}", "raw", 4 * KB * r, [TILE]) for r in range(RAW)]
    whi = [sb(f"whi{r}", "whi", 4 * KB * r, [TILE], F32R) for r in range(SPLIT)]
    wlo = [sb(f"wlo{r}", "wlo", 4 * KB * r, [TILE], F32R) for r in range(SPLIT)]
    x = sb("x_res", "x", 0, [MT, D])
    h_hi = sb("h_hi", "h", 0, [KD, S], F32R)
    h_lo = sb("h_lo", "h", 16 * KB, [KD, S], F32R)
    acc = [sb(f"ada_acc{i}", "acc", 8 * KB * i, [D]) for i in range(2)]
    kxT = sb("cross_kT", "mem", 0, [4, S])
    vx = sb("cross_v", "mem", 4 * KB, [MT, 512])

    off = [0]

    def small(name, shape, dt=F32):
        t = sb(name, "small", off[0], shape, dt)
        off[0] += -(-4 * int(np.prod(shape)) // 32) * 32
        return t

    ident = small("ident", [P])
    causal = small("causal", [S])
    chunk = small("chunk", [S])
    cols = small("param_cols", [NCOL])
    mod = small("mod_cols", [96])
    gsc = small("gain_cols", [KD])
    trig = small("trig", [2, MT, NROT])
    one = small("one", [1])
    mhalf = small("minus_half", [16])
    sil = small("silu_c", [KD])
    sq = small("sum_of_squares", [16])
    sq2 = small("sum_of_squares2", [16])
    nm = [small(f"neg_max{i}", [4]) for i in range(2)]
    den = [small(f"denominator{i}", [4]) for i in range(2)]
    rden = [small(f"reciprocal{i}", [4]) for i in range(2)]
    lam = small("lam", [4])
    posf = small("pos_f", [2 * MT])
    posi = small("pos_i", [2 * MT], I32)
    wi = small("w_idx", [MT, 16])
    m8 = small("max8", [8])

    proj = sb("proj", "big", 0, [MT, IN1])
    count = sb("count", "big", 62 * KB, [S])
    dilated = sb("dilated", "big", 63 * KB, [S])
    norm_x = [sb(f"norm_x{m}", "big", 8 * KB * m, [D]) for m in range(MT)]
    norm_f = sb("norm_f", "big", 16 * KB, [8, S])
    junk = sb("junk", "h", 24 * KB, [D])
    gate_row = sb("gate_row", "big", 50 * KB, [D])
    diag = sb("diag", "h", 0, [KD, P])
    ones_sq = sb("ones_sq", "h", 8 * KB, [P])
    hid1 = sb("hidden1_T", "big", 0, [DFF1 // P, S])
    hid2 = sb("hidden2_T", "big", 0, [DFF2 // P, S])
    sg1 = sb("silu_gate", "big", 58 * KB, [MT, BANK])
    r2 = [sb(f"relu{i}", "acc", 8 * KB * i, [MT, BANK]) for i in range(2)]
    rp_t = sb("rope_t", "h", 0, [D])
    rp_u = [sb(f"rope_u{i}", "h", 8 * KB + 4 * KB * i, [TILE]) for i in range(2)]
    hsq = sb("head_sq", "big", 48 * KB, [TILE])
    mixT = sb("mix_T", "h", 0, [KD, S])
    s_hi = [sb(f"src_hi{i}", "h", 16 * KB + KB * i, [S], F32R) for i in range(4)]
    s_lo = [sb(f"src_lo{i}", "h", 20 * KB + KB * i, [S], F32R) for i in range(4)]
    vec1 = sb("vec_rows1", "big", 24 * KB, [P])
    vec2 = sb("vec_rows2", "big", 25 * KB, [P])
    inv = sb("inv_freq", "big", 26 * KB, [NROT])
    ang = sb("angles", "big", 28 * KB, [MT, NROT])
    rnd = sb("turns", "big", 30 * KB, [MT, NROT])
    angr = sb("reduced", "big", 32 * KB, [2, MT, NROT])
    lamv = sb("lambda_rows", "big", 36 * KB, [4, 64])
    sil_t = sb("silu_tmp", "big", 37 * KB, [KD])
    post_tmp = sb("post_tmp", "big", 0, [D])

    ps = nc.alloc_psum_tensor("ps", [P, 8, BANK], F32)

    def bank_free(b, *toks):
        st["bank", b] = list(toks)

    def r32(ap):
        return ap.bitcast(F32)

    count_t = [0, 0]

    def fetch(src, view):
        r = count_t[0] % RAW
        count_t[0] += 1
        need(SP, st.get(("raw", r)))
        dst = raw[r][:, :] if view is None else raw[r][:, 0:view[0] * view[1]].rearrange("p (k n) -> p k n", k=view[0])
        st["landed", r] = [t_raw[r].done(SP.dma_start(dst, src))]
        return r

    def split(r, n=TILE):
        u = count_t[1] % SPLIT
        count_t[1] += 1
        need(SCA, st["landed", r], st.get(("split", u)))
        hi = done(SCA, SCA.activation(whi[u][:, 0:n], raw[r][:, 0:n], ACT.Copy))
        need(DVE, hi, st["landed", r])
        lo = done(DVE, DVE.tensor_tensor(wlo[u][:, 0:n], raw[r][:, 0:n], r32(whi[u][:, 0:n]), ALU.subtract))
        st["raw", r] = [lo]
        st["halves", u] = [hi, lo]
        return u

    def products(dst, lhs, rhs, first, last, flag):
        (ah, al), (bh, bl) = lhs, rhs
        PE.matmul(dst, ah, bh, start=first, stop=False)
        PE.matmul(dst, al, bh, start=False, stop=False)
        return PE.matmul(dst, ah, bl, start=False, stop=last)

    def col_slot(w, row0, nk, c0, width, banks, A, pend=(), lag=3, extra=None):
        pend = list(pend)
        kt_per = 2 if nk > 1 else 1
        need(PE, *[st.get(("bank", b)) for b in banks])
        ah, al = A
        for j in range(nk // kt_per):
            src = w[row0 + j * kt_per * P:row0 + (j + 1) * kt_per * P, c0] if not isinstance(c0, tuple) else w[row0 + j * kt_per * P:row0 + (j + 1) * kt_per * P, c0[0]:c0[0] + width]
            r = fetch(src.rearrange("(k p) n -> p k n", p=P), (kt_per, width))
            u = split(r, kt_per * width)
            need(PE, st["halves", u])
            for kk in range(kt_per):
                k = j * kt_per + kk
                for m in range(MT):
                    lhs = (ah[:, k, m * P:(m + 1) * P], al[:, k, m * P:(m + 1) * P])
                    rhs = (whi[u][:, kk * width:(kk + 1) * width], wlo[u][:, kk * width:(kk + 1) * width])
                    ins = products(ps[:, banks[m], 0:width], lhs, rhs, k == 0, k == nk - 1, None)
            st["split", u] = [done(PE, ins)]
            if extra:
                extra(j)
            if j >= lag and pend:
                pend.pop(0)()
        st["full", banks[0]] = st["split", u]
        for step in pend:
            step()

    def ada_half(part, kt, half, first):
        r = fetch(a["w_ada"][0][bass.ds(kt * P, P), part * D + half * TILE:part * D + (half + 1) * TILE], None)
        dst = acc[part % 2][:, half * TILE:(half + 1) * TILE]
        c = sil[:, kt:kt + 1] if isinstance(kt, int) else sil[:, bass.ds(kt, 1)]
        need(DVE, st["landed", r], st["silu"])
        if first:
            need(DVE, st.get(("acc", part % 2)))
            t = done(DVE, DVE.tensor_scalar(dst, raw[r][:, :], c, None, ALU.mult))
        else:
            need(DVE, st["accumulated", half])
            t = done(DVE, DVE.scalar_tensor_tensor(dst, raw[r][:, :], c, dst, ALU.mult, ALU.add))
        st["accumulated", half] = [t]
        st["raw", r] = [t]

    def ada_finish(part, bank):
        need(PE, st["accumulated", 0], st["accumulated", 1], st.get(("bank", bank)), st["one"])
        for k in range(KD):
            ins = PE.matmul(ps[:, bank, k:k + 1], acc[part % 2][:, k * P:(k + 1) * P], one[:, :], start=True, stop=True)
        t = done(PE, ins)
        st["acc", part % 2] = [t]
        need(DVE, t, st["cols"])
        c = done(DVE, DVE.tensor_tensor(mod[:, part * 16:part * 16 + 16], ps[:, bank, 0:KD],
                                        cols[:, C_BADA + part * 16:C_BADA + part * 16 + 16], ALU.add))
        bank_free(bank, c)
        st["mod", part] = [c]

    def row_stage(w, srcT, nk, ready, ada=None, tag=""):
        per = 4
        need(SCA, ready)
        need(DVE, ready)
        need(PE, *[st.get(("bank", b)) for b in range(8)])

        def body(i):
            for q in range(per):
                kt = i * per + q
                src = srcT[:, kt, :] if isinstance(kt, int) else srcT[:, bass.ds(kt, 1), :].rearrange("p o n -> p (o n)")
                need(SCA, st.get(("src", q)))
                hi = done(SCA, SCA.activation(s_hi[q][:, :], src, ACT.Copy))
                need(DVE, hi)
                lo = done(DVE, DVE.tensor_tensor(s_lo[q][:, :], src, r32(s_hi[q][:, :]), ALU.subtract))
                for half in range(2):
                    r = fetch(w[bass.ds(kt * P, P), half * TILE:(half + 1) * TILE], None)
                    u = split(r)
                    need(PE, st["halves", u], hi, lo)
                    first = isinstance(i, int) and i == 0 and q == 0
                    last = isinstance(i, int) and i == nk // per - 1 and q == per - 1
                    for m in range(MT):
                        for n in range(2):
                            lhs = (s_hi[q][:, m * P:(m + 1) * P], s_lo[q][:, m * P:(m + 1) * P])
                            rhs = (whi[u][:, n * BANK:(n + 1) * BANK], wlo[u][:, n * BANK:(n + 1) * BANK])
                            ins = products(ps[:, 4 * m + 2 * half + n, :], lhs, rhs, first, last, None)
                    st["split", u] = [done(PE, ins)]
                    if ada is not None:
                        ada_half(ada, kt, half, isinstance(kt, int) and kt == 0)
                st["src", q] = st["split", u]

        repeat(nk // per, body, tail=1)
        return [Tok(tp, tp.n, None, 0)]

    def rsqrt_cols(dst, src, n, scale):
        t = done(POOL, POOL.tensor_scalar(dst, src, scale, EPS, ALU.mult, ALU.add))
        need(POOL, t)
        return done(POOL, POOL.tensor_tensor(dst, dst, mhalf[:, 0:n], ALU.pow))

    def row_rsqrt(src, slot, *ready, junk_ap=None):
        n = src.shape[-1] if len(src.shape) == 2 else int(np.prod(src.shape[1:]))
        need(SCA, ta.last(), *ready)
        t = done(SCA, SCA.activation(junk_ap, src, ACT.Square, accum_out=sq[:, slot:slot + 1]))
        need(POOL, t, st["mhalf"])
        return rsqrt_cols(sq2[:, slot:slot + 1], sq[:, slot:slot + 1], 1, 1.0 / n)

    def barrier():
        toks = [t.last() for t in (tp, tv, ta, tg)]
        for eng in (PE, DVE, SCA, POOL):
            need(eng, toks)
        for b in range(8):
            bank_free(b)
        return toks

    def norm_to_h(src, gain, shift, ready, dst=(None, None)):
        for m in range(MT):
            t = row_rsqrt(src[:, m, :], m, ready, junk_ap=norm_x[m][:, :])
            need(DVE, t)
            st["nx", m] = [done(DVE, DVE.tensor_scalar(norm_x[m][:, :], src[:, m, :], sq2[:, m:m + 1], None, ALU.mult))]
        for m in range(MT):
            need(PE, st["nx", m], st["ident"])
            for k in range(KD):
                ins = PE.transpose(ps[:, k // 2, (k % 2) * S + m * P:(k % 2) * S + (m + 1) * P],
                                   norm_x[m][:, k * P:(k + 1) * P], ident[:, :])
                if m == MT - 1 and k % 8 == 7:
                    st["nt", k // 8] = [done(PE, ins)]
        for g in range(2):
            need(DVE, st["nt", g])
            if g:
                need(DVE, st["nlo"])
            for k in range(8 * g, 8 * g + 8):
                src_ps = ps[:, k // 2, (k % 2) * S:(k % 2 + 1) * S]
                sh = shift[:, k:k + 1] if shift is not None else None
                ins = DVE.tensor_scalar(norm_f[:, k - 8 * g, :], src_ps, gain[:, k:k + 1], sh, ALU.mult,
                                        *([ALU.add] if shift is not None else []))
                if k % 4 == 3:
                    f = done(DVE, ins)
                    need(SCA, f)
                    hi = done(SCA, SCA.activation(h_hi[:, k - 3:k + 1, :], norm_f[:, k - 3 - 8 * g:k + 1 - 8 * g, :], ACT.Copy))
                    st["nhi", k // 4] = [hi]
            for k in (8 * g + 3, 8 * g + 7):
                need(DVE, st["nhi", k // 4])
                lo = done(DVE, DVE.tensor_tensor(h_lo[:, k - 3:k + 1, :], norm_f[:, k - 3 - 8 * g:k + 1 - 8 * g, :],
                                                 r32(h_hi[:, k - 3:k + 1, :]), ALU.subtract))
            st["nlo"] = [lo]
        for b in range(8):
            bank_free(b, lo)
        return [lo, hi]

    def copy_post(banks, dst, width):
        def step():
            need(SCA, st["full", banks[0]])
            t = done(SCA, SCA.activation(dst, ps[:, banks[0]:banks[1] + 1, 0:width], ACT.Copy))
            for b in banks:
                bank_free(b, t)
        return [step]

    def rope(src, dst, heads, half, rot, m, *ready):
        need(DVE, *ready)
        r0 = rot[0]
        cos = trig[:, 0, m, r0:r0 + half]
        sin = trig[:, 1, m, r0:r0 + half]
        s4 = src.rearrange("p h (a b) -> p h a b", a=2)
        d4 = dst.rearrange("p h (a b) -> p h a b", a=2)
        t4 = rp_t[:, 0:heads * 2 * half].rearrange("p (h a b) -> p h a b", a=2, b=half)
        u = [rp_u[i][:, 0:heads * half].rearrange("p (h b) -> p h b", b=half) for i in range(2)]
        need(DVE, st.get("rope"))
        DVE.tensor_tensor(t4, s4, cos.unsqueeze(1).unsqueeze(1).to_broadcast([P, heads, 2, half]), ALU.mult)
        DVE.tensor_tensor(u[0], s4[:, :, 1, :], sin.unsqueeze(1).to_broadcast([P, heads, half]), ALU.mult)
        t = done(DVE, DVE.tensor_tensor(u[1], s4[:, :, 0, :], sin.unsqueeze(1).to_broadcast([P, heads, half]), ALU.mult))
        need(DVE, t)
        DVE.tensor_tensor(d4[:, :, 0, :], t4[:, :, 0, :], u[0], ALU.subtract)
        t = done(DVE, DVE.tensor_tensor(d4[:, :, 1, :], t4[:, :, 1, :], u[1], ALU.add))
        st["rope"] = [t]
        return t

    def transposes(banks, items):
        for col, src in items:
            ins = PE.transpose(ps[:, banks + col // BANK, col % BANK:col % BANK + P], src, ident[:, :])
        return done(PE, ins)

    def attention(p, prep, units, vs, outs, scale, masks, buf, cnt=None, diff=False, nkts=(1, 2)):
        QT, KT, Sc, PT = buf
        b0 = 4 * p
        tok = yield from prep(p, QT, KT)
        for t in range(MT):
            nkt = nkts[t]
            nk = nkt * P
            need(PE, tok, st.get(("set", p)))
            for u in units:
                ins = u(t, nk)
            s_done = done(PE, ins)
            yield
            need(DVE, s_done)
            s_ps = ps[:, b0:b0 + 2, :].rearrange("p b (u n) -> p (b u) n", u=2)[:, :, 0:nk]
            sc = Sc[:, :].rearrange("p (u n) -> p u n", u=4)[:, :, 0:nk]
            mk = masks(t)
            if mk is None:
                mt = done(DVE, DVE.tensor_copy(sc, s_ps))
            else:
                mt = done(DVE, DVE.tensor_tensor(sc, s_ps, mk.unsqueeze(1).to_broadcast([P, 4, nk]), ALU.add))
            need(DVE, mt)
            mx = done(DVE, DVE.tensor_reduce(nm[p][:, :], sc, AX, ALU.max))
            need(DVE, mx)
            ng = done(DVE, DVE.tensor_scalar(nm[p][:, :], nm[p][:, :], -scale, None, ALU.mult))
            yield
            need(SCA, ng)
            for i in range(4):
                e = done(SCA, SCA.activation(sc[:, i, :], sc[:, i, :], ACT.Exp, bias=nm[p][:, i:i + 1], scale=scale,
                                             accum_out=den[p][:, i:i + 1]))
            yield
            need(DVE, e)
            if cnt is not None:
                w = done(DVE, DVE.tensor_tensor(sc, sc, cnt(t).unsqueeze(1).to_broadcast([P, 4, nk]), ALU.mult))
                need(DVE, w)
                e = done(DVE, DVE.tensor_reduce(den[p][:, :], sc, AX, ALU.add))
                need(DVE, e)
            rc = done(DVE, DVE.reciprocal(rden[p][:, :], den[p][:, :]))
            n_out = 4
            if diff:
                need(DVE, rc)
                rv = rden[p][:, :].rearrange("p (h m) -> p h m", m=2)
                rl = done(DVE, DVE.tensor_scalar(rv[:, :, 1], rv[:, :, 1], lam[:, 3:4], None, ALU.mult))
                need(DVE, rl)
                w = done(DVE, DVE.tensor_tensor(sc, sc, rden[p][:, :].unsqueeze(2).to_broadcast([P, 4, nk]), ALU.mult))
                need(DVE, w)
                s4 = Sc[:, :].rearrange("p (h m n) -> p h m n", h=2, m=2)[:, :, :, 0:nk]
                e = done(DVE, DVE.tensor_tensor(s4[:, :, 0, :], s4[:, :, 0, :], s4[:, :, 1, :], ALU.add))
                n_out = 2
            yield
            need(PE, e)
            step = 2 if diff else 1
            pt = transposes(b0 + 2, [(kt * BANK + i * P, sc[:, i * step, kt * P:(kt + 1) * P])
                                     for kt in range(nkt) for i in range(n_out)])
            need(SCA, pt)
            pv = PT[:, :].rearrange("p (k n) -> p k n", k=2)[:, 0:nkt, 0:n_out * P]
            pe_ = done(SCA, SCA.activation(pv, ps[:, b0 + 2:b0 + 2 + nkt, 0:n_out * P], ACT.Copy))
            yield
            need(PE, pe_)
            for i in range(n_out):
                for kt in range(nkt):
                    ins = PE.matmul(ps[:, b0, i * P:(i + 1) * P], pv[:, kt, i * P:(i + 1) * P], vs(i, kt),
                                    start=kt == 0, stop=kt == nkt - 1)
            o = done(PE, ins)
            yield
            need(DVE, o, rc)
            o_ps = ps[:, b0, 0:n_out * P].rearrange("p (h n) -> p h n", h=n_out)
            if diff:
                f = done(DVE, DVE.tensor_copy(outs(t), o_ps))
            else:
                f = done(DVE, DVE.tensor_tensor(outs(t), o_ps, rden[p][:, :].unsqueeze(2).to_broadcast([P, 4, P]), ALU.mult))
            st["set", p] = [f]
            yield

    def run_two(gens):
        live = {}
        gens = list(gens)
        turn = 0
        while gens or live:
            for p in range(2):
                if p not in live and gens and gens[0][0] == p:
                    live[p] = gens.pop(0)[1]
            if turn in live:
                try:
                    next(live[turn])
                except StopIteration:
                    del live[turn]
            turn ^= 1

    def qk_prep(q_items, k_items, extra=None):
        def prep(p, QT, KT):
            need(PE, st.get(("set", p)))
            tq = transposes(4 * p, q_items)
            tk = transposes(4 * p + 2, k_items)
            yield
            need(SCA, tq)
            eq = done(SCA, SCA.activation(QT[:, :].rearrange("p (b n) -> p b n", b=2), ps[:, 4 * p:4 * p + 2, :], ACT.Copy))
            need(DVE, tk)
            ek = done(DVE, DVE.tensor_copy(KT[:, :].rearrange("p (b n) -> p b n", b=2), ps[:, 4 * p + 2:4 * p + 4, :]))
            toks = [eq, ek]
            if extra:
                need(PE, eq)
                toks += extra(p)
            yield
            return toks
        return prep

    def head_norm(view, gain_row, factor, *ready):
        need(DVE, *ready)
        sqv = hsq[:, :].rearrange("p (h n) -> p h n", h=8)
        t = done(DVE, DVE.tensor_tensor(sqv, view, view, ALU.mult))
        need(DVE, t)
        t = done(DVE, DVE.tensor_reduce(sq[:, 0:8], sqv, AX, ALU.add))
        need(POOL, t)
        g = rsqrt_cols(sq2[:, 0:8], sq[:, 0:8], 8, 1.0 / P)
        need(DVE, g)
        t = done(DVE, DVE.tensor_tensor(view, view, sq2[:, 0:8].unsqueeze(2).to_broadcast([P, 8, P]), ALU.mult))
        need(DVE, t)
        t = done(DVE, DVE.scalar_tensor_tensor(view, view, factor, gain_row.unsqueeze(1).to_broadcast([P, 8, P]), ALU.mult, ALU.mult))
        return t

    def gate_bcast(part, gcol):
        need(DVE, st["mod", part], st["cols"])
        g = done(DVE, DVE.tensor_tensor(gsc[:, :], mod[:, part * 16:part * 16 + 16], cols[:, gcol:gcol + 16], ALU.mult))
        need(DVE, g, st["ident"])
        t = done(DVE, DVE.tensor_tensor(diag[:, :, :], ident[:, :].unsqueeze(1).to_broadcast([P, KD, P]),
                                        gsc[:, :].unsqueeze(2).to_broadcast([P, KD, P]), ALU.mult))
        t = done(DVE, DVE.memset(ones_sq[:, :], 1.0))
        need(PE, t)
        for n in range(4):
            ins = PE.matmul(ps[:, n, :], ones_sq[:, :], diag[:, 4 * n:4 * n + 4, :].rearrange("p k n -> p (k n)"), start=True, stop=True)
        t = done(PE, ins)
        need(SCA, t)
        t = done(SCA, SCA.activation(gate_row[:, :].rearrange("p (b n) -> p b n", b=4), ps[:, 0:4, :], ACT.Copy))
        for b in range(4):
            bank_free(b, t)
        return t

    def transposed_mix(srcs, *ready):
        need(PE, *ready)
        last = []
        for g in range(4):
            for k in range(4 * g, 4 * g + 4):
                for m in range(MT):
                    ins = PE.transpose(ps[:, k // 2, (k % 2) * S + m * P:(k % 2) * S + (m + 1) * P], srcs(k, m), ident[:, :])
            t = done(PE, ins)
            eng = (SCA, DVE)[g % 2]
            need(eng, t)
            dst = mixT[:, 4 * g:4 * g + 4, :].rearrange("p (b k) n -> p b (k n)", b=2)
            s_ = ps[:, 2 * g:2 * g + 2, :]
            c = done(eng, eng.activation(dst, s_, ACT.Copy) if eng is SCA else eng.tensor_copy(dst, s_))
            last.append(c)
        for b in range(8):
            bank_free(b, *last)
        return last

    gout = [sb("g_out_rows", "big", 56 * KB, [P]), sb("g_sub_rows", "big", 56 * KB + 512, [P])]
    q = SCA
    par = []

    def pload(dst, src, eng=None):
        par.append(t_par.done((eng or q).dma_start(dst, src)))

    z = done(POOL, POOL.memset(vec2[:, :], 0.0))
    need(q, z)
    pload(vec1[0:16, :], a["c"].rearrange("o (k n) -> (o k) n", n=P))
    pload(vec1[16:112, :], a["b_ada"].rearrange("o (k n) -> (o k) n", n=P))
    pload(vec1[112:128, :], a["g_post_attn"].rearrange("o (k n) -> (o k) n", n=P))
    row = 0
    for name in ("g_pre_attn", "g_pre_ffn", "g_mix_2", "g_cross_2", "g_mem_2", "g_mlp_2", "g_cq_2", "g_ckv_2", "g_post_ffn"):
        n = a[name].shape[1] // P
        pload(vec2[row:row + n, :], a[name].rearrange("o (k n) -> (o k) n", n=P))
        row += n
    assert 128 + row == NCOL
    pload(ident[:, :], a["k_ident"])
    pload(causal[:, :], a["k_causal"])
    pload(chunk[:, :], a["k_chunk"])
    pload(count[:, :], a["k_count"])
    pload(dilated[:, :], a["k_dilated"])
    pload(inv[:, :], a["k_inv"].to_broadcast([P, NROT]))
    for i, n in enumerate(("positions", "positions_2")):
        for m in range(MT):
            pload(posi[:, 2 * i + m:2 * i + m + 1], a[n].rearrange("o (m p) -> m p o", p=P)[m])
    for i, n in enumerate(("lambda_q1", "lambda_k1", "lambda_q2", "lambda_k2")):
        pload(lamv[:, i, :], a[n].to_broadcast([P, 64]))
    pload(gout[0][:, :], a["g_out_a"].to_broadcast([P, P]))
    pload(gout[1][:, :], a["g_subln_b"].to_broadcast([P, P]))
    memt = sb("mem_rows", "x", 0, [MT, D])
    m_in = t_mem.done(q.dma_start(memt[:, :, :], a["mem_2"][0].rearrange("(m p) d -> p m d", p=P)))
    par_tok = [par[-1]]

    ONES = done(DVE, DVE.memset(one[:, :], 1.0))
    MH = done(POOL, POOL.memset(mhalf[:, :], -0.5))
    st["one"], st["mhalf"], st["ident"] = [ONES], [MH], par_tok

    need(PE, par_tok, z)
    t = transposes(0, [(0, vec1[:, :]), (P, vec2[:, :])])
    need(DVE, t)
    st["cols"] = [done(DVE, DVE.tensor_copy(cols[:, 0:NCOL], ps[:, 0, 0:NCOL]))]
    need(SCA, st["cols"])
    t = done(SCA, SCA.activation(sil_t[:, :], cols[:, 0:16], ACT.Exp, scale=-1.0))
    need(DVE, t)
    t = done(DVE, DVE.tensor_scalar(sil_t[:, :], sil_t[:, :], 1.0, None, ALU.add))
    need(DVE, t)
    t = done(DVE, DVE.reciprocal(sil_t[:, :], sil_t[:, :]))
    need(DVE, t)
    st["silu"] = [done(DVE, DVE.tensor_tensor(sil[:, :], sil_t[:, :], cols[:, 0:16], ALU.mult))]
    need(DVE, par_tok)
    t = done(DVE, DVE.tensor_tensor(lamv[:, 0:4:2, :], lamv[:, 0:4:2, :], lamv[:, 1:4:2, :], ALU.mult))
    need(DVE, t)
    t = done(DVE, DVE.tensor_reduce(lam[:, 0:2], lamv[:, 0:4:2, :], AX, ALU.add))
    need(SCA, t)
    t = done(SCA, SCA.activation(lam[:, 0:2], lam[:, 0:2], ACT.Exp))
    need(DVE, t)
    t = done(DVE, DVE.tensor_tensor(lam[:, 2:3], lam[:, 1:2], lam[:, 0:1], ALU.subtract))
    need(DVE, t)
    t = done(DVE, DVE.tensor_scalar(lam[:, 3:4], lam[:, 2:3], -(0.8 - 0.6), None, ALU.add))
    t = done(DVE, DVE.tensor_copy(posf[:, :], posi[:, :]))
    need(DVE, t)
    for m in range(MT):
        DVE.tensor_scalar(ang[:, m, 0:NROT1], inv[:, 0:NROT1], posf[:, m:m + 1], None, ALU.mult)
        t = done(DVE, DVE.tensor_scalar(ang[:, m, NROT1:], inv[:, NROT1:], posf[:, 2 + m:3 + m], None, ALU.mult))
    need(DVE, t)
    for c in range(2):
        t = done(DVE, DVE.tensor_scalar(rnd[:, :, :], ang[:, :, :], 1 / PI2, 0.25 * (1 - c), ALU.mult, ALU.add))
        need(DVE, t)
        t = done(DVE, DVE.tensor_scalar(rnd[:, :, :], rnd[:, :, :], MAGIC, None, ALU.add))
        need(DVE, t)
        t = done(DVE, DVE.tensor_scalar(rnd[:, :, :], rnd[:, :, :], -MAGIC, None, ALU.add))
        src = ang[:, :, :]
        for piece in (PI_A, PI_B, PI_C):
            need(DVE, t)
            t = done(DVE, DVE.scalar_tensor_tensor(angr[:, c, :, :], rnd[:, :, :], -piece, src, ALU.mult, ALU.add))
            src = angr[:, c, :, :]
        if c == 0:
            need(DVE, t)
            t = done(DVE, DVE.tensor_scalar(src, src, np.pi / 2, None, ALU.add))
        need(DVE, t)
        t = done(DVE, DVE.tensor_scalar(src, src, 3.1415925, -3.1415925, ALU.min, ALU.max))
        need(DVE, t)
    need(SCA, t)
    st["trig"] = [done(SCA, SCA.activation(trig[:, :, :, :], angr[:, :, :, :], ACT.Sin))]

    need(SCA, m_in)
    need(DVE, m_in)
    ready = norm_to_h(memt, cols[:, C_GMEM:C_GMEM + 16], None, [m_in])
    need(q, ready)
    x_in = t_x.done(q.dma_start(x[:, :, :], a["x"][0].rearrange("(m p) d -> p m d", p=P)))
    A_h = (h_hi, h_lo)
    need(PE, ready)
    kx = sb("cross_k", "big", 44 * KB, [MT, 512])
    col_slot(a["w_k_cross_2"][0], 0, KD, (0,), 512, (0, 1), A_h)
    col_slot(a["w_v_cross_2"][0], 0, KD, (0,), 512, (2, 3), A_h, copy_post((0, 1), kx[:, :, :], 512))
    for s_ in copy_post((2, 3), vx[:, :, :], 512):
        s_()
    need(PE, ta.last())
    t = transposes(4, [(hh * S + m * P, kx[:, m, hh * P:(hh + 1) * P]) for hh in range(4) for m in range(MT)])
    need(DVE, t)
    kxt = done(DVE, DVE.tensor_copy(kxT[:, :, :].rearrange("p (b k) n -> p b (k n)", b=2), ps[:, 4:6, :]))
    bank_free(4, kxt)
    bank_free(5, kxt)

    for part in (0, 1):
        def ada_body(i, part=part):
            for qq in range(4):
                for half in range(2):
                    ada_half(part, i * 4 + qq, half, isinstance(i, int) and i == 0 and qq == 0)
        repeat(4, ada_body)
        ada_finish(part, 6)

    def modulated_gain(part_scale, gcol):
        need(DVE, st["mod", part_scale])
        return done(DVE, DVE.scalar_tensor_tensor(gsc[:, :], mod[:, part_scale * 16:part_scale * 16 + 16], 1.0,
                                                  cols[:, gcol:gcol + 16], ALU.add, ALU.mult))

    t = modulated_gain(1, C_GPRE)
    need(DVE, t)
    barrier()
    ready = norm_to_h(x, gsc, mod[:, 0:16], [x_in])
    need(PE, ready)
    barrier()

    def cols_of(w, i, slot, pair=1024):
        return None

    def pair_stage(w, n, dst, ada=None, base=0, first_posts=()):
        def body(i):
            prev = copy_post((2, 3), dst(i - 1, 1), 512) if not (isinstance(i, int) and i == 0) else list(first_posts)
            def extra(slot):
                def f(j):
                    if ada is not None and j % 2 == 1:
                        g = slot * 8 + j
                        idx = g // 2
                        kt = i * 4 + idx // 2
                        ada_half(ada, kt, idx % 2, isinstance(i, int) and i == 0 and idx // 2 == 0)
                return f
            c = lambda s: bass.ds(base + i * 1024 + 512 * s, 512)
            col_slot(w, 0, KD, c(0), 512, (0, 1), A_h, prev, extra=extra(0))
            col_slot(w, 0, KD, c(1), 512, (2, 3), A_h, copy_post((0, 1), dst(i, 0), 512), extra=extra(1))
        repeat(n, body, peel=2 if n > 2 else n)
        return copy_post((2, 3), dst(n - 1, 1), 512)

    dst1 = lambda b: (lambda i, s: proj[:, :, bass.ds(b + i * 1024 + 512 * s, 512)])
    rest = pair_stage(a["w_in"][0], 4, dst1(0), ada=2)
    st["proj_part"] = []
    rest = pair_stage(a["w_in"][0], 2, dst1(4096), base=4096, first_posts=rest)
    for s_ in rest:
        s_()
    ada_finish(2, 6)
    barrier()

    need(DVE, st["trig"])
    qkA = [proj[:, m, 0:2048].rearrange("p (h n) -> p h n", n=128) for m in range(MT)]
    qkB = [proj[:, m, 3072:5120].rearrange("p (h n) -> p h n", n=64) for m in range(MT)]
    for m in range(MT):
        ropeA = rope(qkA[m], qkA[m], 16, 64, R_A, m)
    for m in range(MT):
        ropeB = rope(qkB[m], qkB[m], 32, 32, R_B, m)
    barrier()
    work1 = [[sb(f"w1_{n}{p}", "h", (16 * p + 4 * i) * KB, [TILE]) for i, n in enumerate(("qT", "kT", "sc", "pT"))] for p in range(2)]
    st["set", 0] = st["set", 1] = []

    def unit(p, place, pairs):
        def f(t, nk):
            dst = ps[:, 4 * p + place[0], place[1]:place[1] + nk]
            for n, (l, r) in enumerate(pairs):
                ins = PE.matmul(dst, l(t), r(nk), start=n == 0, stop=n == len(pairs) - 1)
            return ins
        return f

    def groupA(g):
        p = g % 2
        QT, KT = (w[:, :].rearrange("p (u n) -> p u n", u=4) for w in work1[p][:2])
        items = lambda base: [(i * S + m * P, proj[:, m, base + (4 * g + i) * P:base + (4 * g + i + 1) * P]) for i in range(4) for m in range(MT)]
        units = [unit(p, (i // 2, (i % 2) * S), [(lambda t, i=i: QT[:, i, t * P:(t + 1) * P], lambda nk, i=i: KT[:, i, 0:nk])]) for i in range(4)]
        return p, attention(p, qk_prep(items(0), items(1024)), units,
                            lambda i, kt: proj[:, kt, 2048 + (4 * g + i) * P:2048 + (4 * g + i + 1) * P],
                            lambda t: proj[:, t, 512 * g:512 * g + 512].rearrange("p (h n) -> p h n", h=4),
                            128 ** -0.5, lambda t: dilated[:, P:S] if t == 0 else dilated[:, :], work1[p],
                            cnt=lambda t: count[:, P:S] if t == 0 else count[:, :])

    def groupB(g):
        p = g % 2
        QT, KT = (w[:, :].rearrange("p (u n) -> p u n", u=4) for w in work1[p][:2])
        items = lambda base: [(mu * S + m * P, proj[:, m, base + 512 * mu + P * g:base + 512 * mu + P * (g + 1)]) for mu in range(2) for m in range(MT)]
        units = []
        for e in range(2):
            for mu in range(2):
                units.append(unit(p, (e, mu * S), [(lambda t, e=e, mu=mu: QT[64 * e:64 * e + 64, mu, t * P:(t + 1) * P],
                                                    lambda nk, e=e, mu=mu: KT[64 * e:64 * e + 64, mu, 0:nk])]))
        return p, attention(p, qk_prep(items(3072), items(4096)), units,
                            lambda i, kt: proj[:, kt, 5120 + (2 * g + i) * P:5120 + (2 * g + i + 1) * P],
                            lambda t: proj[:, t, 1024 + 256 * g:1024 + 256 * g + 256].rearrange("p (h n) -> p h n", h=2),
                            64 ** -0.5, lambda t: causal[:, P:S] if t == 0 else causal[:, :], work1[p], diff=True)

    run_two([groupA(g) for g in range(2)])
    barrier()
    run_two([groupB(g) for g in range(4)])
    barrier()
    for m in range(MT):
        head_norm(proj[:, m, 0:1024].rearrange("p (h n) -> p h n", h=8), gout[0][:, :], 1.0)
        head_norm(proj[:, m, 1024:2048].rearrange("p (h n) -> p h n", h=8), gout[1][:, :], 1.0 - (0.8 - 0.6), tv.last())
    barrier()
    gate_bcast(2, C_GPOSTA)
    barrier()
    mix_ready = transposed_mix(lambda k, m: proj[:, m, k * P:(k + 1) * P], tv.last())
    barrier()

    def post_norm_add(y_done):
        for m in range(MT):
            y = ps[:, 4 * m:4 * m + 4, :]
            need(SCA, y_done, ta.last())
            t = done(SCA, SCA.activation(junk[:, :].rearrange("p (b n) -> p b n", b=4), y, ACT.Square, accum_out=sq[:, m:m + 1]))
            need(POOL, t)
            g = rsqrt_cols(sq2[:, m:m + 1], sq[:, m:m + 1], 1, 1.0 / D)
            need(DVE, g, y_done, tv.last())
            tmp = post_tmp[:, :].rearrange("p (b n) -> p b n", b=4)
            t = done(DVE, DVE.scalar_tensor_tensor(tmp, y, sq2[:, m:m + 1], gate_row[:, :].rearrange("p (b n) -> p b n", b=4), ALU.mult, ALU.mult))
            need(DVE, t)
            done(DVE, DVE.tensor_tensor(x[:, m, :], x[:, m, :], post_tmp[:, :], ALU.add))

    def plain_add(y_done):
        need(DVE, y_done)
        for m in range(MT):
            done(DVE, DVE.tensor_tensor(x[:, m, :].rearrange("p (b n) -> p b n", b=4), x[:, m, :].rearrange("p (b n) -> p b n", b=4),
                                        ps[:, 4 * m:4 * m + 4, :], ALU.add))

    y_done = row_stage(a["w_out"][0], mixT, KD, mix_ready, ada=3)
    post_norm_add(y_done)
    barrier()
    ada_finish(3, 0)

    def ada4(i):
        for qq in range(4):
            for half in range(2):
                ada_half(4, i * 4 + qq, half, isinstance(i, int) and i == 0 and qq == 0)
    repeat(4, ada4)
    ada_finish(4, 6)
    t = modulated_gain(4, C_GFFN)
    need(DVE, t)
    barrier()
    ready = norm_to_h(x, gsc, mod[:, 3 * 16:4 * 16], [])
    barrier()

    def hidden_out(dst, i, banks, src, tok_key):
        def tr():
            need(PE, st[tok_key], st.get(("bank", banks[0])), st.get(("bank", banks[1])))
            for c in range(4):
                for m in range(MT):
                    ins = PE.transpose(ps[:, banks[c // 2], (c % 2) * S + m * P:(c % 2) * S + (m + 1) * P], src[:, m, c * P:(c + 1) * P], ident[:, :])
            st["hid_t", banks[0]] = [done(PE, ins)]

        def ev():
            need(SCA, st["hid_t", banks[0]])
            d = dst[:, bass.ds(i * 4, 4), :].rearrange("p (b k) n -> p b (k n)", b=2)
            t = done(SCA, SCA.activation(d, ps[:, banks[0]:banks[1] + 1, :], ACT.Copy))
            bank_free(banks[0], t)
            bank_free(banks[1], t)
        return [tr, ev]

    def gate_steps():
        g = ps[:, 0:2, :]

        def ex():
            need(SCA, st["full", 0], st.get(("hid_t", 4)))
            st["sg"] = [done(SCA, SCA.activation(sg1[:, :, :], g, ACT.Exp, scale=-1.0))]

        def plus():
            need(DVE, st["sg"])
            st["sg"] = [done(DVE, DVE.tensor_scalar(sg1[:, :, :], sg1[:, :, :], 1.0, None, ALU.add))]

        def rec():
            need(DVE, st["sg"])
            st["sg"] = [done(DVE, DVE.reciprocal(sg1[:, :, :], sg1[:, :, :]))]

        def mul():
            need(DVE, st["sg"])
            t = done(DVE, DVE.tensor_tensor(sg1[:, :, :], g, sg1[:, :, :], ALU.mult))
            st["sg"] = [t]
            bank_free(0, t)
            bank_free(1, t)
        return [ex, plus, rec, mul]

    def up_steps(i):
        def mul():
            need(DVE, st["full", 2], st["sg"])
            t = done(DVE, DVE.tensor_tensor(sg1[:, :, :], ps[:, 2:4, :], sg1[:, :, :], ALU.mult))
            st["sgu"] = [t]
            bank_free(2, t)
            bank_free(3, t)
        return [mul] + hidden_out(hid1, i, (4, 5), sg1, "sgu")

    def ffn1(i):
        prev = up_steps(i - 1) if not (isinstance(i, int) and i == 0) else []
        c = bass.ds(i * 512, 512)
        col_slot(a["w_gate"][0], 0, KD, c, 512, (0, 1), A_h, prev)
        col_slot(a["w_up"][0], 0, KD, c, 512, (2, 3), A_h, gate_steps())
    repeat(DFF1 // 512, ffn1, peel=2)
    for s_ in up_steps(DFF1 // 512 - 1):
        s_()
    barrier()
    def ada5(i):
        for qq in range(4):
            for half in range(2):
                ada_half(5, i * 4 + qq, half, isinstance(i, int) and i == 0 and qq == 0)
    repeat(4, ada5)
    ada_finish(5, 6)
    barrier()
    gate_bcast(5, C_GPOSTF)
    barrier()
    y_done = row_stage(a["w_down"][0], hid1, DFF1 // P, [])
    barrier()
    post_norm_add(y_done)
    barrier()

    ready = norm_to_h(x, cols[:, C_GMIX:C_GMIX + 16], None, [])
    barrier()
    pj = sb("proj_2", "big", 0, [MT, IN2])
    dst2 = lambda i, s: pj[:, :, bass.ds(i * 1024 + 512 * s, 512)]
    rest = pair_stage(a["w_in_2"][0], 4, dst2)
    col_slot(a["w_in_2"][0], 0, KD, (4096,), 512, (0, 1), A_h, rest)
    col_slot(a["w_in_2"][0], 0, KD, (4608,), 400, (2, 3), A_h, copy_post((0, 1), pj[:, :, 4096:4608], 512))
    for s_ in copy_post((2, 3), pj[:, :, 4608:5008], 400):
        s_()
    barrier()
    O_CQ, O_CKV, O_KR, O_QD, O_KD, O_VD, O_QI, O_KI, O_WI = 0, 512, 768, 832, 1856, 2880, 3904, 4928, 4992

    cq_hi = sb("cq_hi", "big", 40 * KB, [6, S], F32R)
    cq_lo = sb("cq_lo", "big", 46 * KB, [6, S], F32R)
    cq_f = sb("cq_f", "big", 52 * KB, [6, S])
    for m in range(MT):
        for s_i, (c0, n) in enumerate(((O_CQ, 512), (O_CKV, 256))):
            t = row_rsqrt(pj[:, m, c0:c0 + n], 2 * m + s_i, tv.last(), junk_ap=junk[:, 0:n])
            need(DVE, t)
            t = done(DVE, DVE.tensor_scalar(pj[:, m, c0:c0 + n], pj[:, m, c0:c0 + n], sq2[:, 2 * m + s_i:2 * m + s_i + 1], None, ALU.mult))
    need(PE, t)
    t = transposes(0, [(k * S + m * P, pj[:, m, k * P:(k + 1) * P]) for k in range(6) for m in range(MT)])
    need(DVE, t)
    for k in range(6):
        t = done(DVE, DVE.tensor_scalar(cq_f[:, k, :], ps[:, k // 2, (k % 2) * S:(k % 2 + 1) * S], cols[:, C_GCQ + k:C_GCQ + k + 1], None, ALU.mult))
    need(SCA, t)
    hi = done(SCA, SCA.activation(cq_hi[:, :, :], cq_f[:, :, :], ACT.Copy))
    need(DVE, hi, t)
    lo = done(DVE, DVE.tensor_tensor(cq_lo[:, :, :], cq_f[:, :, :], r32(cq_hi[:, :, :]), ALU.subtract))
    need(PE, hi, lo)
    barrier()
    qm = sb("mla_q", "h", 0, [MT, 1536])
    kvm = sb("mla_kv", "h", 12 * KB, [MT, 2048])
    rest = []
    for n in range(3):
        b = (0, 1) if n % 2 == 0 else (2, 3)
        col_slot(a["w_qb_2"][0], 0, 4, (n * 512,), 512, b, (cq_hi, cq_lo), rest)
        rest = copy_post(b, qm[:, :, n * 512:(n + 1) * 512], 512)
    ck = (cq_hi[:, 4:6, :], cq_lo[:, 4:6, :])
    for n in range(4):
        b = (2, 3) if n % 2 == 0 else (0, 1)
        col_slot(a["w_kvb_2"][0], 0, 2, (n * 512,), 512, b, ck, rest)
        rest = copy_post(b, kvm[:, :, n * 512:(n + 1) * 512], 512)
    for s_ in rest:
        s_()
    barrier()

    qr = sb("mla_q_rope", "h", 28 * KB, [MT, 8, 64])
    pad = sb("padded_keys", "acc", 8 * KB, [MT, 2, P])
    krT = sb("k_rope_T", "acc", 10 * KB, [2, S])
    kiT = sb("k_idx_T", "acc", 12 * KB, [2, S])
    selb = sb("selection", "acc", 14 * KB, [MT, S])
    rp_t = sb("rope_t2", "big", 40 * KB, [D])
    rp_u = [sb(f"rope_v{i}", "big", 48 * KB + 4 * KB * i, [TILE]) for i in range(2)]
    for m in range(MT):
        qv = pj[:, m, O_QD:O_QD + 2048].rearrange("p (h n) -> p h n", n=128)[:, :, 0:32]
        rope(qv, qv, 16, 16, R_DSA, m)
        iv = pj[:, m, O_QI:O_QI + 1024].rearrange("p (h n) -> p h n", n=64)[:, :, 0:16]
        rope(iv, iv, 16, 8, R_IDX, m)
        kv_ = pj[:, m, O_KI:O_KI + 64].rearrange("p (h n) -> p h n", h=1)[:, :, 0:16]
        rope(kv_, kv_, 1, 8, R_IDX, m)
        rope(qm[:, m, :].rearrange("p (h n) -> p h n", n=192)[:, :, 128:192], qr[:, m, :, :], 8, 32, R_MLA, m)
        kr_ = pj[:, m, O_KR:O_KR + 64].rearrange("p (h n) -> p h n", h=1)
        rope(kr_, kr_, 1, 32, R_MLA, m)
    for n, (c0, dst) in enumerate(((O_KR, krT), (O_KI, kiT))):
        t = done(DVE, DVE.memset(pad[:, :, :, :], 0.0))
        need(DVE, t)
        for m in range(MT):
            DVE.tensor_copy(pad[:, m, 0, 0:64], pj[:, m, c0:c0 + 64])
            t = done(DVE, DVE.tensor_copy(pad[:, m, 1, 64:128], pj[:, m, c0:c0 + 64]))
        need(PE, t)
        t = transposes(n, [(e * S + m * P, pad[:, m, e, :]) for e in range(2) for m in range(MT)])
        need(DVE, t)
        t = done(DVE, DVE.tensor_copy(dst[:, :, :].rearrange("p e n -> p (e n)"), ps[:, n, :]))
    for m in range(MT):
        t = done(DVE, DVE.tensor_scalar(wi[:, m, :], pj[:, m, O_WI:O_WI + 16], 16 ** -0.5 * 64 ** -0.5, None, ALU.mult))
    barrier()

    qiT = sb("q_idx_T", "big", 40 * KB, [8, P])
    rel = [sb(f"idx_relu{i}", "big", 44 * KB + 4 * KB * i, [4, S]) for i in range(2)]
    score = sb("score", "big", 52 * KB, [S])
    kept = sb("score_left", "big", 53 * KB, [S])
    for m in range(MT):
        nk = (m + 1) * P
        need(PE, tv.last(), ta.last())
        t = transposes(0, [(j * P, pj[:, m, O_QI + j * P:O_QI + (j + 1) * P]) for j in range(8)])
        need(SCA, t)
        qt = done(SCA, SCA.activation(qiT[:, :, :].rearrange("p (b k) n -> p b (k n)", b=2), ps[:, 0:2, :], ACT.Copy))
        need(PE, qt)
        stt = None
        for g in range(4):
            b0 = 2 + 2 * (g % 2)
            need(PE, st.get(("idx", g % 2)))
            for i in range(4):
                hh = 4 * g + i
                ins = PE.matmul(ps[:, b0 + i // 2, (i % 2) * S:(i % 2) * S + nk], qiT[:, hh // 2, :], kiT[:, hh % 2, 0:nk], start=True, stop=True)
            t = done(PE, ins)
            need(SCA, t, st.get(("idx_v", g % 2)))
            e = done(SCA, SCA.activation(rel[g % 2][:, :, 0:nk], ps[:, b0:b0 + 2, :].rearrange("p b (u n) -> p (b u) n", u=2)[:, :, 0:nk], ACT.Relu))
            st["idx", g % 2] = [e]
            need(DVE, e)
            for i in range(4):
                hh = 4 * g + i
                need(DVE, stt)
                if hh == 0:
                    stt = done(DVE, DVE.tensor_scalar(score[:, 0:nk], rel[0][:, 0, 0:nk], wi[:, m, 0:1], None, ALU.mult))
                else:
                    stt = done(DVE, DVE.scalar_tensor_tensor(score[:, 0:nk], rel[g % 2][:, i, 0:nk], wi[:, m, hh:hh + 1], score[:, 0:nk], ALU.mult, ALU.add))
            st["idx_v", g % 2] = [stt]
        if m == 0:
            need(DVE, stt)
            stt = done(DVE, DVE.memset(score[0:64, 64:128], DROPPED))
        else:
            need(DVE, stt)
            stt = done(DVE, DVE.memset(score[0:64, 192:256], DROPPED))
        src = score
        for rnd_ in range(TOPK // 8):
            need(DVE, stt)
            t = done(DVE, DVE.max(m8[:, :], src[:, 0:nk]))
            need(DVE, t)
            stt = done(DVE, DVE.match_replace(kept[:, 0:nk], m8[:, :], src[:, 0:nk], TAKEN))
            src = kept
        need(DVE, stt)
        stt = done(DVE, DVE.tensor_scalar(selb[:, m, 0:nk], kept[:, 0:nk], (DROPPED + TAKEN) / 2, NEG, ALU.is_ge, ALU.mult))
    barrier()

    names = ("qT", "kT")
    work2 = [[sb(f"w2_{n}{p}", "big", (40 + 8 * p + 4 * i) * KB, [TILE]) for i, n in enumerate(names)]
             + [sb(f"w2_sc{p}", "big", (56 + 4 * p) * KB, [TILE]), sb(f"w2_pT{p}", "acc", 4 * KB * p, [TILE])] for p in range(2)]
    qrT = [sb("q_rope_T0", "acc", 8 * KB, [2, S]), sb("q_rope_T1", "acc", 12 * KB, [2, S])]
    st["set", 0] = st["set", 1] = []

    def groupM(g):
        p = g % 2
        QT, KT = (w[:, :].rearrange("p (u n) -> p u n", u=4) for w in work2[p][:2])
        items_q = [(i * S + m * P, qm[:, m, 192 * (4 * g + i):192 * (4 * g + i) + P]) for i in range(4) for m in range(MT)]
        items_k = [(i * S + m * P, kvm[:, m, 256 * (4 * g + i):256 * (4 * g + i) + P]) for i in range(4) for m in range(MT)]

        def extra(p):
            qv = qr[:, :, :, :].rearrange("p m h n -> p m (h n)")
            t = transposes(4 * p, [(j * S + m * P, qv[:, m, (2 * g + j) * P:(2 * g + j + 1) * P]) for j in range(2) for m in range(MT)])
            need(SCA, t)
            return [done(SCA, SCA.activation(qrT[p][:, :, :].rearrange("p j n -> p (j n)"), ps[:, 4 * p, :], ACT.Copy))]
        units = [unit(p, (i // 2, (i % 2) * S), [
            (lambda t, i=i: QT[:, i, t * P:(t + 1) * P], lambda nk, i=i: KT[:, i, 0:nk]),
            (lambda t, i=i: qrT[p][:, i // 2, t * P:(t + 1) * P], lambda nk, i=i: krT[:, i % 2, 0:nk])]) for i in range(4)]
        return p, attention(p, qk_prep(items_q, items_k, extra), units,
                            lambda i, kt: kvm[:, kt, 256 * (4 * g + i) + P:256 * (4 * g + i) + 2 * P],
                            lambda t: pj[:, t, O_QI + 512 * g:O_QI + 512 * g + 512].rearrange("p (h n) -> p h n", h=4),
                            192 ** -0.5, lambda t: chunk[:, P:S] if t == 0 else chunk[:, :], work2[p])

    def groupD(g):
        p = g % 2
        QT, KT = (w[:, :].rearrange("p (u n) -> p u n", u=4) for w in work2[p][:2])
        items = lambda base: [(i * S + m * P, pj[:, m, base + (4 * g + i) * P:base + (4 * g + i + 1) * P]) for i in range(4) for m in range(MT)]
        units = [unit(p, (i // 2, (i % 2) * S), [(lambda t, i=i: QT[:, i, t * P:(t + 1) * P], lambda nk, i=i: KT[:, i, 0:nk])]) for i in range(4)]
        return p, attention(p, qk_prep(items(O_QD), items(O_KD)), units,
                            lambda i, kt: pj[:, kt, O_VD + (4 * g + i) * P:O_VD + (4 * g + i + 1) * P],
                            lambda t: pj[:, t, O_QD + 512 * g:O_QD + 512 * g + 512].rearrange("p (h n) -> p h n", h=4),
                            128 ** -0.5, lambda t: selb[:, t, 0:(t + 1) * P], work2[p])

    run_two([groupM(g) for g in range(2)])
    barrier()
    run_two([groupD(g) for g in range(2)])
    barrier()
    mix_ready = transposed_mix(lambda k, m: pj[:, m, O_QI + k * P:O_QI + (k + 1) * P] if k < 8 else
                               pj[:, m, O_QD + (k - 8) * P:O_QD + (k - 7) * P])
    barrier()
    y_done = row_stage(a["w_out_2"][0], mixT, KD, mix_ready)
    plain_add(y_done)
    barrier()

    norm_to_h(x, cols[:, C_GCROSS:C_GCROSS + 16], None, [])
    barrier()
    qx = sb("cross_q", "big", 0, [MT, 512])
    ox = sb("cross_o", "big", 4 * KB, [MT, 512])
    oxT = sb("cross_oT", "big", 8 * KB, [4, S])
    col_slot(a["w_q_cross_2"][0], 0, KD, (0,), 512, (0, 1), A_h)
    for s_ in copy_post((0, 1), qx[:, :, :], 512):
        s_()
    barrier()
    st["set", 0] = st["set", 1] = []

    def prep_x(p, QT, KT):
        t = transposes(4 * p, [(i * S + m * P, qx[:, m, i * P:(i + 1) * P]) for i in range(4) for m in range(MT)])
        need(SCA, t)
        e = done(SCA, SCA.activation(QT[:, :].rearrange("p (b n) -> p b n", b=2), ps[:, 4 * p:4 * p + 2, :], ACT.Copy))
        yield
        return [e]
    QTx = work2[0][0][:, :].rearrange("p (u n) -> p u n", u=4)
    units = [unit(0, (i // 2, (i % 2) * S), [(lambda t, i=i: QTx[:, i, t * P:(t + 1) * P], lambda nk, i=i: kxT[:, i, 0:nk])]) for i in range(4)]
    run_two([(0, attention(0, prep_x, units, lambda i, kt: vx[:, kt, i * P:(i + 1) * P],
                           lambda t: ox[:, t, :].rearrange("p (h n) -> p h n", h=4), 128 ** -0.5, lambda t: None, work2[0], nkts=(2, 2)))])
    need(PE, tv.last())
    t = transposes(4, [(k * S + m * P, ox[:, m, k * P:(k + 1) * P]) for k in range(4) for m in range(MT)])
    need(SCA, t)
    t = done(SCA, SCA.activation(oxT[:, :, :].rearrange("p (b k) n -> p b (k n)", b=2), ps[:, 4:6, :], ACT.Copy))
    barrier()
    y_done = row_stage(a["w_o_cross_2"][0], oxT, 4, [t])
    plain_add(y_done)
    barrier()

    norm_to_h(x, cols[:, C_GMLP:C_GMLP + 16], None, [])
    barrier()

    def relu_steps(i, slot):
        b = (0, 1) if slot == 0 else (2, 3)
        tb = (4, 5) if slot == 0 else (6, 7)

        def rel_():
            need(SCA, st["full", b[0]], st.get(("hid_t", tb[0])))
            t = done(SCA, SCA.activation(r2[slot][:, :, :], ps[:, b[0]:b[1] + 1, :], ACT.Relu))
            st["relu", slot] = [t]
            bank_free(b[0], t)
            bank_free(b[1], t)

        def sq_():
            need(DVE, st["relu", slot])
            st["relu_sq", slot] = [done(DVE, DVE.tensor_tensor(r2[slot][:, :, :], r2[slot][:, :, :], r2[slot][:, :, :], ALU.mult))]
        return [rel_, sq_] + hidden_out(hid2, 2 * i + slot, tb, r2[slot], ("relu_sq", slot))

    def mlp(i):
        prev = relu_steps(i - 1, 1) if not (isinstance(i, int) and i == 0) else []
        col_slot(a["w_up_2"][0], 0, KD, bass.ds(i * 1024, 512), 512, (0, 1), A_h, prev)
        col_slot(a["w_up_2"][0], 0, KD, bass.ds(i * 1024 + 512, 512), 512, (2, 3), A_h, relu_steps(i, 0))
    repeat(DFF2 // 1024, mlp, peel=2)
    for s_ in relu_steps(DFF2 // 1024 - 1, 1):
        s_()
    barrier()
    y_done = row_stage(a["w_down_2"][0], hid2, DFF2 // P, [])
    g_row = sb("g_final_rows", "acc", 0, [D])
    gf = t_late.done(q.dma_start(g_row[:, :], a["g_final_2"].rearrange("(o d) -> o d", o=1).to_broadcast([P, D])))
    plain_add(y_done)
    for m in range(MT):
        t = row_rsqrt(x[:, m, :], m, tv.last(), junk_ap=norm_x[m][:, :])
        need(DVE, t, gf)
        t = done(DVE, DVE.scalar_tensor_tensor(x[:, m, :], x[:, m, :], sq2[:, m:m + 1], g_row[:, :], ALU.mult, ALU.mult))
        need(SP, t)
        o = t_out.done(SP.dma_start(out[0, m * P:(m + 1) * P, :], x[:, m, :]))
    need(SP, o)


_INS = ["x", "c", "positions", "w_ada", "b_ada", "g_pre_attn", "w_in", "g_out_a", "lambda_q1", "lambda_k1", "lambda_q2",
        "lambda_k2", "g_subln_b", "w_out", "g_post_attn", "g_pre_ffn", "w_gate", "w_up", "w_down", "g_post_ffn",
        "mem_2", "positions_2", "g_mix_2", "w_in_2", "g_cq_2", "g_ckv_2", "w_qb_2", "w_kvb_2", "w_out_2", "g_cross_2",
        "g_mem_2", "w_q_cross_2", "w_k_cross_2", "w_v_cross_2", "w_o_cross_2", "g_mlp_2", "w_up_2", "w_down_2",
        "g_final_2"]


def kernel(**inputs):
    import concourse.bacc as bacc
    from concourse.bass_utils import run_bass_kernel_spmd

    nc = bacc.Bacc("TRN2", target_bir_lowering=False, num_devices=1)
    arrays, aps = {}, {}
    given = {n: np.ascontiguousarray(inputs[n]) for n in _INS}
    given.update(shape_constants())
    for name, v in given.items():
        arrays[f"in_{name}"] = v
        aps[name] = nc.dram_tensor(f"in_{name}", v.shape, mybir.dt.from_np(v.dtype), kind="ExternalInput").ap()
    out = nc.dram_tensor("out_x", (1, S, D), F32, kind="ExternalOutput").ap()
    build(nc, aps, out)
    r = run_bass_kernel_spmd(nc, [arrays], core_ids=[0])
    return r.results[0]["out_x"]
```

```python
import numpy as np
import concourse.bass as bass
from concourse import mybir

F32 = mybir.dt.float32
F32R = mybir.dt.float32r
I32 = mybir.dt.int32
ALU = mybir.AluOpType
ACT = mybir.ActivationFunctionType
AX = mybir.AxisListType.X

P = 128
S = 256
MT = S // P
D = 2048
KD = D // P
DFF1, DFF2 = 5632, 8192
IN1, IN2 = 6144, 5008
BANK = 512
RAW, SPLIT = 8, 4
TILE = 1024
EPS = 1e-6
NEG = -1e30
DROPPED = -3.0e38
TAKEN = -3.3e38
MAGIC = 12582912.0
TOPK = 64
KB = 1024

C_C, C_BADA, C_GPOSTA = 0, 16, 112
C_GPRE, C_GFFN, C_GMIX, C_GCROSS, C_GMEM, C_GMLP, C_GCQ, C_GCKV, C_GPOSTF = (
    128, 144, 160, 176, 192, 208, 224, 228, 230)
NCOL = 246

R_A, R_B, R_MLA, R_DSA, R_IDX = (0, 64), (64, 32), (96, 32), (128, 16), (144, 8)
NROT, NROT1 = 152, 96
PI2 = 2 * np.pi
PI_A = 6.28125
PI_B = float(np.float32(PI2 - PI_A))
PI_C = float(np.float32(PI2 - PI_A - PI_B))


def shape_constants():
    t = np.arange(P)[:, None] + P
    k = np.arange(S)[None, :]
    d = t - k
    count = ((d >= 0) & (d <= 128)).astype(np.float32)
    count += (d >= 0) & (d % 4 == 0)
    count += (d >= 0) & (d % 16 == 0)
    dilated = np.where(count > 0, 0, NEG).astype(np.float32)
    causal = np.where(d >= 0, 0, NEG).astype(np.float32)
    chunk = np.where(k // 64 <= t // 64, 0, NEG).astype(np.float32)
    f = lambda theta, half: (np.float32(theta) ** (-np.arange(half, dtype=np.float32) / np.float32(half))).astype(np.float32)
    inv = np.concatenate([f(10000.0, 64), f(10000.0, 32), f(500000.0, 32), f(500000.0, 16), f(500000.0, 8)])
    return {
        "k_ident": np.eye(P, dtype=np.float32), "k_count": count, "k_dilated": dilated,
        "k_causal": causal, "k_chunk": chunk, "k_inv": inv[None, :].astype(np.float32),
    }


class Tok:

    def __init__(self, track, v, loop, epoch):
        self.track, self.v, self.loop, self.epoch = track, v, loop, epoch


class Loop:

    def __init__(self, reg, start, n, per):
        self.reg, self.start, self.n, self.per, self.live = reg, start, n, per, True


class Side:

    def __init__(self, *parts):
        self.parts = list(parts)

    def step(self):
        while self.parts:
            try:
                next(self.parts[0])
                return
            except StopIteration:
                self.parts.pop(0)

    def finish(self):
        while self.parts:
            self.step()


class Clock:

    def __init__(self):
        self.loop, self.epoch, self.tracks = None, 0, []


class Track:

    def __init__(self, nc, clock, name, step=1):
        self.sem, self.clock, self.step, self.n, self.name = nc.alloc_semaphore(name), clock, step, 0, name
        clock.tracks.append(self)

    def done(self, ins):
        ins.then_inc(self.sem, self.step)
        self.n += self.step
        return Tok(self, self.n, self.clock.loop, self.clock.epoch)

    def last(self):
        return Tok(self, self.n, self.clock.loop, self.clock.epoch)


def build(nc, a, out):
    clock = Clock()
    PE, DVE, SCA, POOL, SP = nc.tensor, nc.vector, nc.scalar, nc.gpsimd, nc.sync
    tp, tv, ta, tg = (Track(nc, clock, n) for n in ("s_tensor", "s_vector", "s_scalar", "s_pool"))
    track_of = {id(PE): tp, id(DVE): tv, id(SCA): ta, id(POOL): tg}
    t_raw = [Track(nc, clock, f"s_raw{r}", 16) for r in range(RAW)]
    t_par = Track(nc, clock, "s_parameters", 16)
    t_x = Track(nc, clock, "s_x", 16)
    t_mem = Track(nc, clock, "s_mem", 16)
    t_late = Track(nc, clock, "s_late", 16)
    t_out = Track(nc, clock, "s_out", 16)
    st = {}
    waited = {}

    def need(eng, *toks):
        best = {}
        for tok in toks:
            if tok is None:
                continue
            if isinstance(tok, (list, tuple)):
                for x in tok:
                    if x is not None:
                        best.setdefault(id(x.track), []).append(x)
                continue
            best.setdefault(id(tok.track), []).append(tok)
        for group in best.values():
            fixed = [t for t in group if t.loop is None or not t.loop.live]
            moving = [t for t in group if t.loop is not None and t.loop.live]
            if moving:
                v = max(t.v for t in moving)
                lp, tr = moving[0].loop, moving[0].track
                DVE_ = lp.reg * lp.per[tr] + (v - lp.start * lp.per[tr])
                eng.wait_ge(tr.sem, DVE_)
            if fixed:
                tr = fixed[0].track
                v = max(t.v + ((t.loop.n - 1 - t.loop.start) * t.loop.per[tr] if t.loop else 0) for t in fixed)
                if waited.get((id(eng), id(tr)), 0) >= v:
                    continue
                if clock.loop is None:
                    waited[(id(eng), id(tr))] = v
                eng.wait_ge(tr.sem, v)

    def done(eng, ins):
        return track_of[id(eng)].done(ins)

    def repeat(n, body, peel=1, tail=0):
        peel, ends = min(peel, n), n
        n = max(peel, n - tail)
        for i in range(peel):
            clock.epoch += 1
            before = {t: t.n for t in clock.tracks}
            body(i)
        if n == peel:
            for i in range(n, ends):
                body(i)
            return
        per = {t: t.n - before[t] for t in clock.tracks}
        mine, epoch = clock.epoch, clock.epoch
        clock.epoch += 1
        base = {t: t.n for t in clock.tracks}
        with nc.Fori(peel, n) as reg:
            lp = Loop(reg, peel, n, per)
            clock.loop = lp
            old = dict(st)
            for k, tok in old.items():
                st[k] = [Tok(x.track, x.v, lp, -1) if x.epoch == mine else x for x in tok]
            body(reg)
            for t in clock.tracks:
                assert t.n - base[t] == per[t], (t.name, t.n - base[t], per[t])
            for k, tok in old.items():
                for x, y in zip(tok, st[k]):
                    if x.epoch == mine:
                        assert y.epoch == clock.epoch and y.v == x.v + per[x.track], (k, x.v, y.v, per[x.track])
            lp.live = False
            clock.loop = None
        for t in clock.tracks:
            t.n = base[t] + per[t] * (n - peel)
        clock.epoch += 1
        waited.clear()
        for i in range(n, ends):
            body(i)

    base0 = -(-nc.sbuf_base // 128) * 128
    plan = {}
    at_ = base0
    for name, size in (("raw", 32 * KB), ("whi", 16 * KB), ("wlo", 16 * KB), ("x", 16 * KB), ("h", 32 * KB),
                       ("big", 64 * KB), ("acc", 16 * KB), ("mem", 8 * KB), ("small", 7 * KB + 256)):
        plan[name] = (at_, size)
        at_ += size

    def sb(name, region, off, shape, dt=F32):
        start, size = plan[region]
        n = 4 * int(np.prod(shape))
        assert off + n <= size, (name, off, n, size)
        return nc.alloc_sbuf_tensor_at(name, [P] + list(shape), dt, offset=start + off)

    raw = [sb(f"raw{r}", "raw", 4 * KB * r, [TILE]) for r in range(RAW)]
    whi = [sb(f"whi{r}", "whi", 4 * KB * r, [TILE], F32R) for r in range(SPLIT)]
    wlo = [sb(f"wlo{r}", "wlo", 4 * KB * r, [TILE], F32R) for r in range(SPLIT)]
    x = sb("x_res", "x", 0, [MT, D])
    h_hi = sb("h_hi", "h", 0, [KD, S], F32R)
    h_lo = sb("h_lo", "h", 16 * KB, [KD, S], F32R)
    acc = [sb(f"ada_acc{i}", "acc", 8 * KB * i, [D]) for i in range(2)]
    kxT = sb("cross_kT", "mem", 0, [4, S])
    vx = sb("cross_v", "mem", 4 * KB, [MT, 512])

    off = [0]

    def small(name, shape, dt=F32):
        t = sb(name, "small", off[0], shape, dt)
        off[0] += -(-4 * int(np.prod(shape)) // 32) * 32
        return t

    ident = small("ident", [P])
    causal = small("causal", [S])
    chunk = small("chunk", [S])
    cols = small("param_cols", [NCOL])
    mod = small("mod_cols", [96])
    gsc = small("gain_cols", [KD])
    trig = small("trig", [2, MT, NROT])
    one = small("one", [1])
    mhalf = small("minus_half", [16])
    sil = small("silu_c", [KD])
    sq = small("sum_of_squares", [16])
    sq2 = small("sum_of_squares2", [16])
    nm = [small(f"neg_max{i}", [8]) for i in range(2)]
    den = [small(f"denominator{i}", [8]) for i in range(2)]
    rden = [small(f"reciprocal{i}", [8]) for i in range(2)]
    lam = small("lam", [4])
    posf = small("pos_f", [2 * MT])
    posi = small("pos_i", [2 * MT], I32)
    wi = small("w_idx", [MT, 16])
    m8 = small("max8", [8])

    proj = sb("proj", "big", 0, [MT, IN1])
    count = sb("count", "h", 30 * KB, [S])
    dilated = sb("dilated", "h", 31 * KB, [S])
    norm_x = [sb(f"norm_x{m}", "big", 8 * KB * m, [D]) for m in range(MT)]
    norm_f = sb("norm_f", "big", 16 * KB, [8, S])
    junk = sb("junk", "h", 24 * KB, [D])
    x_T = sb("x_T", "h", 16 * KB, [KD, S])
    rope_a = [sb("rope_t", "h", 0, [D])] + [sb(f"rope_u{i}", "h", 8 * KB + 4 * KB * i, [TILE]) for i in range(2)]
    rope_b = [sb("rope_bt", "acc", 0, [D])] + [sb(f"rope_bu{i}", "big", 48 * KB + 4 * KB * i, [TILE]) for i in range(2)]
    gate_row = sb("gate_row", "big", 50 * KB, [D])
    diag = sb("diag", "h", 0, [KD, P])
    ones_sq = sb("ones_sq", "h", 8 * KB, [P])
    hid1 = sb("hidden1_T", "big", 0, [DFF1 // P, S])
    hid2 = sb("hidden2_T", "big", 0, [DFF2 // P, S])
    sg1 = sb("silu_gate", "big", 58 * KB, [MT, BANK])
    r2 = [sb(f"relu{i}", "acc", 8 * KB * i, [MT, BANK]) for i in range(2)]
    hsq = [sb("head_sq0", "h", 16 * KB, [TILE]), sb("head_sq1", "h", 20 * KB, [TILE]), sb("head_sq2", "h", 24 * KB, [TILE])]
    mixT = sb("mix_T", "h", 0, [KD, S])
    s_hi = [sb(f"src_hi{i}", "h", 16 * KB + KB * i, [S], F32R) for i in range(4)]
    s_lo = [sb(f"src_lo{i}", "h", 20 * KB + KB * i, [S], F32R) for i in range(4)]
    vec1 = sb("vec_rows1", "h", 0 * KB, [P])
    vec2 = sb("vec_rows2", "h", 1 * KB, [P])
    inv = sb("inv_freq", "h", 2 * KB, [NROT])
    ang = sb("angles", "h", 3 * KB, [MT, NROT])
    rnd = sb("turns", "h", 5 * KB, [MT, NROT])
    angr = sb("reduced", "h", 7 * KB, [2, MT, NROT])
    lamv = sb("lambda_rows", "h", 10 * KB, [4, 64])
    sil_t = sb("silu_tmp", "h", 11 * KB, [KD])
    post_tmp = [sb(f"post_tmp{m}", "big", (24 + 8 * m) * KB, [D]) for m in range(MT)]
    junks = [junk, sb("junk1", "h", 0, [D])]

    ps = nc.alloc_psum_tensor("ps", [P, 8, BANK], F32)

    def bank_free(b, *toks):
        st["bank", b] = list(toks)

    def r32(ap):
        return ap.bitcast(F32)

    count_t = [0, 0]

    def fetch(src, view):
        r = count_t[0] % RAW
        count_t[0] += 1
        need(SP, st.get(("raw", r)))
        dst = raw[r][:, :] if view is None else raw[r][:, 0:view[0] * view[1]].rearrange("p (k n) -> p k n", k=view[0])
        st["landed", r] = [t_raw[r].done(SP.dma_start(dst, src))]
        return r

    def split(r, n=TILE):
        u = count_t[1] % SPLIT
        count_t[1] += 1
        need(SCA, st["landed", r], st.get(("split", u)))
        hi = done(SCA, SCA.activation(whi[u][:, 0:n], raw[r][:, 0:n], ACT.Copy))
        need(DVE, hi, st["landed", r])
        lo = done(DVE, DVE.tensor_tensor(wlo[u][:, 0:n], raw[r][:, 0:n], r32(whi[u][:, 0:n]), ALU.subtract))
        st["raw", r] = [lo]
        st["halves", u] = [hi, lo]
        return u

    def products(dst, lhs, rhs, first, last):
        (ah, al), (bh, bl) = lhs, rhs
        PE.matmul(dst, ah, bh, start=first, stop=False)
        PE.matmul(dst, al, bh, start=False, stop=False)
        return PE.matmul(dst, ah, bl, start=False, stop=last)

    def col_tile(w, row, kt_per, c0, width):
        rows = w[row:row + kt_per * P, c0 if not isinstance(c0, tuple) else slice(c0[0], c0[0] + width)]
        return split(fetch(rows.rearrange("(k p) n -> p k n", p=P), (kt_per, width)), kt_per * width)

    ahead = []
    h_wait = {}
    h_make = []

    def look_ahead(w, c0, n=3):
        for j in range(n):
            ahead.append(col_tile(w, 2 * j * P, 2, c0, BANK))

    def col_slot(w, row0, nk, c0, width, banks, A, pend=(), lag=3, extra=None, side=None):
        pend = list(pend)
        kt_per = 2 if nk > 1 else 1
        need(PE, *[st.get(("bank", b)) for b in banks])
        ah, al = A
        for j in range(nk // kt_per):
            if h_make and j % 2 == 0:
                h_make.pop(0)()
            u = ahead.pop(0) if ahead else col_tile(w, row0 + j * kt_per * P, kt_per, c0, width)
            need(PE, st["halves", u])
            for kk in range(kt_per):
                k = j * kt_per + kk
                need(PE, h_wait.pop(k, None))
                for m in range(MT):
                    lhs = (ah[:, k, m * P:(m + 1) * P], al[:, k, m * P:(m + 1) * P])
                    rhs = (whi[u][:, kk * width:(kk + 1) * width], wlo[u][:, kk * width:(kk + 1) * width])
                    ins = products(ps[:, banks[m], 0:width], lhs, rhs, k == 0, k == nk - 1)
            st["split", u] = [done(PE, ins)]
            if extra:
                extra(j)
            if j >= lag and pend:
                pend.pop(0)()
            if side:
                side.step()
        st["full", banks[0]] = st["split", u]
        for step in pend:
            step()

    def wait_steps(n):
        for _ in range(n):
            yield

    def ada_half(part, kt, half, first):
        r = fetch(a["w_ada"][0][bass.ds(kt * P, P), part * D + half * TILE:part * D + (half + 1) * TILE], None)
        dst = acc[part % 2][:, half * TILE:(half + 1) * TILE]
        c = sil[:, kt:kt + 1] if isinstance(kt, int) else sil[:, bass.ds(kt, 1)]
        need(DVE, st["landed", r], st["silu"])
        if first:
            need(DVE, st.get(("acc", part % 2)))
            t = done(DVE, DVE.tensor_scalar(dst, raw[r][:, :], c, None, ALU.mult))
        else:
            need(DVE, st["accumulated", half])
            t = done(DVE, DVE.scalar_tensor_tensor(dst, raw[r][:, :], c, dst, ALU.mult, ALU.add))
        st["accumulated", half] = [t]
        st["raw", r] = [t]

    def ada_finish(part, bank, behind=0):
        need(PE, st["accumulated", 0], st["accumulated", 1], st.get(("bank", bank)), st["one"])
        for k in range(KD):
            ins = PE.matmul(ps[:, bank, k:k + 1], acc[part % 2][:, k * P:(k + 1) * P], one[:, :], start=True, stop=True)
        t = done(PE, ins)
        st["acc", part % 2] = [t]
        yield from wait_steps(behind)
        need(DVE, t, st["cols"])
        c = done(DVE, DVE.tensor_tensor(mod[:, part * 16:part * 16 + 16], ps[:, bank, 0:KD],
                                        cols[:, C_BADA + part * 16:C_BADA + part * 16 + 16], ALU.add))
        bank_free(bank, c)
        st["mod", part] = [c]

    def row_ahead(w, n=3):
        for j in range(n):
            ahead.append(split(fetch(w[j // 2 * P:(j // 2 + 1) * P, j % 2 * TILE:(j % 2 + 1) * TILE], None)))

    def row_stage(w, srcT, nk, ready, ada=None):
        per = 4
        need(SCA, ready)
        need(DVE, ready)
        need(PE, *[st.get(("bank", b)) for b in range(8)])
        y = {}

        def body(i):
            end = isinstance(i, int) and i == nk // per - 1
            held = []
            for q in range(per):
                kt = i * per + q
                src = srcT[:, kt, :] if isinstance(kt, int) else srcT[:, bass.ds(kt, 1), :].rearrange("p o n -> p (o n)")
                need(SCA, st.get(("src", q)))
                hi = done(SCA, SCA.activation(s_hi[q][:, :], src, ACT.Copy))
                need(DVE, hi)
                lo = done(DVE, DVE.tensor_tensor(s_lo[q][:, :], src, r32(s_hi[q][:, :]), ALU.subtract))
                for half in range(2):
                    u = ahead.pop(0) if ahead else split(fetch(w[bass.ds(kt * P, P), half * TILE:(half + 1) * TILE], None))
                    need(PE, st["halves", u], hi, lo)
                    first = isinstance(i, int) and i == 0 and q == 0
                    last = end and q == per - 1

                    def one(ms, q=q, u=u, half=half, first=first, last=last):
                        for m in ms:
                            for n in range(2):
                                lhs = (s_hi[q][:, m * P:(m + 1) * P], s_lo[q][:, m * P:(m + 1) * P])
                                rhs = (whi[u][:, n * BANK:(n + 1) * BANK], wlo[u][:, n * BANK:(n + 1) * BANK])
                                ins = products(ps[:, 4 * m + 2 * half + n, :], lhs, rhs, first, last)
                        return done(PE, ins)
                    if end and q >= per - 2:
                        y[0] = one((0,))
                        held.append((u, q, one))
                    else:
                        st["split", u] = [one(range(MT))]
                    if ada is not None:
                        ada_half(ada, kt, half, isinstance(kt, int) and kt == 0)
                if not held:
                    st["src", q] = st["split", u]
            for u, q, one in held:
                y[1] = one((1,))
                st["split", u] = st["src", q] = [y[1]]

        repeat(nk // per, body, peel=2 if ahead else 1, tail=1)
        return y

    def rsqrt_cols(dst, src, n, scale):
        t = done(POOL, POOL.tensor_scalar(dst, src, scale, EPS, ALU.mult, ALU.add))
        need(POOL, t)
        return done(POOL, POOL.tensor_tensor(dst, dst, mhalf[:, 0:n], ALU.pow))

    def row_rsqrt(src, slot, *ready, junk_ap=None):
        n = src.shape[-1] if len(src.shape) == 2 else int(np.prod(src.shape[1:]))
        need(SCA, ta.last(), *ready)
        t = done(SCA, SCA.activation(junk_ap, src, ACT.Square, accum_out=sq[:, slot:slot + 1]))
        need(POOL, t, st["mhalf"])
        return rsqrt_cols(sq2[:, slot:slot + 1], sq[:, slot:slot + 1], 1, 1.0 / n)

    def barrier():
        toks = [t.last() for t in (tp, tv, ta, tg)]
        for eng in (PE, DVE, SCA, POOL):
            need(eng, toks)
        for b in range(8):
            bank_free(b)
        return toks

    def norm_rows(src, xn, slot, ready):
        for m in range(MT):
            st["rs", m] = [row_rsqrt(src[:, m, :], slot + m, *ready[m], junk_ap=xn[m])]
            yield
        for m in range(MT):
            need(DVE, st["rs", m])
            st["nx", m] = [done(DVE, DVE.tensor_scalar(xn[m], src[:, m, :], sq2[:, slot + m:slot + m + 1], None, ALU.mult))]
            yield

    def norm_to_h(xn, gain, dst):
        hi_t, lo_t = dst
        for n in range(0, KD, 4):
            bs = [n // 2, n // 2 + 1]
            need(PE, st["nx", 0], st["nx", 1], st["ident"], *[st.get(("bank", b)) for b in bs])
            st["nt", n] = [transposes(bs[0], [(k * S + m * P, xn[m][:, (n + k) * P:(n + k + 1) * P]) for k in range(4) for m in range(MT)])]
        yield
        for b in range(8):
            ks = [(2 * b + k, ps[:, b, k * S:(k + 1) * S]) for k in range(2)]
            need(SCA, st["nt", 4 * (b // 2)])
            for kt, s_ in ks:
                hi = done(SCA, SCA.activation(hi_t[:, kt, :], s_, ACT.Copy, scale=gain[:, kt:kt + 1]))
            need(DVE, hi, st["nt", 4 * (b // 2)])
            for kt, s_ in ks:
                lo = done(DVE, DVE.scalar_tensor_tensor(lo_t[:, kt, :], s_, gain[:, kt:kt + 1], r32(hi_t[:, kt, :]), ALU.mult, ALU.subtract))
            for kt, s_ in ks:
                h_wait[kt] = [hi, lo]
            bank_free(b, hi, lo)
            yield

    def norm(src, gain, shift, ready, next_w, c0=(0,), keep=(0, 1)):
        xn = [norm_x[m][:, :] for m in range(MT)]
        for m in range(MT):
            st["rs", m] = [row_rsqrt(src[:, m, :], m, *ready[m], junk_ap=xn[m])]
        for m in range(MT):
            need(DVE, st["rs", m])
            need(SCA, st["rs", m])
            st["nx", m] = [done(DVE, DVE.tensor_scalar(xn[m][:, 0:TILE], src[:, m, 0:TILE], sq2[:, m:m + 1], None, ALU.mult)),
                           done(SCA, SCA.activation(xn[m][:, TILE:], src[:, m, TILE:], ACT.Copy, scale=sq2[:, m:m + 1]))]
        look_ahead(next_w, c0)
        free = [b for b in range(8) if b not in keep]
        pairs = [(free[0], free[1]), (free[2], free[3]), (free[4], free[5]), (free[0], free[1])]

        def tr(g, m):
            need(PE, st["nx", m], *[st.get(("bank", b)) for b in pairs[g]])
            for k in range(4):
                ins = PE.transpose(ps[:, pairs[g][k // 2], (k % 2) * S + m * P:(k % 2) * S + (m + 1) * P],
                                   xn[m][:, (4 * g + k) * P:(4 * g + k + 1) * P], ident[:, :])
            st["nt", g] = [done(PE, ins)]

        for m in range(MT):
            for g in range(3):
                tr(g, m)
        for g in range(4):
            h_make.append(lambda g=g: to_halves(g, pairs[g], gain, shift))
        h_make.pop(0)()
        tr(3, 0)
        tr(3, 1)

    def to_halves(g, pair, gain, shift):
        for n, b in enumerate(pair or (0, 1)):
            ks = [(4 * g + 2 * n + k, ps[:, b, k * S:(k + 1) * S] if pair else x_T[:, 4 * g + 2 * n + k, :]) for k in range(2)]
            if shift is None:
                need(SCA, st["nt", g])
                for kt, s_ in ks:
                    hi = done(SCA, SCA.activation(h_hi[:, kt, :], s_, ACT.Copy, scale=gain[:, kt:kt + 1]))
                need(DVE, hi, st["nt", g])
                for kt, s_ in ks:
                    lo = done(DVE, DVE.scalar_tensor_tensor(h_lo[:, kt, :], s_, gain[:, kt:kt + 1], r32(h_hi[:, kt, :]), ALU.mult, ALU.subtract))
                for kt, s_ in ks:
                    h_wait[kt] = [hi, lo]
                bank_free(b, hi, lo)
            else:
                need(SCA, st["nt", g])
                for kt, s_ in ks:
                    hi = done(SCA, SCA.activation(h_hi[:, kt, :], s_, ACT.Identity, scale=gain[:, kt:kt + 1], bias=shift[:, kt:kt + 1]))
                need(DVE, hi if pair else None, st["nt", g], st.get("nlo"))
                for kt, s_ in ks:
                    f = done(DVE, DVE.tensor_scalar(norm_f[:, kt % 8, :], s_, gain[:, kt:kt + 1], shift[:, kt:kt + 1], ALU.mult, ALU.add))
                if pair:
                    bank_free(b, f)
                need(DVE, hi, f)
                kt = ks[0][0]
                lo = done(DVE, DVE.tensor_tensor(h_lo[:, kt:kt + 2, :], norm_f[:, kt % 8:kt % 8 + 2, :], r32(h_hi[:, kt:kt + 2, :]), ALU.subtract))
                for kt, s_ in ks:
                    h_wait[kt] = [hi, lo]

    def run(gen):
        for _ in gen:
            pass

    def copy_post(banks, dst, width):
        def step():
            need(SCA, st["full", banks[0]])
            t = done(SCA, SCA.activation(dst, ps[:, banks[0]:banks[1] + 1, 0:width], ACT.Copy))
            for b in banks:
                bank_free(b, t)
        return [step]

    def rope(src, dst, heads, half, rot, m, tmp, *ready):
        need(DVE, *ready)
        r0 = rot[0]
        cos = trig[:, 0, m, r0:r0 + half]
        sin = trig[:, 1, m, r0:r0 + half]
        s4 = src.rearrange("p h (a b) -> p h a b", a=2)
        d4 = dst.rearrange("p h (a b) -> p h a b", a=2)
        t4 = tmp[0][:, 0:heads * 2 * half].rearrange("p (h a b) -> p h a b", a=2, b=half)
        u = [tmp[1 + i][:, 0:heads * half].rearrange("p (h b) -> p h b", b=half) for i in range(2)]
        need(DVE, st.get("rope"))
        DVE.tensor_tensor(t4, s4, cos.unsqueeze(1).unsqueeze(1).to_broadcast([P, heads, 2, half]), ALU.mult)
        if heads * half > 512:
            yield
        DVE.tensor_tensor(u[0], s4[:, :, 1, :], sin.unsqueeze(1).to_broadcast([P, heads, half]), ALU.mult)
        t = done(DVE, DVE.tensor_tensor(u[1], s4[:, :, 0, :], sin.unsqueeze(1).to_broadcast([P, heads, half]), ALU.mult))
        yield
        need(DVE, t)
        DVE.tensor_tensor(d4[:, :, 0, :], t4[:, :, 0, :], u[0], ALU.subtract)
        t = done(DVE, DVE.tensor_tensor(d4[:, :, 1, :], t4[:, :, 1, :], u[1], ALU.add))
        st["rope"] = [t]
        yield

    def transposes(banks, items):
        for col, src in items:
            ins = PE.transpose(ps[:, banks + col // BANK, col % BANK:col % BANK + P], src, ident[:, :])
        return done(PE, ins)

    def attention(p, prep, units, vs, outs, scale, masks, buf, cnt=None, diff=False, nkts=(1, 2)):
        QT, KT, sc0, sc1 = buf
        b0 = 4 * p
        tok = yield from prep(p, QT, KT)
        n_out = 2 if diff else 4
        step = 2 if diff else 1
        whole = nkts[0] == 2
        need(PE, tok)
        ts = range(MT)
        pair = [ps[:, b0:b0 + 2, :], ps[:, b0 + 2:b0 + 4, :]]
        sc, s_done, e, rc = {}, {}, {}, {}
        for t in ts:
            nk = nkts[t] * P
            for i in range(4):
                ins = units[i](t, pair[t][:, i // 2, (i % 2) * nk:(i % 2 + 1) * nk], nk)
            s_done[t] = done(PE, ins)
        yield
        yield
        for t in ts:
            nk = nkts[t] * P
            need(DVE, s_done[t])
            s_ps = pair[t][:, :, 0:2 * nk].rearrange("p b (u n) -> p b u n", u=2)
            flat = (sc0, sc1)[t][:, 0:4 * nk]
            sc[t] = flat.rearrange("p (u n) -> p u n", u=4)
            sc4 = flat.rearrange("p (b u n) -> p b u n", b=2, u=2)
            mk = masks(t)
            if mk is None:
                mt = done(DVE, DVE.tensor_copy(sc4, s_ps))
            else:
                mt = done(DVE, DVE.tensor_tensor(sc4, s_ps, mk.unsqueeze(1).unsqueeze(1).to_broadcast([P, 2, 2, nk]), ALU.add))
            need(DVE, mt)
            mx = done(DVE, DVE.tensor_reduce(nm[p][:, 4 * t:4 * t + 4], sc[t], AX, ALU.max))
            need(DVE, mx)
            ng = done(DVE, DVE.tensor_scalar(nm[p][:, 4 * t:4 * t + 4], nm[p][:, 4 * t:4 * t + 4], -scale, None, ALU.mult))
            need(SCA, ng)
            for i in range(4):
                e[t] = done(SCA, SCA.activation(sc[t][:, i, :], sc[t][:, i, :], ACT.Exp, bias=nm[p][:, 4 * t + i:4 * t + i + 1],
                                                scale=scale, accum_out=den[p][:, 4 * t + i:4 * t + i + 1]))
            yield
        for t in ts:
            nk = nkts[t] * P
            d, r = den[p][:, 4 * t:4 * t + 4], rden[p][:, 4 * t:4 * t + 4]
            need(DVE, e[t])
            if cnt is not None:
                w = done(DVE, DVE.tensor_tensor(sc[t], sc[t], cnt(t).unsqueeze(1).to_broadcast([P, 4, nk]), ALU.mult))
                need(DVE, w)
                e[t] = done(DVE, DVE.tensor_reduce(d, sc[t], AX, ALU.add))
                need(DVE, e[t])
            rc[t] = done(DVE, DVE.reciprocal(r, d))
            if diff:
                need(DVE, rc[t])
                rv = r.rearrange("p (h m) -> p h m", m=2)
                rl = done(DVE, DVE.tensor_scalar(rv[:, :, 1], rv[:, :, 1], lam[:, 3:4], None, ALU.mult))
                need(DVE, rl)
                w = done(DVE, DVE.tensor_tensor(sc[t], sc[t], r.unsqueeze(2).to_broadcast([P, 4, nk]), ALU.mult))
                need(DVE, w)
                s4 = sc[t].rearrange("p (h m) n -> p h m n", m=2)
                e[t] = done(DVE, DVE.tensor_tensor(s4[:, :, 0, :], s4[:, :, 0, :], s4[:, :, 1, :], ALU.add))
        yield
        pv, pt, pe_ = {}, {}, {}
        for t in ts:
            need(PE, e[t])
            for kt in range(nkts[t]):
                for i in range(n_out):
                    ins = PE.transpose(pair[t][:, kt, i * P:(i + 1) * P], sc[t][:, i * step, kt * P:(kt + 1) * P], ident[:, :])
            pt[t] = done(PE, ins)
        yield
        yield
        for t in ts:
            need(SCA, pt[t])
            pv[t] = (KT, QT)[t][:, :].rearrange("p (k n) -> p k n", k=2)[:, 0:nkts[t], 0:n_out * P]
            pe_[t] = done(SCA, SCA.activation(pv[t], pair[t][:, 0:nkts[t], 0:n_out * P], ACT.Copy))
        o = {}
        for t in ts:
            need(PE, pe_[t])
            for i in range(n_out):
                for kt in range(nkts[t]):
                    ins = PE.matmul(pair[t][:, 0, i * P:(i + 1) * P], pv[t][:, kt, i * P:(i + 1) * P], vs(i, kt),
                                    start=kt == 0, stop=kt == nkts[t] - 1)
            o[t] = done(PE, ins)
        yield
        yield
        for t in ts:
            o_ps = pair[t][:, 0, 0:n_out * P].rearrange("p (h n) -> p h n", h=n_out)
            if diff:
                need(SCA, o[t])
                f = done(SCA, SCA.activation(outs(t), o_ps, ACT.Copy))
            else:
                need(DVE, o[t], rc[t])
                f = done(DVE, DVE.tensor_tensor(outs(t), o_ps, rden[p][:, 4 * t:4 * t + 4].unsqueeze(2).to_broadcast([P, 4, P]), ALU.mult))
        st["set", p] = [f]

    def run_two(gens):
        live = {}
        gens = list(gens)
        turn = 0
        while gens or live:
            for p in range(2):
                if p not in live and gens and gens[0][0] == p:
                    live[p] = gens.pop(0)[1]
            if turn in live:
                try:
                    next(live[turn])
                except StopIteration:
                    del live[turn]
            turn ^= 1

    def qk_prep(q_items, k_items, extra=None):
        def prep(p, QT, KT):
            need(PE, st.get(("set", p)))
            tq = transposes(4 * p, q_items)
            tk = transposes(4 * p + 2, k_items)
            yield
            yield
            need(SCA, tq)
            eq = done(SCA, SCA.activation(QT[:, :].rearrange("p (b n) -> p b n", b=2), ps[:, 4 * p:4 * p + 2, :], ACT.Copy))
            need(SCA, tk)
            ek = done(SCA, SCA.activation(KT[:, :].rearrange("p (b n) -> p b n", b=2), ps[:, 4 * p + 2:4 * p + 4, :], ACT.Copy))
            toks = [eq, ek]
            if extra:
                need(PE, eq)
                toks += extra(p)
            return toks
        return prep

    def head_norm(view, gain_row, factor, slot, tmp):
        c = slice(8 * slot, 8 * slot + 8)
        need(SCA, tv.last(), ta.last())
        sqv = tmp.rearrange("p (h n) -> p h n", h=8)
        t = done(SCA, SCA.activation(sqv, view, ACT.Square))
        yield
        need(DVE, t)
        t = done(DVE, DVE.tensor_reduce(sq[:, c], sqv, AX, ALU.add))
        need(POOL, t)
        g = rsqrt_cols(sq2[:, c], sq[:, c], 8, 1.0 / P)
        yield
        yield
        need(DVE, g)
        t = done(DVE, DVE.tensor_tensor(view, view, sq2[:, c].unsqueeze(2).to_broadcast([P, 8, P]), ALU.mult))
        yield
        need(DVE, t)
        t = done(DVE, DVE.scalar_tensor_tensor(view, view, factor, gain_row.unsqueeze(1).to_broadcast([P, 8, P]), ALU.mult, ALU.mult))
        yield

    def together(*gens):
        gens = list(gens)
        while gens:
            for g_ in list(gens):
                try:
                    next(g_)
                except StopIteration:
                    gens.remove(g_)

    def gate_bcast(part, gcol):
        need(DVE, st["mod", part], st["cols"])
        g = done(DVE, DVE.tensor_tensor(gsc[:, :], mod[:, part * 16:part * 16 + 16], cols[:, gcol:gcol + 16], ALU.mult))
        need(DVE, g, st["ident"])
        t = done(DVE, DVE.tensor_tensor(diag[:, :, :], ident[:, :].unsqueeze(1).to_broadcast([P, KD, P]),
                                        gsc[:, :].unsqueeze(2).to_broadcast([P, KD, P]), ALU.mult))
        t = done(DVE, DVE.memset(ones_sq[:, :], 1.0))
        need(PE, t)
        for n in range(4):
            ins = PE.matmul(ps[:, n, :], ones_sq[:, :], diag[:, 4 * n:4 * n + 4, :].rearrange("p k n -> p (k n)"), start=True, stop=True)
        t = done(PE, ins)
        need(SCA, t)
        t = done(SCA, SCA.activation(gate_row[:, :].rearrange("p (b n) -> p b n", b=4), ps[:, 0:4, :], ACT.Copy))
        for b in range(4):
            bank_free(b, t)
        return t

    def transposed_mix(srcs, *ready):
        need(PE, *ready)
        last = []
        for g in range(4):
            for k in range(4 * g, 4 * g + 4):
                for m in range(MT):
                    ins = PE.transpose(ps[:, k // 2, (k % 2) * S + m * P:(k % 2) * S + (m + 1) * P], srcs(k, m), ident[:, :])
            t = done(PE, ins)
            eng = (SCA, DVE)[g % 2]
            need(eng, t)
            dst = mixT[:, 4 * g:4 * g + 4, :].rearrange("p (b k) n -> p b (k n)", b=2)
            s_ = ps[:, 2 * g:2 * g + 2, :]
            c = done(eng, eng.activation(dst, s_, ACT.Copy) if eng is SCA else eng.tensor_copy(dst, s_))
            last.append(c)
        for b in range(8):
            bank_free(b, *last)
        return last

    gout = [sb("g_out_rows", "big", 62 * KB, [P]), sb("g_sub_rows", "big", 62 * KB + 512, [P])]
    q = SCA
    par = []

    def pload(dst, src, eng=None):
        par.append(t_par.done((eng or q).dma_start(dst, src)))

    z = done(POOL, POOL.memset(vec2[:, :], 0.0))
    need(q, z)
    pload(vec1[0:16, :], a["c"].rearrange("o (k n) -> (o k) n", n=P))
    pload(vec1[16:112, :], a["b_ada"].rearrange("o (k n) -> (o k) n", n=P))
    pload(vec1[112:128, :], a["g_post_attn"].rearrange("o (k n) -> (o k) n", n=P))
    row = 0
    for name in ("g_pre_attn", "g_pre_ffn", "g_mix_2", "g_cross_2", "g_mem_2", "g_mlp_2", "g_cq_2", "g_ckv_2", "g_post_ffn"):
        n = a[name].shape[1] // P
        pload(vec2[row:row + n, :], a[name].rearrange("o (k n) -> (o k) n", n=P))
        row += n
    assert 128 + row == NCOL
    pload(ident[:, :], a["k_ident"])
    pload(causal[:, :], a["k_causal"])
    pload(chunk[:, :], a["k_chunk"])
    pload(inv[:, :], a["k_inv"].to_broadcast([P, NROT]))
    for i, n in enumerate(("positions", "positions_2")):
        for m in range(MT):
            pload(posi[:, 2 * i + m:2 * i + m + 1], a[n].rearrange("o (m p) -> m p o", p=P)[m])
    for i, n in enumerate(("lambda_q1", "lambda_k1", "lambda_q2", "lambda_k2")):
        pload(lamv[:, i, :], a[n].to_broadcast([P, 64]))
    memt = sb("mem_rows", "h", 16 * KB, [MT, D])
    m_in = t_mem.done(q.dma_start(memt[:, :, :], a["mem_2"][0].rearrange("(m p) d -> p m d", p=P)))
    x_in = t_x.done(q.dma_start(x[:, :, :], a["x"][0].rearrange("(m p) d -> p m d", p=P)))
    par_tok = [par[-1]]

    ONES = done(DVE, DVE.memset(one[:, :], 1.0))
    MH = done(POOL, POOL.memset(mhalf[:, :], -0.5))
    st["one"], st["mhalf"], st["ident"] = [ONES], [MH], par_tok

    need(PE, par_tok, z)
    t = transposes(0, [(0, vec1[:, :]), (P, vec2[:, :])])
    need(DVE, t)
    st["cols"] = [done(DVE, DVE.tensor_copy(cols[:, 0:NCOL], ps[:, 0, 0:NCOL]))]
    need(SCA, st["cols"])
    t = done(SCA, SCA.activation(sil_t[:, :], cols[:, 0:16], ACT.Exp, scale=-1.0))
    need(DVE, t)
    t = done(DVE, DVE.tensor_scalar(sil_t[:, :], sil_t[:, :], 1.0, None, ALU.add))
    need(DVE, t)
    t = done(DVE, DVE.reciprocal(sil_t[:, :], sil_t[:, :]))
    need(DVE, t)
    st["silu"] = [done(DVE, DVE.tensor_tensor(sil[:, :], sil_t[:, :], cols[:, 0:16], ALU.mult))]
    need(DVE, par_tok)
    t = done(DVE, DVE.tensor_tensor(lamv[:, 0:4:2, :], lamv[:, 0:4:2, :], lamv[:, 1:4:2, :], ALU.mult))
    need(DVE, t)
    t = done(DVE, DVE.tensor_reduce(lam[:, 0:2], lamv[:, 0:4:2, :], AX, ALU.add))
    need(SCA, t)
    t = done(SCA, SCA.activation(lam[:, 0:2], lam[:, 0:2], ACT.Exp))
    need(DVE, t)
    t = done(DVE, DVE.tensor_tensor(lam[:, 2:3], lam[:, 1:2], lam[:, 0:1], ALU.subtract))
    need(DVE, t)
    t = done(DVE, DVE.tensor_scalar(lam[:, 3:4], lam[:, 2:3], -(0.8 - 0.6), None, ALU.add))
    t = done(DVE, DVE.tensor_copy(posf[:, :], posi[:, :]))
    need(DVE, t)
    for m in range(MT):
        DVE.tensor_scalar(ang[:, m, 0:NROT1], inv[:, 0:NROT1], posf[:, m:m + 1], None, ALU.mult)
        t = done(DVE, DVE.tensor_scalar(ang[:, m, NROT1:], inv[:, NROT1:], posf[:, 2 + m:3 + m], None, ALU.mult))
    need(DVE, t)
    for c in range(2):
        t = done(DVE, DVE.tensor_scalar(rnd[:, :, :], ang[:, :, :], 1 / PI2, 0.25 * (1 - c), ALU.mult, ALU.add))
        need(DVE, t)
        t = done(DVE, DVE.tensor_scalar(rnd[:, :, :], rnd[:, :, :], MAGIC, None, ALU.add))
        need(DVE, t)
        t = done(DVE, DVE.tensor_scalar(rnd[:, :, :], rnd[:, :, :], -MAGIC, None, ALU.add))
        src = ang[:, :, :]
        for piece in (PI_A, PI_B, PI_C):
            need(DVE, t)
            t = done(DVE, DVE.scalar_tensor_tensor(angr[:, c, :, :], rnd[:, :, :], -piece, src, ALU.mult, ALU.add))
            src = angr[:, c, :, :]
        if c == 0:
            need(DVE, t)
            t = done(DVE, DVE.tensor_scalar(src, src, np.pi / 2, None, ALU.add))
        need(DVE, t)
        t = done(DVE, DVE.tensor_scalar(src, src, 3.1415925, -3.1415925, ALU.min, ALU.max))
        need(DVE, t)
    need(SCA, t)
    st["trig"] = [done(SCA, SCA.activation(trig[:, :, :, :], angr[:, :, :, :], ACT.Sin))]

    ada_list = [(part, kt, half) for part in range(5) for kt in range(KD) for half in range(2)]

    def ada_loop(part):
        def body(i):
            for q_ in range(4):
                for half in range(2):
                    ada_half(part, i * 4 + q_, half, isinstance(i, int) and i == 0 and q_ == 0)
        repeat(4, body)

    ada_done = []

    def ada_next(n):
        for _ in range(n):
            part, kt, half = ada_list.pop(0)
            ada_half(part, kt, half, kt == 0)
            if kt == KD - 1 and half == 1:
                ada_done.append(part)

    ada_loop(1)
    del ada_list[2 * KD:4 * KD]
    mem_hi = sb("mem_hi", "big", 24 * KB, [KD, S], F32R)
    mem_lo = sb("mem_lo", "big", 40 * KB, [KD, S], F32R)
    mem_n = [memt[:, m, :] for m in range(MT)]
    x_n = [norm_x[m][:, :] for m in range(MT)]
    junk_m = sb("junk_m", "big", 16 * KB, [D])

    def memory_norm():
        for m in range(MT):
            st["ms", m] = [row_rsqrt(mem_n[m], 2 + m, m_in, junk_ap=junk_m[:, :])]
        yield
        for m in range(MT):
            need(DVE, st["ms", m])
            st["nx", m] = [done(DVE, DVE.tensor_scalar(mem_n[m], mem_n[m], sq2[:, 2 + m:3 + m], None, ALU.mult))]
            yield
        yield from norm_to_h(mem_n, cols[:, C_GMEM:C_GMEM + 16], dst=(mem_hi, mem_lo))
        yield from norm_rows(x, x_n, 0, [[x_in], [x_in]])

    for _ in memory_norm():
        ada_next(1)

    def modulated_gain(part_scale, gcol):
        need(DVE, st["mod", part_scale])
        return done(DVE, DVE.scalar_tensor_tensor(gsc[:, :], mod[:, part_scale * 16:part_scale * 16 + 16], 1.0,
                                                  cols[:, gcol:gcol + 16], ALU.add, ALU.mult))

    def first_transposes():
        for g in range(4):
            bs = (4, 5) if g % 2 == 0 else (6, 7)
            need(PE, st["nx", 0], st["nx", 1], *[st.get(("bank", b)) for b in bs])
            t = transposes(bs[0], [(k * S + m * P, x_n[m][:, (4 * g + k) * P:(4 * g + k + 1) * P]) for k in range(4) for m in range(MT)])
            yield
            yield
            need(SCA, t)
            t = done(SCA, SCA.activation(x_T[:, 4 * g:4 * g + 4, :].rearrange("p (b k) n -> p b (k n)", b=2), ps[:, bs[0]:bs[1] + 1, :], ACT.Copy))
            bank_free(bs[0], t)
            bank_free(bs[1], t)
            st["nt", g] = [t]

    kx = sb("cross_k", "big", 56 * KB, [MT, 512])
    need(SCA, tp.last(), tv.last())
    side = Side(ada_finish(1, 7, 4), first_transposes())
    A_m = (mem_hi, mem_lo)
    n_left = len(ada_list) - 3 * 2 * KD

    def part_0(slot):
        def f(j):
            while len(ada_list) > 3 * 2 * KD and (8 * slot + j + 1) * n_left > 15 * (3 * 2 * KD + n_left - len(ada_list)):
                ada_next(1)
        return f
    col_slot(a["w_k_cross_2"][0], 0, KD, (0,), 512, (0, 1), A_m, side=side, extra=part_0(0))
    col_slot(a["w_v_cross_2"][0], 0, KD, (0,), 512, (2, 3), A_m, copy_post((0, 1), kx[:, :, :], 512), side=side, extra=part_0(1))
    side.finish()
    need(PE, ta.last())
    t = transposes(4, [(hh * S + m * P, kx[:, m, hh * P:(hh + 1) * P]) for hh in range(4) for m in range(MT)])
    need(DVE, t)
    kxt = done(DVE, DVE.tensor_copy(kxT[:, :, :].rearrange("p (b k) n -> p b (k n)", b=2), ps[:, 4:6, :]))
    bank_free(4, kxt)
    bank_free(5, kxt)
    look_ahead(a["w_in"][0], (3072,))
    run(ada_finish(0, 6))
    t = modulated_gain(1, C_GPRE)
    need(DVE, t)
    need(SCA, t, st["trig"])
    for g in range(4):
        h_make.append(lambda g=g: to_halves(g, None, gsc, mod[:, 0:16]))
    h_make.pop(0)()
    for s_ in copy_post((2, 3), vx[:, :, :], 512):
        s_()
    A_h = (h_hi, h_lo)

    work1 = [[sb(f"w1_{n}{p}", reg, (o0 + o) * KB, [w]) for n, o, w in (("qT", 0, TILE), ("kT", 4, TILE), ("s0", 8, 512), ("s1", 10, TILE))]
             for p, (reg, o0) in enumerate((("h", 0), ("big", 48)))]
    qkA = [proj[:, m, 0:2048].rearrange("p (h n) -> p h n", n=128) for m in range(MT)]
    qkB = [proj[:, m, 3072:5120].rearrange("p (h n) -> p h n", n=64) for m in range(MT)]

    def unit(pairs):
        def f(t, dst, nk):
            for n, (l, r) in enumerate(pairs):
                ins = PE.matmul(dst, l(t), r(nk), start=n == 0, stop=n == len(pairs) - 1)
            return ins
        return f

    def groupA(g):
        p = g % 2
        QT, KT = (w[:, :].rearrange("p (u n) -> p u n", u=4) for w in work1[p][:2])
        items = lambda base: [(i * S + m * P, proj[:, m, base + (4 * g + i) * P:base + (4 * g + i + 1) * P]) for i in range(4) for m in range(MT)]
        units = [unit([(lambda t, i=i: QT[:, i, t * P:(t + 1) * P], lambda nk, i=i: KT[:, i, 0:nk])]) for i in range(4)]
        return p, attention(p, qk_prep(items(0), items(1024)), units,
                            lambda i, kt: proj[:, kt, 2048 + (4 * g + i) * P:2048 + (4 * g + i + 1) * P],
                            lambda t: proj[:, t, 512 * g:512 * g + 512].rearrange("p (h n) -> p h n", h=4),
                            128 ** -0.5, lambda t: dilated[:, P:S] if t == 0 else dilated[:, :], work1[p],
                            cnt=lambda t: count[:, P:S] if t == 0 else count[:, :])

    def mix_col(k):
        return k * P if k < 8 else 3072 + 512 * (k % 2) + P * ((k - 8) // 2)

    def groupB(g):
        p = 1
        QT, KT = (w[:, :].rearrange("p (u n) -> p u n", u=4) for w in work1[p][:2])
        items = lambda base: [(mu * S + m * P, proj[:, m, base + 512 * mu + P * g:base + 512 * mu + P * (g + 1)]) for mu in range(2) for m in range(MT)]
        units = []
        for e in range(2):
            for mu in range(2):
                units.append(unit([(lambda t, e=e, mu=mu: QT[64 * e:64 * e + 64, mu, t * P:(t + 1) * P],
                                                    lambda nk, e=e, mu=mu: KT[64 * e:64 * e + 64, mu, 0:nk])]))
        return p, attention(p, qk_prep(items(3072), items(4096)), units,
                            lambda i, kt: proj[:, kt, 5120 + (2 * g + i) * P:5120 + (2 * g + i + 1) * P],
                            lambda t: proj[:, t, 3072:4096].rearrange("p (e n) -> p e n", e=2)[:, :, P * g:P * (g + 1)],
                            64 ** -0.5, lambda t: causal[:, P:S] if t == 0 else causal[:, :], work1[p], diff=True)

    def slots(w, starts, dst, side=None, extra=None, first_posts=()):
        posts = list(first_posts)
        for n, c0 in enumerate(starts):
            width = min(512, w.shape[1] - c0)
            b = (0, 1) if n % 2 == 0 else (2, 3)
            col_slot(w, 0, KD, (c0,), width, b, A_h, posts, side=side, extra=(lambda j, n=n: extra(8 * n + j)) if extra else None)
            posts = copy_post(b, dst[:, :, c0:c0 + width], width)
        return posts

    posts = slots(a["w_in"][0], range(3072, 6144, 512), proj, extra=lambda j: ada_next(1))

    def ropes_b():
        need(DVE, ta.last())
        for m in range(MT):
            yield from rope(qkB[m], qkB[m], 32, 32, R_B, m, rope_b)
        need(PE, st["rope"])
        need(SCA, st["rope"])

    st["set", 0] = st["set", 1] = []
    need(DVE, st["trig"])
    side = Side(wait_steps(2), ada_finish(2, 7, 4), ropes_b(), *[groupB(g)[1] for g in range(4)])
    posts = slots(a["w_in"][0], range(0, 3072, 512), proj, side=side, first_posts=posts,
                  extra=lambda j: ada_next(1) if j % 3 == 2 else None)
    for s_ in posts:
        s_()
    side.finish()
    barrier()

    for n_, (dst_, src_) in enumerate(((count, "k_count"), (dilated, "k_dilated"), (gout[0], "g_out_a"), (gout[1], "g_subln_b"))):
        v = a[src_] if n_ < 2 else a[src_].to_broadcast([P, P])
        late = t_late.done(q.dma_start(dst_[:, :], v))
    for m in range(MT):
        run(rope(qkA[m], qkA[m], 16, 64, R_A, m, rope_a))
    barrier()
    need(DVE, late)
    heads = lambda m, c0: proj[:, m, c0:c0 + 1024].rearrange("p (h n) -> p h n", h=8)

    def norm_b():
        for m in range(MT):
            yield from head_norm(heads(m, 3072), gout[1][:, :], 1.0 - (0.8 - 0.6), 1, hsq[0][:, :])
    together(groupA(0)[1], groupA(1)[1], norm_b())
    barrier()
    together(*[head_norm(heads(m, 0), gout[0][:, :], 1.0, m, hsq[1 + m][:, :]) for m in range(MT)])
    while len(ada_list) > 2 * KD:
        ada_next(1)
    run(ada_finish(3, 7))
    barrier()
    gate_bcast(2, C_GPOSTA)
    barrier()
    mix_ready = transposed_mix(lambda k, m: proj[:, m, mix_col(k):mix_col(k) + P], tv.last())
    barrier()

    def post_norm_add(y_done):
        for m in range(MT):
            y = ps[:, 4 * m:4 * m + 4, :]
            need(SCA, y_done[m])
            t = done(SCA, SCA.activation(junks[m][:, :].rearrange("p (b n) -> p b n", b=4), y, ACT.Square, accum_out=sq[:, 2 + m:3 + m]))
            need(POOL, t)
            st["ys", m] = [rsqrt_cols(sq2[:, 2 + m:3 + m], sq[:, 2 + m:3 + m], 1, 1.0 / D)]
        for m in range(MT):
            y = ps[:, 4 * m:4 * m + 4, :]
            need(DVE, st["ys", m], y_done[m])
            tmp = post_tmp[m][:, :].rearrange("p (b n) -> p b n", b=4)
            t = done(DVE, DVE.scalar_tensor_tensor(tmp, y, sq2[:, 2 + m:3 + m], gate_row[:, :].rearrange("p (b n) -> p b n", b=4), ALU.mult, ALU.mult))
            for b in range(4 * m, 4 * m + 4):
                bank_free(b, t)
            need(DVE, t)
            st["x", m] = [done(DVE, DVE.tensor_tensor(x[:, m, :], x[:, m, :], post_tmp[m][:, :], ALU.add))]

    def plain_add(y_done):
        for m in range(MT):
            need(DVE, y_done[m])
            t = done(DVE, DVE.tensor_tensor(x[:, m, :].rearrange("p (b n) -> p b n", b=4), x[:, m, :].rearrange("p (b n) -> p b n", b=4),
                                            ps[:, 4 * m:4 * m + 4, :], ALU.add))
            for b in range(4 * m, 4 * m + 4):
                bank_free(b, t)
            st["x", m] = [t]

    x_ready = lambda: [st["x", 0], st["x", 1]]

    y_done = row_stage(a["w_out"][0], mixT, KD, mix_ready, ada=4)
    post_norm_add(y_done)

    run(ada_finish(4, 0))
    t = modulated_gain(4, C_GFFN)
    need(DVE, t)
    norm(x, gsc, mod[:, 3 * 16:4 * 16], x_ready(), a["w_gate"][0])

    def hidden_out(dst, i, banks, src, tok_key):
        def tr():
            need(PE, st[tok_key], st.get(("bank", banks[0])), st.get(("bank", banks[1])))
            for c in range(4):
                for m in range(MT):
                    ins = PE.transpose(ps[:, banks[c // 2], (c % 2) * S + m * P:(c % 2) * S + (m + 1) * P], src[:, m, c * P:(c + 1) * P], ident[:, :])
            st["hid_t", banks[0]] = [done(PE, ins)]

        def ev():
            need(SCA, st["hid_t", banks[0]])
            d = dst[:, bass.ds(i * 4, 4), :].rearrange("p (b k) n -> p b (k n)", b=2)
            t = done(SCA, SCA.activation(d, ps[:, banks[0]:banks[1] + 1, :], ACT.Copy))
            bank_free(banks[0], t)
            bank_free(banks[1], t)
        return [tr, ev]

    def gate_steps():
        g = ps[:, 0:2, :]

        def ex():
            need(SCA, st["full", 0], st.get(("hid_t", 4)))
            st["sg"] = [done(SCA, SCA.activation(sg1[:, :, :], g, ACT.Exp, scale=-1.0))]

        def plus():
            need(DVE, st["sg"])
            st["sg"] = [done(DVE, DVE.tensor_scalar(sg1[:, :, :], sg1[:, :, :], 1.0, None, ALU.add))]

        def rec():
            need(DVE, st["sg"])
            st["sg"] = [done(DVE, DVE.reciprocal(sg1[:, :, :], sg1[:, :, :]))]

        def mul():
            need(DVE, st["sg"])
            t = done(DVE, DVE.tensor_tensor(sg1[:, :, :], g, sg1[:, :, :], ALU.mult))
            st["sg"] = [t]
            bank_free(0, t)
            bank_free(1, t)
        return [ex, plus, rec, mul]

    def up_steps(i):
        def mul():
            need(DVE, st["full", 2], st["sg"])
            t = done(DVE, DVE.tensor_tensor(sg1[:, :, :], ps[:, 2:4, :], sg1[:, :, :], ALU.mult))
            st["sgu"] = [t]
            bank_free(2, t)
            bank_free(3, t)
        return [mul] + hidden_out(hid1, i, (4, 5), sg1, "sgu")

    def ffn1(i, i0):
        prev = up_steps(i0 + i - 1) if not (isinstance(i, int) and i + i0 == 0) else []
        c = bass.ds((i0 + i) * 512, 512)

        def extra(slot):
            def f(j):
                if i0 == 0 and j % 2 == 1:
                    n = slot * 4 + j // 2
                    ada_half(5, i * 4 + n // 2, n % 2, isinstance(i, int) and i == 0 and n // 2 == 0)
            return f
        col_slot(a["w_gate"][0], 0, KD, c, 512, (0, 1), A_h, prev, extra=extra(0))
        col_slot(a["w_up"][0], 0, KD, c, 512, (2, 3), A_h, gate_steps(), extra=extra(1))
    repeat(4, lambda i: ffn1(i, 0), peel=2)
    repeat(DFF1 // 512 - 4, lambda i: ffn1(i, 4), peel=1)
    for s_ in up_steps(DFF1 // 512 - 1):
        s_()
    barrier()
    run(ada_finish(5, 6))
    barrier()
    gate_bcast(5, C_GPOSTF)
    barrier()
    y_done = row_stage(a["w_down"][0], hid1, DFF1 // P, [])
    post_norm_add(y_done)

    norm(x, cols[:, C_GMIX:C_GMIX + 16], None, x_ready(), a["w_in_2"][0], (4096,))
    pj = sb("proj_2", "big", 0, [MT, IN2])
    O_CQ, O_CKV, O_KR, O_QD, O_KD, O_VD, O_QI, O_KI, O_WI = 0, 512, 768, 832, 1856, 2880, 3904, 4928, 4992
    cq_hi = sb("cq_hi", "big", 40 * KB, [6, S], F32R)
    cq_lo = sb("cq_lo", "big", 54 * KB, [6, S], F32R)
    cq_junk = sb("cq_junk", "big", 46 * KB, [512])
    qr = sb("mla_q_rope", "h", 28 * KB, [MT, 8, 64])
    pad = sb("padded_keys", "acc", 8 * KB, [MT, 2, P])
    krT = sb("k_rope_T", "acc", 10 * KB, [2, S])
    kiT = sb("k_idx_T", "acc", 12 * KB, [2, S])
    selb = sb("selection", "acc", 14 * KB, [MT, S])
    rope_c = [sb("rope_t2", "big", 48 * KB, [512])] + [sb(f"rope_v{i}", "big", (50 + i) * KB, [256]) for i in range(2)]
    qiT = sb("q_idx_T", "big", 40 * KB, [8, P])
    rel = [sb("idx_relu0", "big", 44 * KB, [4, S]), sb("idx_relu1", "acc", 0, [4, S])]
    score = sb("score", "big", 52 * KB, [S])
    kept = sb("score_left", "big", 53 * KB, [S])

    def rotated(cols_, heads, width, half, rot, dst=None):
        for m in range(MT):
            v = cols_(m).rearrange("p (h n) -> p h n", h=heads)[:, :, width[0]:width[1]]
            yield from rope(v, dst(m) if dst else v, heads, half, rot, m, rope_c)

    def padded_T(c0, dst, bank):
        t = done(DVE, DVE.memset(pad[:, :, :, :], 0.0))
        need(DVE, t)
        for m in range(MT):
            DVE.tensor_copy(pad[:, m, 0, 0:64], pj[:, m, c0:c0 + 64])
            t = done(DVE, DVE.tensor_copy(pad[:, m, 1, 64:128], pj[:, m, c0:c0 + 64]))
        need(PE, t, st.get(("bank", bank)))
        t = transposes(bank, [(e * S + m * P, pad[:, m, e, :]) for e in range(2) for m in range(MT)])
        yield
        yield
        need(DVE, t)
        t = done(DVE, DVE.tensor_copy(dst[:, :, :].rearrange("p e n -> p (e n)"), ps[:, bank, :]))
        bank_free(bank, t)
        need(PE, t)

    def index_keys():
        need(DVE, ta.last())
        yield from rotated(lambda m: pj[:, m, O_QI:O_QI + 1024], 16, (0, 16), 8, R_IDX)
        yield from rotated(lambda m: pj[:, m, O_KI:O_KI + 64], 1, (0, 16), 8, R_IDX)
        yield from padded_T(O_KI, kiT, 6)
        for m in range(MT):
            t = done(DVE, DVE.tensor_scalar(wi[:, m, :], pj[:, m, O_WI:O_WI + 16], 16 ** -0.5 * 64 ** -0.5, None, ALU.mult))
        need(DVE, t)

    def indexer():
        for m in range(MT):
            nk = (m + 1) * P
            need(PE, st.get(("bank", 4)), st.get(("bank", 5)))
            t = transposes(4, [(j * P, pj[:, m, O_QI + j * P:O_QI + (j + 1) * P]) for j in range(8)])
            yield
            yield
            need(SCA, t)
            qt = done(SCA, SCA.activation(qiT[:, :, :].rearrange("p (b k) n -> p b (k n)", b=2), ps[:, 4:6, :], ACT.Copy))
            bank_free(4, qt)
            bank_free(5, qt)
            need(PE, qt)
            stt = None
            for g in range(4):
                need(PE, st.get(("bank", 6)), st.get(("bank", 7)))
                for i in range(4):
                    ins = PE.matmul(ps[:, 6 + i // 2, (i % 2) * S:(i % 2) * S + nk], qiT[:, 2 * g + i // 2, :], kiT[:, i % 2, 0:nk],
                                    start=True, stop=True)
                t = done(PE, ins)
                yield
                yield
                need(SCA, t, st.get(("idx_v", g % 2)))
                e = done(SCA, SCA.activation(rel[g % 2][:, :, 0:nk].rearrange("p (b u) n -> p b u n", b=2),
                                             ps[:, 6:8, :].rearrange("p b (u n) -> p b u n", u=2)[:, :, :, 0:nk], ACT.Relu))
                bank_free(6, e)
                bank_free(7, e)
                need(DVE, e)
                for i in range(4):
                    hh = 4 * g + i
                    need(DVE, stt)
                    if hh == 0:
                        stt = done(DVE, DVE.tensor_scalar(score[:, 0:nk], rel[0][:, 0, 0:nk], wi[:, m, 0:1], None, ALU.mult))
                    else:
                        stt = done(DVE, DVE.scalar_tensor_tensor(score[:, 0:nk], rel[g % 2][:, i, 0:nk], wi[:, m, hh:hh + 1],
                                                                 score[:, 0:nk], ALU.mult, ALU.add))
                st["idx_v", g % 2] = [stt]
            need(DVE, stt)
            stt = done(DVE, DVE.memset(score[0:64, nk - 64:nk], DROPPED))
            src = score
            for rnd_ in range(TOPK // 8):
                need(DVE, stt)
                t = done(DVE, DVE.max(m8[:, :], src[:, 0:nk]))
                need(DVE, t)
                stt = done(DVE, DVE.match_replace(kept[:, 0:nk], m8[:, :], src[:, 0:nk], TAKEN))
                src = kept
                if rnd_ % 2:
                    yield
            need(DVE, stt)
            done(DVE, DVE.tensor_scalar(selb[:, m, 0:nk], kept[:, 0:nk], (DROPPED + TAKEN) / 2, NEG, ALU.is_ge, ALU.mult))

    def latents():
        need(SCA, tv.last())
        for m in range(MT):
            for s_i, (c0, n) in enumerate(((O_CQ, 512), (O_CKV, 256))):
                st["lt", m, s_i] = [row_rsqrt(pj[:, m, c0:c0 + n], 2 * m + s_i, junk_ap=cq_junk[:, 0:n])]
            yield
        for m in range(MT):
            for s_i, (c0, n) in enumerate(((O_CQ, 512), (O_CKV, 256))):
                need(DVE, st["lt", m, s_i])
                t = done(DVE, DVE.tensor_scalar(pj[:, m, c0:c0 + n], pj[:, m, c0:c0 + n], sq2[:, 2 * m + s_i:2 * m + s_i + 1], None, ALU.mult))
        need(PE, t, *[st.get(("bank", b)) for b in (4, 5, 6)])
        t = transposes(4, [(k * S + m * P, pj[:, m, k * P:(k + 1) * P]) for k in range(6) for m in range(MT)])
        yield
        yield
        for b in range(3):
            halves = [(k, ps[:, 4 + b, (k % 2) * S:(k % 2 + 1) * S], cols[:, C_GCQ + k:C_GCQ + k + 1]) for k in (2 * b, 2 * b + 1)]
            need(SCA, t)
            for k, src, gain in halves:
                hi = done(SCA, SCA.activation(cq_hi[:, k, :], src, ACT.Copy, scale=gain))
            need(DVE, hi, t)
            for k, src, gain in halves:
                lo = done(DVE, DVE.scalar_tensor_tensor(cq_lo[:, k, :], src, gain, r32(cq_hi[:, k, :]), ALU.mult, ALU.subtract))
            bank_free(4 + b, lo)
            yield
        st["latents"] = [hi, lo]

    posts = slots(a["w_in_2"][0], [4096, 3584, 4608], pj)
    side = Side(wait_steps(4), index_keys(), indexer(), latents())
    for n in range(7):
        b = (2, 3) if n % 2 == 0 else (0, 1)
        col_slot(a["w_in_2"][0], 0, KD, (512 * n,), 512, b, A_h, posts, side=side)
        posts = copy_post(b, pj[:, :, 512 * n:512 * n + 512], 512)
    for s_ in posts:
        s_()
    side.finish()

    need(PE, st["latents"])
    qm = sb("mla_q", "h", 0, [MT, 1536])
    kvm = sb("mla_kv", "h", 12 * KB, [MT, 2048])

    def rest_rotary():
        need(DVE, ta.last())
        for c in (O_QD, O_KD):
            yield from rotated(lambda m, c=c: pj[:, m, c:c + 1024], 8, (0, 32), 16, R_DSA)
        yield from rotated(lambda m: pj[:, m, O_KR:O_KR + 64], 1, (0, 64), 32, R_MLA)
        yield from padded_T(O_KR, krT, 4)

    side = Side(rest_rotary())
    rest = []
    for n in range(3):
        b = (0, 1) if n % 2 == 0 else (2, 3)
        col_slot(a["w_qb_2"][0], 0, 4, (n * 512,), 512, b, (cq_hi, cq_lo), rest, lag=1, side=side)
        rest = copy_post(b, qm[:, :, n * 512:(n + 1) * 512], 512)
    ck = (cq_hi[:, 4:6, :], cq_lo[:, 4:6, :])
    for n in range(4):
        b = (2, 3) if n % 2 == 0 else (0, 1)
        col_slot(a["w_kvb_2"][0], 0, 2, (n * 512,), 512, b, ck, rest, lag=0, side=side)
        rest = copy_post(b, kvm[:, :, n * 512:(n + 1) * 512], 512)
    side.finish()
    need(DVE, ta.last())
    run(rotated(lambda m: qm[:, m, :], 8, (128, 192), 32, R_MLA, lambda m: qr[:, m, :, :]))
    for s_ in rest:
        s_()
    barrier()

    names = ("qT", "kT")
    work2 = [[sb(f"w2_{n}{p}", "big", (40 + 8 * p + 4 * i) * KB, [TILE]) for i, n in enumerate(names)]
             + [sb(f"w2_s0{p}", "acc", 4 * KB * p, [TILE]), sb(f"w2_s1{p}", "big", (56 + 4 * p) * KB, [TILE])] for p in range(2)]
    qrT = [sb("q_rope_T0", "acc", 8 * KB, [2, S]), sb("q_rope_T1", "acc", 12 * KB, [2, S])]
    st["set", 0] = st["set", 1] = []

    def groupM(g):
        p = g % 2
        QT, KT = (w[:, :].rearrange("p (u n) -> p u n", u=4) for w in work2[p][:2])
        items_q = [(i * S + m * P, qm[:, m, 192 * (4 * g + i):192 * (4 * g + i) + P]) for i in range(4) for m in range(MT)]
        items_k = [(i * S + m * P, kvm[:, m, 256 * (4 * g + i):256 * (4 * g + i) + P]) for i in range(4) for m in range(MT)]

        def extra(p):
            qv = qr[:, :, :, :].rearrange("p m h n -> p m (h n)")
            t = transposes(4 * p, [(j * S + m * P, qv[:, m, (2 * g + j) * P:(2 * g + j + 1) * P]) for j in range(2) for m in range(MT)])
            need(SCA, t)
            return [done(SCA, SCA.activation(qrT[p][:, :, :].rearrange("p j n -> p (j n)"), ps[:, 4 * p, :], ACT.Copy))]
        units = [unit([
            (lambda t, i=i: QT[:, i, t * P:(t + 1) * P], lambda nk, i=i: KT[:, i, 0:nk]),
            (lambda t, i=i: qrT[p][:, i // 2, t * P:(t + 1) * P], lambda nk, i=i: krT[:, i % 2, 0:nk])]) for i in range(4)]
        return p, attention(p, qk_prep(items_q, items_k, extra), units,
                            lambda i, kt: kvm[:, kt, 256 * (4 * g + i) + P:256 * (4 * g + i) + 2 * P],
                            lambda t: pj[:, t, O_QI + 512 * g:O_QI + 512 * g + 512].rearrange("p (h n) -> p h n", h=4),
                            192 ** -0.5, lambda t: chunk[:, P:S] if t == 0 else chunk[:, :], work2[p])

    def groupD(g):
        p = g % 2
        QT, KT = (w[:, :].rearrange("p (u n) -> p u n", u=4) for w in work2[p][:2])
        items = lambda base: [(i * S + m * P, pj[:, m, base + (4 * g + i) * P:base + (4 * g + i + 1) * P]) for i in range(4) for m in range(MT)]
        units = [unit([(lambda t, i=i: QT[:, i, t * P:(t + 1) * P], lambda nk, i=i: KT[:, i, 0:nk])]) for i in range(4)]
        return p, attention(p, qk_prep(items(O_QD), items(O_KD)), units,
                            lambda i, kt: pj[:, kt, O_VD + (4 * g + i) * P:O_VD + (4 * g + i + 1) * P],
                            lambda t: pj[:, t, O_QD + 512 * g:O_QD + 512 * g + 512].rearrange("p (h n) -> p h n", h=4),
                            128 ** -0.5, lambda t: selb[:, t, 0:(t + 1) * P], work2[p])

    run_two([groupM(0), groupM(1), groupD(0), groupD(1)])
    barrier()
    mix_ready = transposed_mix(lambda k, m: pj[:, m, O_QI + k * P:O_QI + (k + 1) * P] if k < 8 else
                               pj[:, m, O_QD + (k - 8) * P:O_QD + (k - 7) * P])
    barrier()
    y_done = row_stage(a["w_out_2"][0], mixT, KD, mix_ready)
    plain_add(y_done)

    norm(x, cols[:, C_GCROSS:C_GCROSS + 16], None, x_ready(), a["w_q_cross_2"][0])
    qx = sb("cross_q", "big", 0, [MT, 512])
    ox = sb("cross_o", "big", 4 * KB, [MT, 512])
    oxT = sb("cross_oT", "big", 8 * KB, [4, S])
    col_slot(a["w_q_cross_2"][0], 0, KD, (0,), 512, (0, 1), A_h)
    for s_ in copy_post((0, 1), qx[:, :, :], 512):
        s_()
    barrier()
    st["set", 0] = st["set", 1] = []

    def prep_x(p, QT, KT):
        t = transposes(4 * p, [(i * S + m * P, qx[:, m, i * P:(i + 1) * P]) for i in range(4) for m in range(MT)])
        need(SCA, t)
        e = done(SCA, SCA.activation(QT[:, :].rearrange("p (b n) -> p b n", b=2), ps[:, 4 * p:4 * p + 2, :], ACT.Copy))
        yield
        return [e]
    QTx = work2[0][0][:, :].rearrange("p (u n) -> p u n", u=4)
    units = [unit([(lambda t, i=i: QTx[:, i, t * P:(t + 1) * P], lambda nk, i=i: kxT[:, i, 0:nk])]) for i in range(4)]
    run_two([(0, attention(0, prep_x, units, lambda i, kt: vx[:, kt, i * P:(i + 1) * P],
                           lambda t: ox[:, t, :].rearrange("p (h n) -> p h n", h=4), 128 ** -0.5, lambda t: None, work2[0], nkts=(2, 2)))])
    need(PE, tv.last())
    t = transposes(4, [(k * S + m * P, ox[:, m, k * P:(k + 1) * P]) for k in range(4) for m in range(MT)])
    need(SCA, t)
    t = done(SCA, SCA.activation(oxT[:, :, :].rearrange("p (b k) n -> p b (k n)", b=2), ps[:, 4:6, :], ACT.Copy))
    barrier()
    y_done = row_stage(a["w_o_cross_2"][0], oxT, 4, [t])
    plain_add(y_done)

    norm(x, cols[:, C_GMLP:C_GMLP + 16], None, x_ready(), a["w_up_2"][0])

    def relu_steps(i, slot):
        b = (0, 1) if slot == 0 else (2, 3)
        tb = (4, 5) if slot == 0 else (6, 7)

        def rel_():
            need(SCA, st["full", b[0]], st.get(("hid_t", tb[0])))
            t = done(SCA, SCA.activation(r2[slot][:, :, :], ps[:, b[0]:b[1] + 1, :], ACT.Relu))
            st["relu", slot] = [t]
            bank_free(b[0], t)
            bank_free(b[1], t)

        def sq_():
            need(DVE, st["relu", slot])
            st["relu_sq", slot] = [done(DVE, DVE.tensor_tensor(r2[slot][:, :, :], r2[slot][:, :, :], r2[slot][:, :, :], ALU.mult))]
        return [rel_, sq_] + hidden_out(hid2, 2 * i + slot, tb, r2[slot], ("relu_sq", slot))

    def mlp(i):
        prev = relu_steps(i - 1, 1) if not (isinstance(i, int) and i == 0) else []
        col_slot(a["w_up_2"][0], 0, KD, bass.ds(i * 1024, 512), 512, (0, 1), A_h, prev)
        col_slot(a["w_up_2"][0], 0, KD, bass.ds(i * 1024 + 512, 512), 512, (2, 3), A_h, relu_steps(i, 0))
    repeat(DFF2 // 1024, mlp, peel=2)
    for s_ in relu_steps(DFF2 // 1024 - 1, 1):
        s_()
    barrier()
    y_done = row_stage(a["w_down_2"][0], hid2, DFF2 // P, [])
    g_row = sb("g_final_rows", "acc", 0, [D])
    gf = t_late.done(q.dma_start(g_row[:, :], a["g_final_2"].rearrange("(o d) -> o d", o=1).to_broadcast([P, D])))
    plain_add(y_done)
    for m in range(MT):
        t = row_rsqrt(x[:, m, :], m, tv.last(), junk_ap=norm_x[m][:, :])
        need(DVE, t, gf)
        t = done(DVE, DVE.scalar_tensor_tensor(x[:, m, :], x[:, m, :], sq2[:, m:m + 1], g_row[:, :], ALU.mult, ALU.mult))
        need(SP, t)
        o = t_out.done(SP.dma_start(out[0, m * P:(m + 1) * P, :], x[:, m, :]))
    need(SP, o)


_INS = ["x", "c", "positions", "w_ada", "b_ada", "g_pre_attn", "w_in", "g_out_a", "lambda_q1", "lambda_k1", "lambda_q2",
        "lambda_k2", "g_subln_b", "w_out", "g_post_attn", "g_pre_ffn", "w_gate", "w_up", "w_down", "g_post_ffn",
        "mem_2", "positions_2", "g_mix_2", "w_in_2", "g_cq_2", "g_ckv_2", "w_qb_2", "w_kvb_2", "w_out_2", "g_cross_2",
        "g_mem_2", "w_q_cross_2", "w_k_cross_2", "w_v_cross_2", "w_o_cross_2", "g_mlp_2", "w_up_2", "w_down_2",
        "g_final_2"]


def kernel(**inputs):
    import concourse.bacc as bacc
    from concourse.bass_utils import run_bass_kernel_spmd

    nc = bacc.Bacc("TRN2", target_bir_lowering=False, num_devices=1)
    arrays, aps = {}, {}
    given = {n: np.ascontiguousarray(inputs[n]) for n in _INS}
    given.update(shape_constants())
    for name, v in given.items():
        arrays[f"in_{name}"] = v
        aps[name] = nc.dram_tensor(f"in_{name}", v.shape, mybir.dt.from_np(v.dtype), kind="ExternalInput").ap()
    out = nc.dram_tensor("out_x", (1, S, D), F32, kind="ExternalOutput").ap()
    build(nc, aps, out)
    r = run_bass_kernel_spmd(nc, [arrays], core_ids=[0])
    return r.results[0]["out_x"]
```

```python
import numpy as np
import concourse.bass as bass
from concourse import mybir

F32 = mybir.dt.float32
F32R = mybir.dt.float32r
I32 = mybir.dt.int32
ALU = mybir.AluOpType
ACT = mybir.ActivationFunctionType
AX = mybir.AxisListType.X

P = 128
S = 256
MT = S // P
D = 2048
KD = D // P
DFF1, DFF2 = 5632, 8192
IN1, IN2 = 6144, 5008
BANK = 512
RAW, SPLIT = 8, 4
TILE = 1024
EPS = 1e-6
NEG = -1e30
DROPPED = -3.0e38
TAKEN = -3.3e38
MAGIC = 12582912.0
TOPK = 64
KB = 1024

C_C, C_BADA, C_GPOSTA = 0, 16, 112
C_GPRE, C_GFFN, C_GMIX, C_GCROSS, C_GMEM, C_GMLP, C_GCQ, C_GCKV, C_GPOSTF = (
    128, 144, 160, 176, 192, 208, 224, 228, 230)
NCOL = 246

R_A, R_B, R_MLA, R_DSA, R_IDX = (0, 64), (64, 32), (96, 32), (128, 16), (144, 8)
NROT, NROT1 = 152, 96
PI2 = 2 * np.pi
PI_A = 6.28125
PI_B = float(np.float32(PI2 - PI_A))
PI_C = float(np.float32(PI2 - PI_A - PI_B))


def shape_constants():
    t = np.arange(P)[:, None] + P
    k = np.arange(S)[None, :]
    d = t - k
    count = ((d >= 0) & (d <= 128)).astype(np.float32)
    count += (d >= 0) & (d % 4 == 0)
    count += (d >= 0) & (d % 16 == 0)
    dilated = np.where(count > 0, 0, NEG).astype(np.float32)
    causal = np.where(d >= 0, 0, NEG).astype(np.float32)
    chunk = np.where(k // 64 <= t // 64, 0, NEG).astype(np.float32)
    f = lambda theta, half: (np.float32(theta) ** (-np.arange(half, dtype=np.float32) / np.float32(half))).astype(np.float32)
    inv = np.concatenate([f(10000.0, 64), f(10000.0, 32), f(500000.0, 32), f(500000.0, 16), f(500000.0, 8)])
    return {
        "k_ident": np.eye(P, dtype=np.float32), "k_count": count, "k_dilated": dilated,
        "k_causal": causal, "k_chunk": chunk, "k_inv": inv[None, :].astype(np.float32),
    }


class Tok:

    def __init__(self, track, v, loop, epoch):
        self.track, self.v, self.loop, self.epoch = track, v, loop, epoch


class Loop:

    def __init__(self, reg, start, n, per):
        self.reg, self.start, self.n, self.per, self.live = reg, start, n, per, True


class Side:

    def __init__(self, *parts):
        self.parts = list(parts)

    def step(self):
        while self.parts:
            try:
                next(self.parts[0])
                return
            except StopIteration:
                self.parts.pop(0)

    def finish(self):
        while self.parts:
            self.step()


class Clock:

    def __init__(self):
        self.loop, self.epoch, self.tracks = None, 0, []


class Track:

    def __init__(self, nc, clock, name, step=1):
        self.sem, self.clock, self.step, self.n, self.name = nc.alloc_semaphore(name), clock, step, 0, name
        clock.tracks.append(self)

    def done(self, ins):
        ins.then_inc(self.sem, self.step)
        self.n += self.step
        return Tok(self, self.n, self.clock.loop, self.clock.epoch)

    def last(self):
        return Tok(self, self.n, self.clock.loop, self.clock.epoch)


def build(nc, a, out):
    clock = Clock()
    PE, DVE, SCA, POOL, SP = nc.tensor, nc.vector, nc.scalar, nc.gpsimd, nc.sync
    tp, tv, ta, tg = (Track(nc, clock, n) for n in ("s_tensor", "s_vector", "s_scalar", "s_pool"))
    track_of = {id(PE): tp, id(DVE): tv, id(SCA): ta, id(POOL): tg}
    t_raw = [Track(nc, clock, f"s_raw{r}", 16) for r in range(RAW)]
    t_par = Track(nc, clock, "s_parameters", 16)
    t_x = Track(nc, clock, "s_x", 16)
    t_mem = Track(nc, clock, "s_mem", 16)
    t_late = Track(nc, clock, "s_late", 16)
    t_out = Track(nc, clock, "s_out", 16)
    st = {}
    waited = {}

    def need(eng, *toks):
        best = {}
        for tok in toks:
            if tok is None:
                continue
            if isinstance(tok, (list, tuple)):
                for x in tok:
                    if x is not None:
                        best.setdefault(id(x.track), []).append(x)
                continue
            best.setdefault(id(tok.track), []).append(tok)
        for group in best.values():
            fixed = [t for t in group if t.loop is None or not t.loop.live]
            moving = [t for t in group if t.loop is not None and t.loop.live]
            if moving:
                v = max(t.v for t in moving)
                lp, tr = moving[0].loop, moving[0].track
                value = lp.reg * lp.per[tr] + (v - lp.start * lp.per[tr])
                eng.wait_ge(tr.sem, value)
            if fixed:
                tr = fixed[0].track
                v = max(t.v + ((t.loop.n - 1 - t.loop.start) * t.loop.per[tr] if t.loop else 0) for t in fixed)
                if waited.get((id(eng), id(tr)), 0) >= v:
                    continue
                if clock.loop is None:
                    waited[(id(eng), id(tr))] = v
                eng.wait_ge(tr.sem, v)

    def done(eng, ins):
        return track_of[id(eng)].done(ins)

    def repeat(n, body, peel=1, tail=0):
        peel, ends = min(peel, n), n
        n = max(peel, n - tail)
        for i in range(peel):
            clock.epoch += 1
            before = {t: t.n for t in clock.tracks}
            body(i)
        if n == peel:
            for i in range(n, ends):
                body(i)
            return
        per = {t: t.n - before[t] for t in clock.tracks}
        mine, epoch = clock.epoch, clock.epoch
        clock.epoch += 1
        base = {t: t.n for t in clock.tracks}
        with nc.Fori(peel, n) as reg:
            lp = Loop(reg, peel, n, per)
            clock.loop = lp
            old = dict(st)
            for k, tok in old.items():
                st[k] = [Tok(x.track, x.v, lp, -1) if x.epoch == mine else x for x in tok]
            body(reg)
            for t in clock.tracks:
                assert t.n - base[t] == per[t], (t.name, t.n - base[t], per[t])
            for k, tok in old.items():
                for x, y in zip(tok, st[k]):
                    if x.epoch == mine:
                        assert y.epoch == clock.epoch and y.v == x.v + per[x.track], (k, x.v, y.v, per[x.track])
            lp.live = False
            clock.loop = None
        for t in clock.tracks:
            t.n = base[t] + per[t] * (n - peel)
        clock.epoch += 1
        waited.clear()
        for i in range(n, ends):
            body(i)

    base0 = -(-nc.sbuf_base // 128) * 128
    plan = {}
    at_ = base0
    for name, size in (("raw", 32 * KB), ("whi", 16 * KB), ("wlo", 16 * KB), ("x", 16 * KB), ("h", 32 * KB),
                       ("big", 64 * KB), ("acc", 16 * KB), ("mem", 8 * KB), ("small", 7 * KB + 256)):
        plan[name] = (at_, size)
        at_ += size

    def sb(name, region, off, shape, dt=F32):
        start, size = plan[region]
        n = 4 * int(np.prod(shape))
        assert off + n <= size, (name, off, n, size)
        return nc.alloc_sbuf_tensor_at(name, [P] + list(shape), dt, offset=start + off)

    raw = [sb(f"raw{r}", "raw", 4 * KB * r, [TILE]) for r in range(RAW)]
    whi = [sb(f"whi{r}", "whi", 4 * KB * r, [TILE], F32R) for r in range(SPLIT)]
    wlo = [sb(f"wlo{r}", "wlo", 4 * KB * r, [TILE], F32R) for r in range(SPLIT)]
    x = sb("x_res", "x", 0, [MT, D])
    h_hi = sb("h_hi", "h", 0, [KD, S], F32R)
    h_lo = sb("h_lo", "h", 16 * KB, [KD, S], F32R)
    acc = [sb(f"ada_acc{i}", "acc", 8 * KB * i, [D]) for i in range(2)]
    kxT = sb("cross_kT", "mem", 0, [4, S])
    vx = sb("cross_v", "mem", 4 * KB, [MT, 512])

    off = [0]

    def small(name, shape, dt=F32):
        t = sb(name, "small", off[0], shape, dt)
        off[0] += -(-4 * int(np.prod(shape)) // 32) * 32
        return t

    ident = small("ident", [P])
    causal = small("causal", [S])
    chunk = small("chunk", [S])
    cols = small("param_cols", [NCOL])
    mod = small("mod_cols", [96])
    gsc = small("gain_cols", [KD])
    trig = small("trig", [2, MT, NROT])
    one = small("one", [1])
    mhalf = small("minus_half", [16])
    sil = small("silu_c", [KD])
    sq = small("sum_of_squares", [32])
    sq2 = small("sum_of_squares2", [32])
    nm = [small(f"neg_max{i}", [8]) for i in range(2)]
    den = [small(f"denominator{i}", [8]) for i in range(2)]
    rden = [small(f"reciprocal{i}", [8]) for i in range(2)]
    lam = small("lam", [4])
    posf = small("pos_f", [2 * MT])
    posi = small("pos_i", [2 * MT], I32)
    wi = small("w_idx", [MT, 16])
    m8 = small("max8", [8])

    proj = sb("proj", "big", 0, [MT, IN1])
    count = sb("count", "h", 30 * KB, [S])
    dilated = sb("dilated", "h", 31 * KB, [S])
    norm_x = [sb(f"norm_x{m}", "big", 8 * KB * m, [D]) for m in range(MT)]
    norm_f = sb("norm_f", "big", 16 * KB, [8, S])
    junk = sb("junk", "h", 24 * KB, [D])
    x_T = sb("x_T", "h", 16 * KB, [KD, S])
    rope_a = [sb("rope_t", "acc", 0, [TILE])] + [sb(f"rope_u{i}", "acc", 4 * KB + 2 * KB * i, [512]) for i in range(2)]
    rope_b = [sb("rope_bt", "acc", 0, [D])] + [sb(f"rope_bu{i}", "big", 48 * KB + 4 * KB * i, [TILE]) for i in range(2)]
    gate_row = sb("gate_row", "big", 50 * KB, [D])
    diag = sb("diag", "acc", 0, [KD, P])
    ones_sq = sb("ones_sq", "big", 63 * KB, [P])
    hid1 = sb("hidden1_T", "big", 0, [DFF1 // P, S])
    hid2 = sb("hidden2_T", "big", 0, [DFF2 // P, S])
    sg1 = sb("silu_gate", "big", 58 * KB, [MT, BANK])
    r2 = [sb(f"relu{i}", "acc", 8 * KB * i, [MT, BANK]) for i in range(2)]
    hsq_b = [sb(f"head_sq_b{m}", "h", 4 * KB * m, [TILE]) for m in range(MT)]
    hsq_a = [sb(f"head_sq_a{i}", "h", 8 * KB + 2 * KB * i, [512]) for i in range(4)]
    mixT = sb("mix_T", "h", 0, [KD, S])
    s_hi = [sb(f"src_hi{i}", "h", 16 * KB + KB * i, [S], F32R) for i in range(4)]
    s_lo = [sb(f"src_lo{i}", "h", 20 * KB + KB * i, [S], F32R) for i in range(4)]
    vec1 = sb("vec_rows1", "h", 0 * KB, [P])
    vec2 = sb("vec_rows2", "h", 1 * KB, [P])
    inv = sb("inv_freq", "h", 2 * KB, [NROT])
    ang = sb("angles", "h", 3 * KB, [MT, NROT])
    rnd = sb("turns", "h", 5 * KB, [MT, NROT])
    angr = sb("reduced", "h", 7 * KB, [2, MT, NROT])
    lamv = sb("lambda_rows", "h", 10 * KB, [4, 64])
    sil_t = sb("silu_tmp", "h", 11 * KB, [KD])
    post_tmp = [sb(f"post_tmp{m}", "big", (24 + 8 * m) * KB, [D]) for m in range(MT)]
    junks = [junk, sb("junk1", "h", 0, [D])]

    ps = nc.alloc_psum_tensor("ps", [P, 8, BANK], F32)

    def bank_free(b, *toks):
        st["bank", b] = list(toks)

    def r32(ap):
        return ap.bitcast(F32)

    issued = [0, 0]

    def fetch(src, view):
        r = issued[0] % RAW
        issued[0] += 1
        need(SP, st.get(("raw", r)))
        dst = raw[r][:, :] if view is None else raw[r][:, 0:view[0] * view[1]].rearrange("p (k n) -> p k n", k=view[0])
        st["landed", r] = [t_raw[r].done(SP.dma_start(dst, src))]
        return r

    def split(r, n=TILE, later=None):
        u = issued[1] % SPLIT
        issued[1] += 1
        need(SCA, st["landed", r], st.get(("split", u)))
        hi = done(SCA, SCA.activation(whi[u][:, 0:n], raw[r][:, 0:n], ACT.Copy))

        def low():
            need(DVE, hi, st["landed", r])
            lo = done(DVE, DVE.tensor_tensor(wlo[u][:, 0:n], raw[r][:, 0:n], r32(whi[u][:, 0:n]), ALU.subtract))
            st["raw", r] = [lo]
            st["halves", u] = [hi, lo]
        if later is None:
            low()
        else:
            later.append(low)
        return u

    def products(dst, lhs, rhs, first, last):
        (ah, al), (bh, bl) = lhs, rhs
        PE.matmul(dst, ah, bh, start=first, stop=False)
        PE.matmul(dst, al, bh, start=False, stop=False)
        return PE.matmul(dst, ah, bl, start=False, stop=last)

    def col_tile(w, row, kt_per, c0, width, later=None):
        rows = w[row:row + kt_per * P, c0 if not isinstance(c0, tuple) else slice(c0[0], c0[0] + width)]
        return split(fetch(rows.rearrange("(k p) n -> p k n", p=P), (kt_per, width)), kt_per * width, later)

    ahead = []
    h_wait = {}
    h_make = []

    def look_ahead(w, c0, tiles=range(3), later=None):
        for j in tiles:
            ahead.append(col_tile(w, 2 * j * P, 2, c0, BANK, later))

    def col_slot(w, row0, nk, c0, width, banks, A, pend=(), lag=3, extra=None, side=None):
        pend = list(pend)
        kt_per = 2 if nk > 1 else 1
        need(PE, *[st.get(("bank", b)) for b in banks])
        ah, al = A
        for j in range(nk // kt_per):
            if h_make and j % 2 == 0:
                h_make.pop(0)()
            u = ahead.pop(0) if ahead else col_tile(w, row0 + j * kt_per * P, kt_per, c0, width)
            need(PE, st["halves", u])
            for kk in range(kt_per):
                k = j * kt_per + kk
                need(PE, h_wait.pop(k, None))
                for m in range(MT):
                    lhs = (ah[:, k, m * P:(m + 1) * P], al[:, k, m * P:(m + 1) * P])
                    rhs = (whi[u][:, kk * width:(kk + 1) * width], wlo[u][:, kk * width:(kk + 1) * width])
                    ins = products(ps[:, banks[m], 0:width], lhs, rhs, k == 0, k == nk - 1)
            st["split", u] = [done(PE, ins)]
            if extra:
                extra(j)
            if j >= lag and pend:
                pend.pop(0)()
            if side:
                side.step()
        st["full", banks[0]] = st["split", u]
        for step in pend:
            step()

    def wait_steps(n):
        for _ in range(n):
            yield

    def ada_half(part, kt, half, first):
        r = fetch(a["w_ada"][0][bass.ds(kt * P, P), part * D + half * TILE:part * D + (half + 1) * TILE], None)
        dst = acc[part % 2][:, half * TILE:(half + 1) * TILE]
        c = sil[:, kt:kt + 1] if isinstance(kt, int) else sil[:, bass.ds(kt, 1)]
        need(DVE, st["landed", r], st["silu"])
        if first:
            need(DVE, st.get(("acc", part % 2)))
            t = done(DVE, DVE.tensor_scalar(dst, raw[r][:, :], c, None, ALU.mult))
        else:
            need(DVE, st["accumulated", half])
            t = done(DVE, DVE.scalar_tensor_tensor(dst, raw[r][:, :], c, dst, ALU.mult, ALU.add))
        st["accumulated", half] = [t]
        st["raw", r] = [t]

    def ada_finish(part, bank, behind=0):
        need(PE, st["accumulated", 0], st["accumulated", 1], st.get(("bank", bank)), st["one"])
        for k in range(KD):
            ins = PE.matmul(ps[:, bank, k:k + 1], acc[part % 2][:, k * P:(k + 1) * P], one[:, :], start=True, stop=True)
        t = done(PE, ins)
        st["acc", part % 2] = [t]
        yield from wait_steps(behind)
        need(DVE, t, st["cols"])
        c = done(DVE, DVE.tensor_tensor(mod[:, part * 16:part * 16 + 16], ps[:, bank, 0:KD],
                                        cols[:, C_BADA + part * 16:C_BADA + part * 16 + 16], ALU.add))
        bank_free(bank, c)
        st["mod", part] = [c]

    def row_ahead(w, n=3):
        for j in range(n):
            ahead.append(split(fetch(w[j // 2 * P:(j // 2 + 1) * P, j % 2 * TILE:(j % 2 + 1) * TILE], None)))

    def row_stage(w, srcT, nk, ready, ada=None):
        per = 4
        y = {}

        def body(i):
            end = isinstance(i, int) and i == nk // per - 1
            held = []
            if isinstance(i, int) and i < 2:
                need(SCA, ready[0:1] if i == 0 else ready[1:])
                need(DVE, ready[0:1] if i == 0 else ready[1:])
            for q in range(per):
                kt = i * per + q
                src = srcT[:, kt, :] if isinstance(kt, int) else srcT[:, bass.ds(kt, 1), :].rearrange("p o n -> p (o n)")
                need(SCA, st.get(("src", q)))
                hi = done(SCA, SCA.activation(s_hi[q][:, :], src, ACT.Copy))
                need(DVE, hi)
                lo = done(DVE, DVE.tensor_tensor(s_lo[q][:, :], src, r32(s_hi[q][:, :]), ALU.subtract))
                for half in range(2):
                    u = ahead.pop(0) if ahead else split(fetch(w[bass.ds(kt * P, P), half * TILE:(half + 1) * TILE], None))
                    need(PE, st["halves", u], hi, lo)
                    first = isinstance(i, int) and i == 0 and q == 0
                    last = end and q == per - 1
                    if first:
                        need(PE, *[st.get(("bank", 4 * m + 2 * half + n)) for m in range(MT) for n in range(2)])

                    def one(ms, q=q, u=u, half=half, first=first, last=last):
                        for m in ms:
                            for n in range(2):
                                lhs = (s_hi[q][:, m * P:(m + 1) * P], s_lo[q][:, m * P:(m + 1) * P])
                                rhs = (whi[u][:, n * BANK:(n + 1) * BANK], wlo[u][:, n * BANK:(n + 1) * BANK])
                                ins = products(ps[:, 4 * m + 2 * half + n, :], lhs, rhs, first, last)
                        return done(PE, ins)
                    if end and q >= per - 2:
                        y[0] = one((0,))
                        held.append((u, q, one))
                    else:
                        st["split", u] = [one(range(MT))]
                    if ada is not None:
                        ada_half(ada, kt, half, isinstance(kt, int) and kt == 0)
                if not held:
                    st["src", q] = st["split", u]
            for u, q, one in held:
                y[1] = one((1,))
                st["split", u] = st["src", q] = [y[1]]

        repeat(nk // per, body, peel=2, tail=1)
        return y

    def rsqrt_cols(dst, src, n, scale):
        t = done(POOL, POOL.tensor_scalar(dst, src, scale, EPS, ALU.mult, ALU.add))
        need(POOL, t)
        return done(POOL, POOL.tensor_tensor(dst, dst, mhalf[:, 0:n], ALU.pow))

    def row_rsqrt(src, slot, *ready, junk_ap=None):
        n = src.shape[-1] if len(src.shape) == 2 else int(np.prod(src.shape[1:]))
        need(SCA, ta.last(), *ready)
        t = done(SCA, SCA.activation(junk_ap, src, ACT.Square, accum_out=sq[:, slot:slot + 1]))
        need(POOL, t, st["mhalf"])
        return rsqrt_cols(sq2[:, slot:slot + 1], sq[:, slot:slot + 1], 1, 1.0 / n)

    def barrier():
        toks = [t.last() for t in (tp, tv, ta, tg)]
        for eng in (PE, DVE, SCA, POOL):
            need(eng, toks)
        for b in range(8):
            bank_free(b)
        return toks

    def norm_rows(src, xn, slot, ready):
        for m in range(MT):
            st["rs", m] = [row_rsqrt(src[:, m, :], slot + m, *ready[m], junk_ap=xn[m])]
            yield
        for m in range(MT):
            need(DVE, st["rs", m])
            st["nx", m] = [done(DVE, DVE.tensor_scalar(xn[m], src[:, m, :], sq2[:, slot + m:slot + m + 1], None, ALU.mult))]
            yield

    def norm_to_h(xn, gain, dst):
        hi_t, lo_t = dst
        for n in range(0, KD, 4):
            bs = [n // 2, n // 2 + 1]
            need(PE, st["nx", 0], st["nx", 1], st["ident"], *[st.get(("bank", b)) for b in bs])
            st["nt", n] = [transposes(bs[0], [(k * S + m * P, xn[m][:, (n + k) * P:(n + k + 1) * P]) for k in range(4) for m in range(MT)])]
        yield
        for b in range(8):
            ks = [(2 * b + k, ps[:, b, k * S:(k + 1) * S]) for k in range(2)]
            need(SCA, st["nt", 4 * (b // 2)])
            for kt, s_ in ks:
                hi = done(SCA, SCA.activation(hi_t[:, kt, :], s_, ACT.Copy, scale=gain[:, kt:kt + 1]))
            need(DVE, hi, st["nt", 4 * (b // 2)])
            for kt, s_ in ks:
                lo = done(DVE, DVE.scalar_tensor_tensor(lo_t[:, kt, :], s_, gain[:, kt:kt + 1], r32(hi_t[:, kt, :]), ALU.mult, ALU.subtract))
            for kt, s_ in ks:
                h_wait[kt] = [hi, lo]
            bank_free(b, hi, lo)
            yield

    def norm(src, gain, shift, ready, next_w, c0=(0,), keep=(0, 1), before_h=None):
        xn = [norm_x[m][:, :] for m in range(MT)]
        low_parts = []
        look_ahead(next_w, c0, range(2), low_parts)
        for m in range(MT):
            st["rs", m] = [row_rsqrt(src[:, m, :], m, *ready[m], junk_ap=xn[m])]
        for m in range(MT):
            need(DVE, st["rs", m])
            need(SCA, st["rs", m])
            st["nx", m] = [done(DVE, DVE.tensor_scalar(xn[m][:, 0:TILE], src[:, m, 0:TILE], sq2[:, m:m + 1], None, ALU.mult)),
                           done(SCA, SCA.activation(xn[m][:, TILE:], src[:, m, TILE:], ACT.Copy, scale=sq2[:, m:m + 1]))]
            while low_parts:
                low_parts.pop(0)()
        look_ahead(next_w, c0, (2,))
        if before_h:
            before_h()
        free = [b for b in range(8) if b not in keep]
        pairs = [(free[0], free[1]), (free[2], free[3]), (free[4], free[5]), (free[0], free[1])]

        def tr(g, m):
            need(PE, st["nx", m], *[st.get(("bank", b)) for b in pairs[g]])
            for k in range(4):
                ins = PE.transpose(ps[:, pairs[g][k // 2], (k % 2) * S + m * P:(k % 2) * S + (m + 1) * P],
                                   xn[m][:, (4 * g + k) * P:(4 * g + k + 1) * P], ident[:, :])
            st["nt", g] = [done(PE, ins)]

        for m in range(MT):
            for g in range(3):
                tr(g, m)
        for g in range(4):
            h_make.append(lambda g=g: to_halves(g, pairs[g], gain, shift))
        h_make.pop(0)()
        tr(3, 0)
        tr(3, 1)

    def to_halves(g, pair, gain, shift):
        for n, b in enumerate(pair or (0, 1)):
            ks = [(4 * g + 2 * n + k, ps[:, b, k * S:(k + 1) * S] if pair else x_T[:, 4 * g + 2 * n + k, :]) for k in range(2)]
            if shift is None:
                need(SCA, st["nt", g])
                for kt, s_ in ks:
                    hi = done(SCA, SCA.activation(h_hi[:, kt, :], s_, ACT.Copy, scale=gain[:, kt:kt + 1]))
                need(DVE, hi, st["nt", g])
                for kt, s_ in ks:
                    lo = done(DVE, DVE.scalar_tensor_tensor(h_lo[:, kt, :], s_, gain[:, kt:kt + 1], r32(h_hi[:, kt, :]), ALU.mult, ALU.subtract))
                for kt, s_ in ks:
                    h_wait[kt] = [hi, lo]
                bank_free(b, hi, lo)
            else:
                need(SCA, st["nt", g])
                for kt, s_ in ks:
                    hi = done(SCA, SCA.activation(h_hi[:, kt, :], s_, ACT.Identity, scale=gain[:, kt:kt + 1], bias=shift[:, kt:kt + 1]))
                need(DVE, hi if pair else None, st["nt", g])
                for kt, s_ in ks:
                    f = done(DVE, DVE.tensor_scalar(norm_f[:, kt % 8, :], s_, gain[:, kt:kt + 1], shift[:, kt:kt + 1], ALU.mult, ALU.add))
                if pair:
                    bank_free(b, f)
                need(DVE, hi, f)
                kt = ks[0][0]
                lo = done(DVE, DVE.tensor_tensor(h_lo[:, kt:kt + 2, :], norm_f[:, kt % 8:kt % 8 + 2, :], r32(h_hi[:, kt:kt + 2, :]), ALU.subtract))
                for kt, s_ in ks:
                    h_wait[kt] = [hi, lo]

    def run(gen):
        for _ in gen:
            pass

    def copy_post(banks, dst, width, key=None):
        def step():
            need(SCA, st["full", banks[0]])
            t = done(SCA, SCA.activation(dst, ps[:, banks[0]:banks[1] + 1, 0:width], ACT.Copy))
            st["posted", key] = [t]
            for b in banks:
                bank_free(b, t)
        return [step]

    def rope(src, dst, heads, half, rot, m, tmp, *ready):
        need(DVE, *ready)
        r0 = rot[0]
        cos = trig[:, 0, m, r0:r0 + half]
        sin = trig[:, 1, m, r0:r0 + half]
        s4 = src.rearrange("p h (a b) -> p h a b", a=2)
        d4 = dst.rearrange("p h (a b) -> p h a b", a=2)
        t4 = tmp[0][:, 0:heads * 2 * half].rearrange("p (h a b) -> p h a b", a=2, b=half)
        u = [tmp[1 + i][:, 0:heads * half].rearrange("p (h b) -> p h b", b=half) for i in range(2)]
        need(DVE, st.get("rope"))
        DVE.tensor_tensor(t4, s4, cos.unsqueeze(1).unsqueeze(1).to_broadcast([P, heads, 2, half]), ALU.mult)
        if heads * half > 512:
            yield
        DVE.tensor_tensor(u[0], s4[:, :, 1, :], sin.unsqueeze(1).to_broadcast([P, heads, half]), ALU.mult)
        t = done(DVE, DVE.tensor_tensor(u[1], s4[:, :, 0, :], sin.unsqueeze(1).to_broadcast([P, heads, half]), ALU.mult))
        yield
        need(DVE, t)
        DVE.tensor_tensor(d4[:, :, 0, :], t4[:, :, 0, :], u[0], ALU.subtract)
        t = done(DVE, DVE.tensor_tensor(d4[:, :, 1, :], t4[:, :, 1, :], u[1], ALU.add))
        st["rope"] = [t]
        yield

    def transposes(banks, items):
        for col, src in items:
            ins = PE.transpose(ps[:, banks + col // BANK, col % BANK:col % BANK + P], src, ident[:, :])
        return done(PE, ins)

    def attention(p, prep, units, vs, outs, scale, masks, buf, cnt=None, diff=False, nkts=(1, 2)):
        QT, KT, sc0, sc1 = buf
        b0 = 4 * p
        tok = yield from prep(p, QT, KT)
        n_out = 2 if diff else 4
        step = 2 if diff else 1
        whole = nkts[0] == 2
        need(PE, tok)
        ts = range(MT)
        pair = [ps[:, b0:b0 + 2, :], ps[:, b0 + 2:b0 + 4, :]]
        sc, s_done, e, rc, ng = {}, {}, {}, {}, {}
        for t in ts:
            nk = nkts[t] * P
            for i in range(4):
                ins = units[i](t, pair[t][:, i // 2, (i % 2) * nk:(i % 2 + 1) * nk], nk)
            s_done[t] = done(PE, ins)
        yield
        yield
        def scores(t):
            nk = nkts[t] * P
            need(DVE, s_done[t])
            s_ps = pair[t][:, :, 0:2 * nk].rearrange("p b (u n) -> p b u n", u=2)
            flat = (sc0, sc1)[t][:, 0:4 * nk]
            sc[t] = flat.rearrange("p (u n) -> p u n", u=4)
            sc4 = flat.rearrange("p (b u n) -> p b u n", b=2, u=2)
            mk = masks(t)
            if mk is None:
                mt = done(DVE, DVE.tensor_copy(sc4, s_ps))
            else:
                mt = done(DVE, DVE.tensor_tensor(sc4, s_ps, mk.unsqueeze(1).unsqueeze(1).to_broadcast([P, 2, 2, nk]), ALU.add))
            need(DVE, mt)
            mx = done(DVE, DVE.tensor_reduce(nm[p][:, 4 * t:4 * t + 4], sc[t], AX, ALU.max))
            need(DVE, mx)
            ng[t] = done(DVE, DVE.tensor_scalar(nm[p][:, 4 * t:4 * t + 4], nm[p][:, 4 * t:4 * t + 4], -scale, None, ALU.mult))

        def exps(t):
            need(SCA, ng[t])
            for i in range(4):
                e[t] = done(SCA, SCA.activation(sc[t][:, i, :], sc[t][:, i, :], ACT.Exp, bias=nm[p][:, 4 * t + i:4 * t + i + 1],
                                                scale=scale, accum_out=den[p][:, 4 * t + i:4 * t + i + 1]))
        scores(0)
        yield
        scores(1)
        exps(0)
        yield
        exps(1)
        yield
        for t in ts:
            nk = nkts[t] * P
            d, r = den[p][:, 4 * t:4 * t + 4], rden[p][:, 4 * t:4 * t + 4]
            need(DVE, e[t])
            if cnt is not None:
                w = done(DVE, DVE.tensor_tensor(sc[t], sc[t], cnt(t).unsqueeze(1).to_broadcast([P, 4, nk]), ALU.mult))
                need(DVE, w)
                e[t] = done(DVE, DVE.tensor_reduce(d, sc[t], AX, ALU.add))
                need(DVE, e[t])
            rc[t] = done(DVE, DVE.reciprocal(r, d))
            if diff:
                need(DVE, rc[t])
                rv = r.rearrange("p (h m) -> p h m", m=2)
                rl = done(DVE, DVE.tensor_scalar(rv[:, :, 1], rv[:, :, 1], lam[:, 3:4], None, ALU.mult))
                need(DVE, rl)
                w = done(DVE, DVE.tensor_tensor(sc[t], sc[t], r.unsqueeze(2).to_broadcast([P, 4, nk]), ALU.mult))
                need(DVE, w)
                s4 = sc[t].rearrange("p (h m) n -> p h m n", m=2)
                e[t] = done(DVE, DVE.tensor_tensor(s4[:, :, 0, :], s4[:, :, 0, :], s4[:, :, 1, :], ALU.add))
        yield
        pv, pt, pe_ = {}, {}, {}
        for t in ts:
            need(PE, e[t])
            for kt in range(nkts[t]):
                for i in range(n_out):
                    ins = PE.transpose(pair[t][:, kt, i * P:(i + 1) * P], sc[t][:, i * step, kt * P:(kt + 1) * P], ident[:, :])
            pt[t] = done(PE, ins)
        yield
        yield
        for t in ts:
            need(SCA, pt[t])
            pv[t] = (KT, QT)[t][:, :].rearrange("p (k n) -> p k n", k=2)[:, 0:nkts[t], 0:n_out * P]
            pe_[t] = done(SCA, SCA.activation(pv[t], pair[t][:, 0:nkts[t], 0:n_out * P], ACT.Copy))
        o = {}
        for t in ts:
            need(PE, pe_[t])
            for i in range(n_out):
                for kt in range(nkts[t]):
                    ins = PE.matmul(pair[t][:, 0, i * P:(i + 1) * P], pv[t][:, kt, i * P:(i + 1) * P], vs(i, kt),
                                    start=kt == 0, stop=kt == nkts[t] - 1)
            o[t] = done(PE, ins)
        yield
        yield
        for t in ts:
            o_ps = pair[t][:, 0, 0:n_out * P].rearrange("p (h n) -> p h n", h=n_out)
            if diff:
                need(SCA, o[t])
                f = done(SCA, SCA.activation(outs(t), o_ps, ACT.Copy))
            else:
                need(DVE, o[t], rc[t])
                f = done(DVE, DVE.tensor_tensor(outs(t), o_ps, rden[p][:, 4 * t:4 * t + 4].unsqueeze(2).to_broadcast([P, 4, P]), ALU.mult))
        st["set", p] = [f]

    def run_two(gens):
        live = {}
        gens = list(gens)
        turn = 0
        while gens or live:
            for p in range(2):
                if p not in live and gens and gens[0][0] == p:
                    live[p] = gens.pop(0)[1]
            if turn in live:
                try:
                    next(live[turn])
                except StopIteration:
                    del live[turn]
            turn ^= 1

    def qk_prep(q_items, k_items, extra=None):
        def prep(p, QT, KT):
            need(PE, st.get(("set", p)))
            tq = transposes(4 * p, q_items)
            tk = transposes(4 * p + 2, k_items)
            yield
            yield
            need(SCA, tq)
            eq = done(SCA, SCA.activation(QT[:, :].rearrange("p (b n) -> p b n", b=2), ps[:, 4 * p:4 * p + 2, :], ACT.Copy))
            need(SCA, tk)
            ek = done(SCA, SCA.activation(KT[:, :].rearrange("p (b n) -> p b n", b=2), ps[:, 4 * p + 2:4 * p + 4, :], ACT.Copy))
            toks = [eq, ek]
            if extra:
                need(PE, eq)
                toks += extra(p)
            return toks
        return prep

    def head_norm(view, gain_row, factor, c0, tmp, ready):
        n = view.shape[1]
        c = slice(c0, c0 + n)
        need(SCA, ready())
        sqv = tmp.rearrange("p (h n) -> p h n", h=n)
        t = done(SCA, SCA.activation(sqv, view, ACT.Square))
        yield
        need(DVE, t)
        t = done(DVE, DVE.tensor_reduce(sq[:, c], sqv, AX, ALU.add))
        need(POOL, t)
        g = rsqrt_cols(sq2[:, c], sq[:, c], n, 1.0 / P)
        yield
        yield
        need(DVE, g)
        t = done(DVE, DVE.tensor_tensor(view, view, sq2[:, c].unsqueeze(2).to_broadcast([P, n, P]), ALU.mult))
        yield
        need(DVE, t)
        t = done(DVE, DVE.scalar_tensor_tensor(view, view, factor, gain_row.unsqueeze(1).to_broadcast([P, n, P]), ALU.mult, ALU.mult))
        yield

    def weave(*gens):
        gens = list(gens)
        while gens:
            for g_ in list(gens):
                try:
                    next(g_)
                except StopIteration:
                    gens.remove(g_)
            yield

    def chain(*gens):
        for g_ in gens:
            yield from g_

    def gate_diag(part, gcol):
        need(DVE, st["mod", part], st["cols"], st.get("gate"))
        g = done(DVE, DVE.tensor_tensor(gsc[:, :], mod[:, part * 16:part * 16 + 16], cols[:, gcol:gcol + 16], ALU.mult))
        yield
        need(DVE, g)
        st["diag"] = [done(DVE, DVE.tensor_tensor(diag[:, :, :], ident[:, :].unsqueeze(1).to_broadcast([P, KD, P]),
                                                  gsc[:, :].unsqueeze(2).to_broadcast([P, KD, P]), ALU.mult))]
        yield

    def gate_bcast(banks, behind):
        k = len(banks)
        for n in range(0, 4, k):
            need(PE, st["diag"], st["ones_sq"], *[st.get(("bank", b)) for b in banks])
            for i, b in enumerate(banks):
                ins = PE.matmul(ps[:, b, :], ones_sq[:, :], diag[:, 4 * (n + i):4 * (n + i) + 4, :].rearrange("p k n -> p (k n)"), start=True, stop=True)
            t = done(PE, ins)
            yield from wait_steps(behind)
            need(SCA, t)
            e = done(SCA, SCA.activation(gate_row[:, n * BANK:(n + k) * BANK].rearrange("p (b n) -> p b n", b=k),
                                         ps[:, banks[0]:banks[0] + k, :], ACT.Copy))
            for b in banks:
                bank_free(b, e)
        st["gate"] = [t]

    def transposed_mix(srcs, *ready):
        need(PE, *ready)
        last = []
        for g in range(4):
            b = (0, 4, 2, 6)[g]
            t = transposes(b, [(k * S + m * P, srcs(4 * g + k, m)) for k in range(4) for m in range(MT)])
            eng = (SCA, DVE)[g % 2]
            need(eng, t)
            dst = mixT[:, 4 * g:4 * g + 4, :].rearrange("p (b k) n -> p b (k n)", b=2)
            s_ = ps[:, b:b + 2, :]
            c = done(eng, eng.activation(dst, s_, ACT.Copy) if eng is SCA else eng.tensor_copy(dst, s_))
            last.append(c)
            bank_free(b, c)
            bank_free(b + 1, c)
        return last

    gout = [sb("g_out_rows", "big", 62 * KB, [P]), sb("g_sub_rows", "big", 62 * KB + 512, [P])]
    q = SCA
    par = []

    def pload(dst, src, eng=None):
        par.append(t_par.done((eng or q).dma_start(dst, src)))

    z = done(POOL, POOL.memset(vec2[:, :], 0.0))
    need(q, z)
    pload(vec1[0:16, :], a["c"].rearrange("o (k n) -> (o k) n", n=P))
    pload(vec1[16:112, :], a["b_ada"].rearrange("o (k n) -> (o k) n", n=P))
    pload(vec1[112:128, :], a["g_post_attn"].rearrange("o (k n) -> (o k) n", n=P))
    row = 0
    for name in ("g_pre_attn", "g_pre_ffn", "g_mix_2", "g_cross_2", "g_mem_2", "g_mlp_2", "g_cq_2", "g_ckv_2", "g_post_ffn"):
        n = a[name].shape[1] // P
        pload(vec2[row:row + n, :], a[name].rearrange("o (k n) -> (o k) n", n=P))
        row += n
    assert 128 + row == NCOL
    pload(ident[:, :], a["k_ident"])
    pload(causal[:, :], a["k_causal"])
    pload(chunk[:, :], a["k_chunk"])
    pload(inv[:, :], a["k_inv"].to_broadcast([P, NROT]))
    for i, n in enumerate(("positions", "positions_2")):
        for m in range(MT):
            pload(posi[:, 2 * i + m:2 * i + m + 1], a[n].rearrange("o (m p) -> m p o", p=P)[m])
    for i, n in enumerate(("lambda_q1", "lambda_k1", "lambda_q2", "lambda_k2")):
        pload(lamv[:, i, :], a[n].to_broadcast([P, 64]))
    memt = sb("mem_rows", "h", 16 * KB, [MT, D])
    m_in = t_mem.done(q.dma_start(memt[:, :, :], a["mem_2"][0].rearrange("(m p) d -> p m d", p=P)))
    x_in = t_x.done(q.dma_start(x[:, :, :], a["x"][0].rearrange("(m p) d -> p m d", p=P)))
    par_tok = [par[-1]]

    ONES = done(DVE, DVE.memset(one[:, :], 1.0))
    MH = done(POOL, POOL.memset(mhalf[:, :], -0.5))
    st["one"], st["mhalf"], st["ident"] = [ONES], [MH], par_tok

    need(PE, par_tok, z)
    t = transposes(0, [(0, vec1[:, :]), (P, vec2[:, :])])
    need(DVE, t)
    st["cols"] = [done(DVE, DVE.tensor_copy(cols[:, 0:NCOL], ps[:, 0, 0:NCOL]))]
    need(SCA, st["cols"])
    t = done(SCA, SCA.activation(sil_t[:, :], cols[:, 0:16], ACT.Exp, scale=-1.0))
    need(DVE, t)
    t = done(DVE, DVE.tensor_scalar(sil_t[:, :], sil_t[:, :], 1.0, None, ALU.add))
    need(DVE, t)
    t = done(DVE, DVE.reciprocal(sil_t[:, :], sil_t[:, :]))
    need(DVE, t)
    st["silu"] = [done(DVE, DVE.tensor_tensor(sil[:, :], sil_t[:, :], cols[:, 0:16], ALU.mult))]
    need(DVE, par_tok)
    t = done(DVE, DVE.tensor_tensor(lamv[:, 0:4:2, :], lamv[:, 0:4:2, :], lamv[:, 1:4:2, :], ALU.mult))
    need(DVE, t)
    t = done(DVE, DVE.tensor_reduce(lam[:, 0:2], lamv[:, 0:4:2, :], AX, ALU.add))
    need(SCA, t)
    t = done(SCA, SCA.activation(lam[:, 0:2], lam[:, 0:2], ACT.Exp))
    need(DVE, t)
    t = done(DVE, DVE.tensor_tensor(lam[:, 2:3], lam[:, 1:2], lam[:, 0:1], ALU.subtract))
    need(DVE, t)
    t = done(DVE, DVE.tensor_scalar(lam[:, 3:4], lam[:, 2:3], -(0.8 - 0.6), None, ALU.add))
    t = done(DVE, DVE.tensor_copy(posf[:, :], posi[:, :]))
    need(DVE, t)
    for m in range(MT):
        DVE.tensor_scalar(ang[:, m, 0:NROT1], inv[:, 0:NROT1], posf[:, m:m + 1], None, ALU.mult)
        t = done(DVE, DVE.tensor_scalar(ang[:, m, NROT1:], inv[:, NROT1:], posf[:, 2 + m:3 + m], None, ALU.mult))
    need(DVE, t)
    for c in range(2):
        t = done(DVE, DVE.tensor_scalar(rnd[:, :, :], ang[:, :, :], 1 / PI2, 0.25 * (1 - c), ALU.mult, ALU.add))
        need(DVE, t)
        t = done(DVE, DVE.tensor_scalar(rnd[:, :, :], rnd[:, :, :], MAGIC, None, ALU.add))
        need(DVE, t)
        t = done(DVE, DVE.tensor_scalar(rnd[:, :, :], rnd[:, :, :], -MAGIC, None, ALU.add))
        src = ang[:, :, :]
        for piece in (PI_A, PI_B, PI_C):
            need(DVE, t)
            t = done(DVE, DVE.scalar_tensor_tensor(angr[:, c, :, :], rnd[:, :, :], -piece, src, ALU.mult, ALU.add))
            src = angr[:, c, :, :]
        if c == 0:
            need(DVE, t)
            t = done(DVE, DVE.tensor_scalar(src, src, np.pi / 2, None, ALU.add))
        need(DVE, t)
        t = done(DVE, DVE.tensor_scalar(src, src, 3.1415925, -3.1415925, ALU.min, ALU.max))
        need(DVE, t)
    need(SCA, t)
    st["trig"] = [done(SCA, SCA.activation(trig[:, :, :, :], angr[:, :, :, :], ACT.Sin))]

    ada_list = [(part, kt, half) for part in range(5) for kt in range(KD) for half in range(2)]

    def ada_loop(part):
        def body(i):
            for q_ in range(4):
                for half in range(2):
                    ada_half(part, i * 4 + q_, half, isinstance(i, int) and i == 0 and q_ == 0)
        repeat(4, body)

    def ada_next(n):
        for _ in range(n):
            part, kt, half = ada_list.pop(0)
            ada_half(part, kt, half, kt == 0)

    ada_loop(1)
    del ada_list[2 * KD:4 * KD]
    mem_hi = sb("mem_hi", "big", 24 * KB, [KD, S], F32R)
    mem_lo = sb("mem_lo", "big", 40 * KB, [KD, S], F32R)
    mem_n = [memt[:, m, :] for m in range(MT)]
    x_n = [norm_x[m][:, :] for m in range(MT)]
    junk_m = sb("junk_m", "big", 16 * KB, [D])

    def memory_norm():
        for m in range(MT):
            st["ms", m] = [row_rsqrt(mem_n[m], 2 + m, m_in, junk_ap=junk_m[:, :])]
        yield
        for m in range(MT):
            need(DVE, st["ms", m])
            st["nx", m] = [done(DVE, DVE.tensor_scalar(mem_n[m], mem_n[m], sq2[:, 2 + m:3 + m], None, ALU.mult))]
            yield
        yield from norm_to_h(mem_n, cols[:, C_GMEM:C_GMEM + 16], dst=(mem_hi, mem_lo))
        yield from norm_rows(x, x_n, 0, [[x_in], [x_in]])

    for _ in memory_norm():
        ada_next(1)

    def modulated_gain(part_scale, gcol):
        need(DVE, st["mod", part_scale])
        return done(DVE, DVE.scalar_tensor_tensor(gsc[:, :], mod[:, part_scale * 16:part_scale * 16 + 16], 1.0,
                                                  cols[:, gcol:gcol + 16], ALU.add, ALU.mult))

    def first_transposes():
        for g in range(4):
            bs = (4, 5) if g % 2 == 0 else (6, 7)
            need(PE, st["nx", 0], st["nx", 1], *[st.get(("bank", b)) for b in bs])
            t = transposes(bs[0], [(k * S + m * P, x_n[m][:, (4 * g + k) * P:(4 * g + k + 1) * P]) for k in range(4) for m in range(MT)])
            yield
            yield
            need(SCA, t)
            t = done(SCA, SCA.activation(x_T[:, 4 * g:4 * g + 4, :].rearrange("p (b k) n -> p b (k n)", b=2), ps[:, bs[0]:bs[1] + 1, :], ACT.Copy))
            bank_free(bs[0], t)
            bank_free(bs[1], t)
            st["nt", g] = [t]

    kx = sb("cross_k", "big", 56 * KB, [MT, 512])
    need(SCA, tp.last(), tv.last())
    side = Side(ada_finish(1, 7, 4), first_transposes())
    A_m = (mem_hi, mem_lo)
    n_left = len(ada_list) - 3 * 2 * KD

    def part_0(slot):
        def f(j):
            while len(ada_list) > 3 * 2 * KD and (8 * slot + j + 1) * n_left > 15 * (3 * 2 * KD + n_left - len(ada_list)):
                ada_next(1)
        return f
    col_slot(a["w_k_cross_2"][0], 0, KD, (0,), 512, (0, 1), A_m, side=side, extra=part_0(0))
    col_slot(a["w_v_cross_2"][0], 0, KD, (0,), 512, (2, 3), A_m, copy_post((0, 1), kx[:, :, :], 512), side=side, extra=part_0(1))
    side.finish()
    need(PE, ta.last())
    t = transposes(4, [(hh * S + m * P, kx[:, m, hh * P:(hh + 1) * P]) for hh in range(4) for m in range(MT)])
    need(DVE, t)
    kxt = done(DVE, DVE.tensor_copy(kxT[:, :, :].rearrange("p (b k) n -> p b (k n)", b=2), ps[:, 4:6, :]))
    bank_free(4, kxt)
    bank_free(5, kxt)
    look_ahead(a["w_in"][0], (3072,))
    run(ada_finish(0, 6))
    t = modulated_gain(1, C_GPRE)
    need(DVE, t)
    need(SCA, t, st["trig"])
    for g in range(4):
        h_make.append(lambda g=g: to_halves(g, None, gsc, mod[:, 0:16]))
    h_make.pop(0)()
    for s_ in copy_post((2, 3), vx[:, :, :], 512):
        s_()
    A_h = (h_hi, h_lo)

    work1 = [[sb(f"w1_{n}{p}", reg, (o0 + o) * KB, [w]) for n, o, w in (("qT", 0, TILE), ("kT", 4, TILE), ("s0", 8, 512), ("s1", 10, TILE))]
             for p, (reg, o0) in enumerate((("h", 16), ("big", 48)))]
    qkA = [proj[:, m, 0:2048].rearrange("p (h n) -> p h n", n=128) for m in range(MT)]
    qkB = [proj[:, m, 3072:5120].rearrange("p (h n) -> p h n", n=64) for m in range(MT)]

    def unit(pairs):
        def f(t, dst, nk):
            for n, (l, r) in enumerate(pairs):
                ins = PE.matmul(dst, l(t), r(nk), start=n == 0, stop=n == len(pairs) - 1)
            return ins
        return f

    def groupA(g):
        p = g % 2
        QT, KT = (w[:, :].rearrange("p (u n) -> p u n", u=4) for w in work1[p][:2])
        items = lambda base: [(i * S + m * P, proj[:, m, base + (4 * g + i) * P:base + (4 * g + i + 1) * P]) for i in range(4) for m in range(MT)]
        units = [unit([(lambda t, i=i: QT[:, i, t * P:(t + 1) * P], lambda nk, i=i: KT[:, i, 0:nk])]) for i in range(4)]
        return p, attention(p, qk_prep(items(0), items(1024)), units,
                            lambda i, kt: proj[:, kt, 2048 + (4 * g + i) * P:2048 + (4 * g + i + 1) * P],
                            lambda t: proj[:, t, 512 * g:512 * g + 512].rearrange("p (h n) -> p h n", h=4),
                            128 ** -0.5, lambda t: dilated[:, P:S] if t == 0 else dilated[:, :], work1[p],
                            cnt=lambda t: count[:, P:S] if t == 0 else count[:, :])

    def mix_col(k):
        return k * P if k < 8 else 3072 + 512 * (k % 2) + P * ((k - 8) // 2)

    def groupB(g):
        p = 1
        QT, KT = (w[:, :].rearrange("p (u n) -> p u n", u=4) for w in work1[p][:2])
        items = lambda base: [(mu * S + m * P, proj[:, m, base + 512 * mu + P * g:base + 512 * mu + P * (g + 1)]) for mu in range(2) for m in range(MT)]
        units = []
        for e in range(2):
            for mu in range(2):
                units.append(unit([(lambda t, e=e, mu=mu: QT[64 * e:64 * e + 64, mu, t * P:(t + 1) * P],
                                                    lambda nk, e=e, mu=mu: KT[64 * e:64 * e + 64, mu, 0:nk])]))
        return p, attention(p, qk_prep(items(3072), items(4096)), units,
                            lambda i, kt: proj[:, kt, 5120 + (2 * g + i) * P:5120 + (2 * g + i + 1) * P],
                            lambda t: proj[:, t, 3072:4096].rearrange("p (e n) -> p e n", e=2)[:, :, P * g:P * (g + 1)],
                            64 ** -0.5, lambda t: causal[:, P:S] if t == 0 else causal[:, :], work1[p], diff=True)

    def slots(w, starts, dst, side=None, extra=None, first_posts=()):
        posts = list(first_posts)
        for n, c0 in enumerate(starts):
            width = min(512, w.shape[1] - c0)
            b = (0, 1) if n % 2 == 0 else (2, 3)
            col_slot(w, 0, KD, (c0,), width, b, A_h, posts, side=side, extra=(lambda j, n=n: extra(8 * n + j)) if extra else None)
            posts = copy_post(b, dst[:, :, c0:c0 + width], width, c0)
        return posts

    posts = slots(a["w_in"][0], range(3072, 5120, 512), proj, extra=lambda j: ada_next(1))

    def ropes_b():
        need(DVE, ta.last())
        for m in range(MT):
            yield from rope(qkB[m], qkB[m], 32, 32, R_B, m, rope_b)
        need(PE, st["rope"])
        need(SCA, st["rope"])

    st["set", 0] = st["set", 1] = []
    need(DVE, st["trig"])
    def ropes_a(c0):
        while ("posted", c0 + 512) not in st:
            yield
        need(DVE, st["posted", c0], st["posted", c0 + 512])
        for m in range(MT):
            v = proj[:, m, c0:c0 + TILE].rearrange("p (h n) -> p h n", n=P)
            yield from rope(v, v, 8, 64, R_A, m, rope_a)
        need(PE, st["rope"])
        st["rotated", c0] = st["rope"]

    side = Side(wait_steps(1), ada_finish(2, 7, 4), ropes_b(), *[groupB(g)[1] for g in range(3)],
                ropes_a(0), ropes_a(1024), groupB(3)[1])
    posts = slots(a["w_in"][0], [5120, 5632] + list(range(0, 3072, 512)), proj, side=side, first_posts=posts,
                  extra=lambda j: ada_next(1) if j % 2 else None)
    for s_ in posts:
        s_()

    need(q, tp.last(), tv.last())
    for n_, (dst_, src_) in enumerate(((count, "k_count"), (dilated, "k_dilated"), (gout[0], "g_out_a"), (gout[1], "g_subln_b"))):
        v = a[src_] if n_ < 2 else a[src_].to_broadcast([P, P])
        late = t_late.done(q.dma_start(dst_[:, :], v))
    need(SCA, tp.last(), tv.last())
    need(DVE, tp.last(), ta.last())
    st["ones_sq"] = [done(DVE, DVE.memset(ones_sq[:, :], 1.0))]
    heads = lambda m, c0, n: proj[:, m, c0:c0 + n * P].rearrange("p (h n) -> p h n", h=n)

    def norm_b():
        while "diag" not in st:
            yield
        need(DVE, late)
        for m in range(MT):
            yield from head_norm(heads(m, 3072, 8), gout[1][:, :], 1.0 - (0.8 - 0.6), 16 + 8 * m, hsq_b[m][:, :], lambda: [ta.last(), tv.last()])

    def norm_a(g, m):
        yield from head_norm(heads(m, 512 * g, 4), gout[0][:, :], 1.0, 4 * (2 * g + m), hsq_a[2 * g + m][:, :], lambda: st["out", g])

    def rest_ada():
        while len(ada_list) > 2 * KD:
            ada_next(1)
            yield
        yield from ada_finish(3, 3)

    def dilated_group(g):
        while ("rotated", 1024) not in st:
            yield
        need(DVE, late)
        yield from groupA(g)[1]
        st["out", g] = [tv.last()]
        for b in range(4 * g, 4 * g + 4):
            bank_free(b, st["out", g][0])

    need(PE, ta.last())
    run(weave(chain(dilated_group(0), weave(norm_a(0, 0), norm_a(0, 1))),
              chain(*side.parts, gate_diag(2, C_GPOSTA), dilated_group(1), weave(norm_a(1, 0), norm_a(1, 1), gate_bcast((4, 5, 6, 7), 0))),
              norm_b()))
    run(rest_ada())
    barrier()
    row_ahead(a["w_out"][0])
    mix_ready = transposed_mix(lambda k, m: proj[:, m, mix_col(k):mix_col(k) + P])

    def post_norm_add(y_done):
        for m in range(MT):
            y = ps[:, 4 * m:4 * m + 4, :]
            need(SCA, y_done[m])
            t = done(SCA, SCA.activation(junks[m][:, :].rearrange("p (b n) -> p b n", b=4), y, ACT.Square, accum_out=sq[:, 2 + m:3 + m]))
            need(POOL, t)
            st["ys", m] = [rsqrt_cols(sq2[:, 2 + m:3 + m], sq[:, 2 + m:3 + m], 1, 1.0 / D)]
        for m in range(MT):
            y = ps[:, 4 * m:4 * m + 4, :]
            need(DVE, st["ys", m], y_done[m])
            tmp = post_tmp[m][:, :].rearrange("p (b n) -> p b n", b=4)
            t = done(DVE, DVE.scalar_tensor_tensor(tmp, y, sq2[:, 2 + m:3 + m], gate_row[:, :].rearrange("p (b n) -> p b n", b=4), ALU.mult, ALU.mult))
            for b in range(4 * m, 4 * m + 4):
                bank_free(b, t)
            need(DVE, t)
            st["x", m] = [done(DVE, DVE.tensor_tensor(x[:, m, :], x[:, m, :], post_tmp[m][:, :], ALU.add))]

    def plain_add(y_done):
        for m in range(MT):
            need(DVE, y_done[m])
            t = done(DVE, DVE.tensor_tensor(x[:, m, :].rearrange("p (b n) -> p b n", b=4), x[:, m, :].rearrange("p (b n) -> p b n", b=4),
                                            ps[:, 4 * m:4 * m + 4, :], ALU.add))
            for b in range(4 * m, 4 * m + 4):
                bank_free(b, t)
            st["x", m] = [t]

    x_ready = lambda: [st["x", 0], st["x", 1]]

    y_done = row_stage(a["w_out"][0], mixT, KD, mix_ready, ada=4)
    post_norm_add(y_done)

    scale_sum = ada_finish(4, 0, 1)
    next(scale_sum)

    def ffn_gain():
        run(scale_sum)
        t = modulated_gain(4, C_GFFN)
        need(DVE, t)
        need(SCA, t)
    norm(x, gsc, mod[:, 3 * 16:4 * 16], x_ready(), a["w_gate"][0], before_h=ffn_gain)

    def hidden_out(dst, i, banks, src, tok_key, pause):
        def tr():
            need(PE, st[tok_key], st.get(("bank", banks[0])), st.get(("bank", banks[1])))
            for c in range(4):
                for m in range(MT):
                    ins = PE.transpose(ps[:, banks[c // 2], (c % 2) * S + m * P:(c % 2) * S + (m + 1) * P], src[:, m, c * P:(c + 1) * P], ident[:, :])
            st["hid_t", banks[0]] = [done(PE, ins)]

        def ev():
            need(SCA, st["hid_t", banks[0]])
            d = dst[:, bass.ds(i * 4, 4), :].rearrange("p (b k) n -> p b (k n)", b=2)
            t = done(SCA, SCA.activation(d, ps[:, banks[0]:banks[1] + 1, :], ACT.Copy))
            bank_free(banks[0], t)
            bank_free(banks[1], t)
        return [tr] + [lambda: None] * pause + [ev]

    def gate_steps():
        g = ps[:, 0:2, :]

        def ex():
            need(SCA, st["full", 0], st.get(("hid_t", 4)))
            st["sg"] = [done(SCA, SCA.activation(sg1[:, :, :], g, ACT.Exp, scale=-1.0))]

        def plus():
            need(DVE, st["sg"])
            st["sg"] = [done(DVE, DVE.tensor_scalar(sg1[:, :, :], sg1[:, :, :], 1.0, None, ALU.add))]

        def rec():
            need(DVE, st["sg"])
            st["sg"] = [done(DVE, DVE.reciprocal(sg1[:, :, :], sg1[:, :, :]))]

        def mul():
            need(DVE, st["sg"])
            t = done(DVE, DVE.tensor_tensor(sg1[:, :, :], g, sg1[:, :, :], ALU.mult))
            st["sg"] = [t]
            bank_free(0, t)
            bank_free(1, t)
        return [ex, plus, rec, mul]

    def up_steps(i):
        def mul():
            need(DVE, st["full", 2], st["sg"])
            t = done(DVE, DVE.tensor_tensor(sg1[:, :, :], ps[:, 2:4, :], sg1[:, :, :], ALU.mult))
            st["sgu"] = [t]
            bank_free(2, t)
            bank_free(3, t)
        return [mul] + hidden_out(hid1, i, (4, 5), sg1, "sgu", 2)

    def ffn1(i, i0, side=None):
        prev = up_steps(i0 + i - 1) if not (isinstance(i, int) and i + i0 == 0) else []
        c = bass.ds((i0 + i) * 512, 512)

        def extra(slot):
            def f(j):
                if i0 == 0 and j % 2 == 1:
                    n = slot * 4 + j // 2
                    ada_half(5, i * 4 + n // 2, n % 2, isinstance(i, int) and i == 0 and n // 2 == 0)
            return f
        col_slot(a["w_gate"][0], 0, KD, c, 512, (0, 1), A_h, prev, extra=extra(0), side=side)
        col_slot(a["w_up"][0], 0, KD, c, 512, (2, 3), A_h, gate_steps(), extra=extra(1), side=side)
    repeat(4, lambda i: ffn1(i, 0), peel=2)
    gate_side = Side(wait_steps(1), ada_finish(5, 6, 4), gate_diag(5, C_GPOSTF), gate_bcast((6, 7), 4))
    repeat(DFF1 // 512 - 4, lambda i: ffn1(i, 4, gate_side if isinstance(i, int) and i == 0 else None), peel=2)
    assert not gate_side.parts
    row_ahead(a["w_down"][0])
    for s_ in up_steps(DFF1 // 512 - 1):
        s_()
    barrier()
    y_done = row_stage(a["w_down"][0], hid1, DFF1 // P, [])
    post_norm_add(y_done)

    norm(x, cols[:, C_GMIX:C_GMIX + 16], None, x_ready(), a["w_in_2"][0], (4096,))
    pj = sb("proj_2", "big", 0, [MT, IN2])
    O_CQ, O_CKV, O_KR, O_QD, O_KD, O_VD, O_QI, O_KI, O_WI = 0, 512, 768, 832, 1856, 2880, 3904, 4928, 4992
    cq_hi = sb("cq_hi", "big", 40 * KB, [6, S], F32R)
    cq_lo = sb("cq_lo", "big", 54 * KB, [6, S], F32R)
    cq_junk = sb("cq_junk", "big", 46 * KB, [512])
    qr = sb("mla_q_rope", "h", 28 * KB, [MT, 8, 64])
    pad = sb("padded_keys", "acc", 8 * KB, [MT, 2, P])
    krT = sb("k_rope_T", "acc", 10 * KB, [2, S])
    kiT = sb("k_idx_T", "acc", 12 * KB, [2, S])
    selb = sb("selection", "acc", 14 * KB, [MT, S])
    rope_c = [sb("rope_t2", "big", 48 * KB, [512])] + [sb(f"rope_v{i}", "big", (50 + i) * KB, [256]) for i in range(2)]
    qiT = sb("q_idx_T", "big", 40 * KB, [8, P])
    rel = [sb("idx_relu0", "big", 44 * KB, [4, S]), sb("idx_relu1", "acc", 0, [4, S])]
    score = sb("score", "big", 52 * KB, [S])
    kept = sb("score_left", "big", 53 * KB, [S])

    def rotated(cols_, heads, width, half, rot, dst=None):
        for m in range(MT):
            v = cols_(m).rearrange("p (h n) -> p h n", h=heads)[:, :, width[0]:width[1]]
            yield from rope(v, dst(m) if dst else v, heads, half, rot, m, rope_c)

    def padded_T(c0, dst, bank):
        t = done(DVE, DVE.memset(pad[:, :, :, :], 0.0))
        need(DVE, t)
        for m in range(MT):
            DVE.tensor_copy(pad[:, m, 0, 0:64], pj[:, m, c0:c0 + 64])
            t = done(DVE, DVE.tensor_copy(pad[:, m, 1, 64:128], pj[:, m, c0:c0 + 64]))
        need(PE, t, st.get(("bank", bank)))
        t = transposes(bank, [(e * S + m * P, pad[:, m, e, :]) for e in range(2) for m in range(MT)])
        yield
        yield
        need(DVE, t)
        t = done(DVE, DVE.tensor_copy(dst[:, :, :].rearrange("p e n -> p (e n)"), ps[:, bank, :]))
        bank_free(bank, t)
        need(PE, t)

    def index_keys():
        need(DVE, ta.last())
        yield from rotated(lambda m: pj[:, m, O_QI:O_QI + 1024], 16, (0, 16), 8, R_IDX)
        yield from rotated(lambda m: pj[:, m, O_KI:O_KI + 64], 1, (0, 16), 8, R_IDX)
        yield from padded_T(O_KI, kiT, 6)
        for m in range(MT):
            t = done(DVE, DVE.tensor_scalar(wi[:, m, :], pj[:, m, O_WI:O_WI + 16], 16 ** -0.5 * 64 ** -0.5, None, ALU.mult))
        need(DVE, t)

    def indexer():
        for m in range(MT):
            nk = (m + 1) * P
            need(PE, st.get(("bank", 4)), st.get(("bank", 5)))
            t = transposes(4, [(j * P, pj[:, m, O_QI + j * P:O_QI + (j + 1) * P]) for j in range(8)])
            yield
            yield
            need(SCA, t)
            qt = done(SCA, SCA.activation(qiT[:, :, :].rearrange("p (b k) n -> p b (k n)", b=2), ps[:, 4:6, :], ACT.Copy))
            bank_free(4, qt)
            bank_free(5, qt)
            need(PE, qt)
            stt = None
            for g in range(4):
                need(PE, st.get(("bank", 6)), st.get(("bank", 7)))
                for i in range(4):
                    ins = PE.matmul(ps[:, 6 + i // 2, (i % 2) * S:(i % 2) * S + nk], qiT[:, 2 * g + i // 2, :], kiT[:, i % 2, 0:nk],
                                    start=True, stop=True)
                t = done(PE, ins)
                yield
                yield
                need(SCA, t, st.get(("idx_v", g % 2)))
                e = done(SCA, SCA.activation(rel[g % 2][:, :, 0:nk].rearrange("p (b u) n -> p b u n", b=2),
                                             ps[:, 6:8, :].rearrange("p b (u n) -> p b u n", u=2)[:, :, :, 0:nk], ACT.Relu))
                bank_free(6, e)
                bank_free(7, e)
                need(DVE, e)
                for i in range(4):
                    hh = 4 * g + i
                    need(DVE, stt)
                    if hh == 0:
                        stt = done(DVE, DVE.tensor_scalar(score[:, 0:nk], rel[0][:, 0, 0:nk], wi[:, m, 0:1], None, ALU.mult))
                    else:
                        stt = done(DVE, DVE.scalar_tensor_tensor(score[:, 0:nk], rel[g % 2][:, i, 0:nk], wi[:, m, hh:hh + 1],
                                                                 score[:, 0:nk], ALU.mult, ALU.add))
                st["idx_v", g % 2] = [stt]
            need(DVE, stt)
            stt = done(DVE, DVE.memset(score[0:64, nk - 64:nk], DROPPED))
            src = score
            for rnd_ in range(TOPK // 8):
                need(DVE, stt)
                t = done(DVE, DVE.max(m8[:, :], src[:, 0:nk]))
                need(DVE, t)
                stt = done(DVE, DVE.match_replace(kept[:, 0:nk], m8[:, :], src[:, 0:nk], TAKEN))
                src = kept
                if rnd_ % 2:
                    yield
            need(DVE, stt)
            done(DVE, DVE.tensor_scalar(selb[:, m, 0:nk], kept[:, 0:nk], (DROPPED + TAKEN) / 2, NEG, ALU.is_ge, ALU.mult))

    def latents():
        need(SCA, tv.last())
        for m in range(MT):
            for s_i, (c0, n) in enumerate(((O_CQ, 512), (O_CKV, 256))):
                st["lt", m, s_i] = [row_rsqrt(pj[:, m, c0:c0 + n], 2 * m + s_i, junk_ap=cq_junk[:, 0:n])]
            yield
        for m in range(MT):
            for s_i, (c0, n) in enumerate(((O_CQ, 512), (O_CKV, 256))):
                need(DVE, st["lt", m, s_i])
                t = done(DVE, DVE.tensor_scalar(pj[:, m, c0:c0 + n], pj[:, m, c0:c0 + n], sq2[:, 2 * m + s_i:2 * m + s_i + 1], None, ALU.mult))
        need(PE, t, *[st.get(("bank", b)) for b in (4, 5, 6)])
        t = transposes(4, [(k * S + m * P, pj[:, m, k * P:(k + 1) * P]) for k in range(6) for m in range(MT)])
        yield
        yield
        for b in range(3):
            halves = [(k, ps[:, 4 + b, (k % 2) * S:(k % 2 + 1) * S], cols[:, C_GCQ + k:C_GCQ + k + 1]) for k in (2 * b, 2 * b + 1)]
            need(SCA, t)
            for k, src, gain in halves:
                hi = done(SCA, SCA.activation(cq_hi[:, k, :], src, ACT.Copy, scale=gain))
            need(DVE, hi, t)
            for k, src, gain in halves:
                lo = done(DVE, DVE.scalar_tensor_tensor(cq_lo[:, k, :], src, gain, r32(cq_hi[:, k, :]), ALU.mult, ALU.subtract))
            bank_free(4 + b, lo)
            yield
        st["latents"] = [hi, lo]

    posts = slots(a["w_in_2"][0], [4096, 3584, 4608], pj)
    side = Side(wait_steps(4), index_keys(), indexer(), latents())
    for n in range(7):
        b = (2, 3) if n % 2 == 0 else (0, 1)
        col_slot(a["w_in_2"][0], 0, KD, (512 * n,), 512, b, A_h, posts, side=side)
        posts = copy_post(b, pj[:, :, 512 * n:512 * n + 512], 512)
    look_ahead(a["w_qb_2"][0], (0,), range(2))
    side.finish()

    need(PE, st["latents"])
    qm = sb("mla_q", "h", 0, [MT, 1536])
    kvm = sb("mla_kv", "h", 12 * KB, [MT, 2048])

    def rest_rotary():
        need(DVE, ta.last())
        for c in (O_QD, O_KD):
            yield from rotated(lambda m, c=c: pj[:, m, c:c + 1024], 8, (0, 32), 16, R_DSA)
        yield from rotated(lambda m: pj[:, m, O_KR:O_KR + 64], 1, (0, 64), 32, R_MLA)
        yield from padded_T(O_KR, krT, 4)

    side = Side(rest_rotary())
    jobs = [(a["w_qb_2"][0], 4, n * 512, (cq_hi, cq_lo), qm) for n in range(3)]
    jobs += [(a["w_kvb_2"][0], 2, n * 512, (cq_hi[:, 4:6, :], cq_lo[:, 4:6, :]), kvm) for n in range(4)]
    rest = list(posts)
    for n, (w, nk, c0, A, dst) in enumerate(jobs):
        b = ((0, 1), (6, 7), (2, 3))[n % 3]
        post = [rest.pop(0)] if n == 0 or len(rest) == 2 else []
        col_slot(w, 0, nk, (c0,), 512, b, A, post, lag=0, side=side)
        rest += copy_post(b, dst[:, :, c0:c0 + 512], 512)
    side.finish()
    for s_ in rest:
        s_()
    barrier()

    def mla_rotary():
        yield from rotated(lambda m: qm[:, m, :], 8, (128, 192), 32, R_MLA, lambda m: qr[:, m, :, :])
        st["q_rope"] = st["rope"]
        need(PE, st["rope"])
        need(SCA, st["rope"])

    def mla_group(g):
        while "q_rope" not in st:
            yield
        yield from groupM(g)[1]

    names = ("qT", "kT")
    work2 = [[sb(f"w2_{n}{p}", "big", (40 + 8 * p + 4 * i) * KB, [TILE]) for i, n in enumerate(names)]
             + [sb(f"w2_s0{p}", "acc", 4 * KB * p, [TILE]), sb(f"w2_s1{p}", "big", (56 + 4 * p) * KB, [TILE])] for p in range(2)]
    qrT = [sb("q_rope_T0", "acc", 8 * KB, [2, S]), sb("q_rope_T1", "acc", 12 * KB, [2, S])]
    st["set", 0] = st["set", 1] = []

    def groupM(g):
        p = g % 2
        QT, KT = (w[:, :].rearrange("p (u n) -> p u n", u=4) for w in work2[p][:2])
        items_q = [(i * S + m * P, qm[:, m, 192 * (4 * g + i):192 * (4 * g + i) + P]) for i in range(4) for m in range(MT)]
        items_k = [(i * S + m * P, kvm[:, m, 256 * (4 * g + i):256 * (4 * g + i) + P]) for i in range(4) for m in range(MT)]

        def extra(p):
            qv = qr[:, :, :, :].rearrange("p m h n -> p m (h n)")
            t = transposes(4 * p, [(j * S + m * P, qv[:, m, (2 * g + j) * P:(2 * g + j + 1) * P]) for j in range(2) for m in range(MT)])
            need(SCA, t)
            return [done(SCA, SCA.activation(qrT[p][:, :, :].rearrange("p j n -> p (j n)"), ps[:, 4 * p, :], ACT.Copy))]
        units = [unit([
            (lambda t, i=i: QT[:, i, t * P:(t + 1) * P], lambda nk, i=i: KT[:, i, 0:nk]),
            (lambda t, i=i: qrT[p][:, i // 2, t * P:(t + 1) * P], lambda nk, i=i: krT[:, i % 2, 0:nk])]) for i in range(4)]
        return p, attention(p, qk_prep(items_q, items_k, extra), units,
                            lambda i, kt: kvm[:, kt, 256 * (4 * g + i) + P:256 * (4 * g + i) + 2 * P],
                            lambda t: pj[:, t, O_QI + 512 * g:O_QI + 512 * g + 512].rearrange("p (h n) -> p h n", h=4),
                            192 ** -0.5, lambda t: chunk[:, P:S] if t == 0 else chunk[:, :], work2[p])

    def groupD(g):
        p = g % 2
        QT, KT = (w[:, :].rearrange("p (u n) -> p u n", u=4) for w in work2[p][:2])
        items = lambda base: [(i * S + m * P, pj[:, m, base + (4 * g + i) * P:base + (4 * g + i + 1) * P]) for i in range(4) for m in range(MT)]
        units = [unit([(lambda t, i=i: QT[:, i, t * P:(t + 1) * P], lambda nk, i=i: KT[:, i, 0:nk])]) for i in range(4)]
        return p, attention(p, qk_prep(items(O_QD), items(O_KD)), units,
                            lambda i, kt: pj[:, kt, O_VD + (4 * g + i) * P:O_VD + (4 * g + i + 1) * P],
                            lambda t: pj[:, t, O_QD + 512 * g:O_QD + 512 * g + 512].rearrange("p (h n) -> p h n", h=4),
                            128 ** -0.5, lambda t: selb[:, t, 0:(t + 1) * P], work2[p])

    run(weave(chain(groupD(0)[1], mla_group(0)), chain(mla_rotary(), groupD(1)[1], mla_group(1))))
    barrier()
    row_ahead(a["w_out_2"][0])
    mix_ready = transposed_mix(lambda k, m: pj[:, m, O_QI + k * P:O_QI + (k + 1) * P] if k < 8 else
                               pj[:, m, O_QD + (k - 8) * P:O_QD + (k - 7) * P])
    y_done = row_stage(a["w_out_2"][0], mixT, KD, mix_ready)
    plain_add(y_done)

    norm(x, cols[:, C_GCROSS:C_GCROSS + 16], None, x_ready(), a["w_q_cross_2"][0])
    qx = sb("cross_q", "big", 0, [MT, 512])
    ox = sb("cross_o", "big", 4 * KB, [MT, 512])
    oxT = sb("cross_oT", "big", 8 * KB, [4, S])
    col_slot(a["w_q_cross_2"][0], 0, KD, (0,), 512, (0, 1), A_h)
    for s_ in copy_post((0, 1), qx[:, :, :], 512):
        s_()
    barrier()
    st["set", 0] = st["set", 1] = []

    def prep_x(p, QT, KT):
        t = transposes(4 * p, [(i * S + m * P, qx[:, m, i * P:(i + 1) * P]) for i in range(4) for m in range(MT)])
        need(SCA, t)
        e = done(SCA, SCA.activation(QT[:, :].rearrange("p (b n) -> p b n", b=2), ps[:, 4 * p:4 * p + 2, :], ACT.Copy))
        yield
        return [e]
    QTx = work2[0][0][:, :].rearrange("p (u n) -> p u n", u=4)
    units = [unit([(lambda t, i=i: QTx[:, i, t * P:(t + 1) * P], lambda nk, i=i: kxT[:, i, 0:nk])]) for i in range(4)]
    run_two([(0, attention(0, prep_x, units, lambda i, kt: vx[:, kt, i * P:(i + 1) * P],
                           lambda t: ox[:, t, :].rearrange("p (h n) -> p h n", h=4), 128 ** -0.5, lambda t: None, work2[0], nkts=(2, 2)))])
    row_ahead(a["w_o_cross_2"][0])
    need(PE, st["set", 0])
    t = transposes(4, [(k * S + m * P, ox[:, m, k * P:(k + 1) * P]) for k in range(4) for m in range(MT)])
    need(SCA, t)
    t = done(SCA, SCA.activation(oxT[:, :, :].rearrange("p (b k) n -> p b (k n)", b=2), ps[:, 4:6, :], ACT.Copy))
    barrier()
    y_done = row_stage(a["w_o_cross_2"][0], oxT, 4, [t])
    plain_add(y_done)

    norm(x, cols[:, C_GMLP:C_GMLP + 16], None, x_ready(), a["w_up_2"][0])

    def relu_steps(i, slot):
        b = (0, 1) if slot == 0 else (2, 3)
        tb = (4, 5) if slot == 0 else (6, 7)

        def rel_():
            need(SCA, st["full", b[0]], st.get(("hid_t", tb[0])))
            t = done(SCA, SCA.activation(r2[slot][:, :, :], ps[:, b[0]:b[1] + 1, :], ACT.Relu))
            st["relu", slot] = [t]
            bank_free(b[0], t)
            bank_free(b[1], t)

        def sq_():
            need(DVE, st["relu", slot])
            st["relu_sq", slot] = [done(DVE, DVE.tensor_tensor(r2[slot][:, :, :], r2[slot][:, :, :], r2[slot][:, :, :], ALU.mult))]
        return [rel_, sq_] + hidden_out(hid2, 2 * i + slot, tb, r2[slot], ("relu_sq", slot), 1)

    def mlp(i):
        prev = relu_steps(i - 1, 1) if not (isinstance(i, int) and i == 0) else []
        col_slot(a["w_up_2"][0], 0, KD, bass.ds(i * 1024, 512), 512, (0, 1), A_h, prev)
        col_slot(a["w_up_2"][0], 0, KD, bass.ds(i * 1024 + 512, 512), 512, (2, 3), A_h, relu_steps(i, 0))
    repeat(DFF2 // 1024, mlp, peel=2)
    row_ahead(a["w_down_2"][0])
    for s_ in relu_steps(DFF2 // 1024 - 1, 1):
        s_()
    barrier()
    y_done = row_stage(a["w_down_2"][0], hid2, DFF2 // P, [])
    g_row = sb("g_final_rows", "acc", 0, [D])
    gf = t_late.done(q.dma_start(g_row[:, :], a["g_final_2"].rearrange("(o d) -> o d", o=1).to_broadcast([P, D])))
    plain_add(y_done)
    for m in range(MT):
        st["rs", m] = [row_rsqrt(x[:, m, :], m, st["x", m], junk_ap=norm_x[m][:, :])]
    for m in range(MT):
        for c in (slice(0, TILE), slice(TILE, D)):
            need(DVE, st["rs", m], gf)
            t = done(DVE, DVE.scalar_tensor_tensor(x[:, m, c], x[:, m, c], sq2[:, m:m + 1], g_row[:, c], ALU.mult, ALU.mult))
            need(SP, t)
            o = t_out.done(SP.dma_start(out[0, m * P:(m + 1) * P, c], x[:, m, c]))
    need(SP, o)


_INS = ["x", "c", "positions", "w_ada", "b_ada", "g_pre_attn", "w_in", "g_out_a", "lambda_q1", "lambda_k1", "lambda_q2",
        "lambda_k2", "g_subln_b", "w_out", "g_post_attn", "g_pre_ffn", "w_gate", "w_up", "w_down", "g_post_ffn",
        "mem_2", "positions_2", "g_mix_2", "w_in_2", "g_cq_2", "g_ckv_2", "w_qb_2", "w_kvb_2", "w_out_2", "g_cross_2",
        "g_mem_2", "w_q_cross_2", "w_k_cross_2", "w_v_cross_2", "w_o_cross_2", "g_mlp_2", "w_up_2", "w_down_2",
        "g_final_2"]


def kernel(**inputs):
    import concourse.bacc as bacc
    from concourse.bass_utils import run_bass_kernel_spmd

    nc = bacc.Bacc("TRN2", target_bir_lowering=False, num_devices=1)
    arrays, aps = {}, {}
    given = {n: np.ascontiguousarray(inputs[n]) for n in _INS}
    given.update(shape_constants())
    for name, v in given.items():
        arrays[f"in_{name}"] = v
        aps[name] = nc.dram_tensor(f"in_{name}", v.shape, mybir.dt.from_np(v.dtype), kind="ExternalInput").ap()
    out = nc.dram_tensor("out_x", (1, S, D), F32, kind="ExternalOutput").ap()
    build(nc, aps, out)
    r = run_bass_kernel_spmd(nc, [arrays], core_ids=[0])
    return r.results[0]["out_x"]
```
